# Optimizing a Trainium2 kernel written in Bass

```python
import math
import jax
import jax.numpy as jnp
from jax import lax
import numpy as np

D_MODEL = 1024
BATCH = 1
SEQ = 512
DEPTH = 2
DEC_BATCH = 8
DEC_SEQ = 8
PAST_LEN = 256
PAGE_SIZE = 128

N_META = 16
N_EVEN = (DEPTH + 1) // 2
N_ODD = DEPTH // 2
A_HEAD_DIM = 64
A_HEADS = (D_MODEL // 2) // A_HEAD_DIM
A_KV_HEADS = 2
IDX_HEADS = 4
IDX_DIM = 64
TOPK_MAX = 256
META_BONUS = 1e30
Q_BLOCK = 128
ROPE_THETA = 500000.0
ROPE_FRAC = 4
DN_DK = 128
DN_DV = 128
DN_HEADS = (D_MODEL // 2) // DN_DV
CONV_W = 4
HG_DK = 128
HG_HEADS = D_MODEL // HG_DK
HG_DV = D_MODEL // HG_HEADS
CHUNK = 64
D_FF = 4 * D_MODEL

A_Q_W = A_HEADS * A_HEAD_DIM
A_KV_W = A_KV_HEADS * A_HEAD_DIM
IDX_Q_W = IDX_HEADS * IDX_DIM
DN_QK_W = DN_HEADS * DN_DK
DN_V_W = DN_HEADS * DN_DV
CONV_DIM = 2 * DN_QK_W + DN_V_W
EVEN_SPLITS = (A_Q_W, A_KV_W, A_KV_W, IDX_Q_W, IDX_DIM, IDX_HEADS, CONV_DIM, DN_HEADS, DN_HEADS, DN_V_W)
EVEN_IN = A_Q_W + 2 * A_KV_W + IDX_Q_W + IDX_DIM + IDX_HEADS + CONV_DIM + 2 * DN_HEADS + DN_V_W
EVEN_OUT = A_Q_W + DN_V_W
HG_F = HG_HEADS * HG_DK
HG_V = HG_HEADS * HG_DV
ODD_IN = 2 * HG_F + 2 * HG_V

kernel_name = 'hybrid_dsa_gdn_hgrn2_step'

def _rmsnorm(x, g, eps=1e-6):
    xf = x.astype(jnp.float32)
    y = xf * lax.rsqrt(jnp.mean(xf * xf, axis=-1, keepdims=True) + eps)
    return (y * g.astype(jnp.float32)).astype(x.dtype)

def _l2norm(x, eps=1e-6):
    xf = x.astype(jnp.float32)
    return xf * lax.rsqrt(jnp.sum(xf * xf, axis=-1, keepdims=True) + eps)

def _partial_rope(x, pos):
    rot = x.shape[-1] // ROPE_FRAC
    half = rot // 2
    inv = ROPE_THETA ** (-jnp.arange(half, dtype=jnp.float32) / half)
    ang = pos.astype(jnp.float32)[:, None] * inv[None, :]
    shape = (1, pos.shape[0]) + (1,) * (x.ndim - 3) + (half,)
    cos = jnp.cos(ang).reshape(shape)
    sin = jnp.sin(ang).reshape(shape)
    xf = x.astype(jnp.float32)
    x1 = xf[..., :half]
    x2 = xf[..., half:rot]
    out = jnp.concatenate([x1 * cos - x2 * sin, x2 * cos + x1 * sin, xf[..., rot:]], axis=-1)
    return out.astype(x.dtype)

def _gather_pages(pool, page_table):
    g = pool[page_table]
    return g.reshape((g.shape[0], g.shape[1] * g.shape[2]) + g.shape[3:])

def _short_conv(u, buf, w):
    full = jnp.concatenate([buf.astype(u.dtype), u], axis=1)
    out = lax.conv_general_dilated(full, w[:, None, :].astype(u.dtype), window_strides=(1,), padding='VALID',
                                   dimension_numbers=('NWC', 'WIO', 'NWC'), feature_group_count=u.shape[-1])
    return jax.nn.silu(out), full[:, full.shape[1] - (CONV_W - 1):, :]

def _dsa_attention(q, iq, iw, k, v, ik, q_pos, k_sel):
    b, L, h, hd = q.shape
    s = k.shape[1]
    qb = min(Q_BLOCK, L)
    nb = -(-L // qb)
    pad = nb * qb - L

    def blocks(t):
        t = jnp.pad(t, [(0, 0), (0, pad)] + [(0, 0)] * (t.ndim - 2))
        return jnp.moveaxis(t.reshape((b, nb, qb) + t.shape[2:]), 1, 0)

    pos_b = jnp.pad(q_pos, (0, pad), mode='edge').reshape(nb, qb)
    key_pos = jnp.arange(s, dtype=jnp.int32)
    is_meta = key_pos < N_META
    ikf = ik.astype(jnp.float32)
    rep = h // A_KV_HEADS
    idx_scale = (IDX_HEADS * IDX_DIM) ** -0.5
    att_scale = hd ** -0.5

    def one_block(args):
        qq, qi, wi, pp = args
        rel = jax.nn.relu(jnp.einsum('bqhd,bsd->bqhs', qi.astype(jnp.float32), ikf))
        score = jnp.einsum('bqh,bqhs->bqs', wi.astype(jnp.float32) * idx_scale, rel)
        score = jnp.where(is_meta, META_BONUS, score)
        visible = key_pos[None, :] <= pp[:, None]
        score = jnp.where(visible[None], score, -jnp.inf)
        _, sel = lax.top_k(score, k_sel)
        valid = sel <= pp[None, :, None]
        kg = jax.vmap(lambda kk, ii: kk[ii])(k, sel).astype(jnp.float32)
        vg = jax.vmap(lambda vv, ii: vv[ii])(v, sel).astype(jnp.float32)
        qg = qq.astype(jnp.float32).reshape(b, qb, A_KV_HEADS, rep, hd)
        logits = jnp.einsum('bqgrd,bqkgd->bqgrk', qg, kg) * att_scale
        logits = jnp.where(valid[:, :, None, None, :], logits, -jnp.inf)
        p = jax.nn.softmax(logits, axis=-1)
        o = jnp.einsum('bqgrk,bqkgd->bqgrd', p, vg)
        return o.reshape(b, qb, h * hd).astype(q.dtype)

    out = lax.map(one_block, (blocks(q), blocks(iq), blocks(iw), pos_b))
    return jnp.moveaxis(out, 0, 1).reshape(b, nb * qb, h * hd)[:, :L]

def _to_chunks(t, n, c):
    t = t.reshape((t.shape[0], n, c) + t.shape[2:])
    return jnp.transpose(t, (1, 0, 3, 2) + tuple(range(4, t.ndim)))

def _from_chunks(o):
    n, b, h, c, d = o.shape
    return jnp.transpose(o, (1, 0, 3, 2, 4)).reshape(b, n * c, h, d)

def _gated_delta_chunks(q, k, v, g, beta, s0, chunk):
    b, L, h, dk = q.shape
    dv = v.shape[-1]
    n = L // chunk
    qc, kc, vc, gc, bc = (_to_chunks(t.astype(jnp.float32), n, chunk) for t in (q, k, v, g, beta))
    incl = jnp.tril(jnp.ones((chunk, chunk), bool))
    strict = jnp.tril(jnp.ones((chunk, chunk), bool), k=-1)
    eye = jnp.eye(chunk, dtype=jnp.float32)

    def step(S, inp):
        qq, kk, vv, gg, bb = inp
        gam = jnp.cumsum(gg, axis=-1)
        diff = gam[..., :, None] - gam[..., None, :]
        dec = jnp.exp(jnp.where(incl, diff, -jnp.inf))
        kkt = jnp.einsum('bhtd,bhsd->bhts', kk, kk)
        m = jnp.where(strict, bb[..., :, None] * kkt * dec, 0.0) + eye
        rhs = jnp.concatenate([vv * bb[..., None], kk * (bb * jnp.exp(gam))[..., None]], axis=-1)
        sol = lax.linalg.triangular_solve(m, rhs, left_side=True, lower=True, unit_diagonal=True)
        u, w = sol[..., :dv], sol[..., dv:]
        v_new = u - jnp.einsum('bhtd,bhde->bhte', w, S)
        attn = jnp.einsum('bhtd,bhsd->bhts', qq, kk) * dec
        o = jnp.einsum('bhtd,bhde->bhte', qq * jnp.exp(gam)[..., None], S) + jnp.einsum('bhts,bhse->bhte', attn, v_new)
        gl = gam[..., -1:]
        S = S * jnp.exp(gl)[..., None] + jnp.einsum('bhsd,bhse->bhde', kk * jnp.exp(gl - gam)[..., None], v_new)
        return S, o

    S, o = lax.scan(step, s0.astype(jnp.float32), (qc, kc, vc, gc, bc))
    return _from_chunks(o), S

def _hgrn2_chunks(q, k, v, logf, s0, chunk):
    b, L, h, dk = q.shape
    n = L // chunk
    qc, kc, vc, fc = (_to_chunks(t.astype(jnp.float32), n, chunk) for t in (q, k, v, logf))
    incl = jnp.tril(jnp.ones((chunk, chunk), bool))[:, :, None]

    def step(S, inp):
        qq, kk, vv, ff = inp
        cb = jnp.cumsum(ff, axis=-2)
        diff = cb[..., :, None, :] - cb[..., None, :, :]
        dec = jnp.exp(jnp.where(incl, diff, -jnp.inf))
        attn = jnp.sum(qq[..., :, None, :] * dec * kk[..., None, :, :], axis=-1)
        o = jnp.einsum('bhtd,bhde->bhte', qq * jnp.exp(cb), S) + jnp.einsum('bhts,bhse->bhte', attn, vv)
        cl = cb[..., -1:, :]
        S = S * jnp.exp(cl[..., 0, :])[..., None] + jnp.einsum('bhsd,bhse->bhde', kk * jnp.exp(cl - cb), vv)
        return S, o

    S, o = lax.scan(step, s0.astype(jnp.float32), (qc, kc, vc, fc))
    return _from_chunks(o), S

def _chunked(fn, seqs, s0, pad_front, chunk):
    L = seqs[0].shape[1]
    pad_end = (-(pad_front + L)) % chunk
    padded = [jnp.pad(t, [(0, 0), (pad_front, pad_end)] + [(0, 0)] * (t.ndim - 2)) for t in seqs]
    o, S = fn(*padded, s0, chunk)
    return o[:, pad_front:pad_front + L], S

def _even_mixer(hn, pos, past_k, past_v, past_ik, conv_buf, s0, k_sel, pad_front, chunk,
                w_in, w_out, conv_w, a_log, dt_bias, dn_norm):
    b, L, _ = hn.shape
    offs = np.cumsum(EVEN_SPLITS)[:-1].tolist()
    aq, ak, av, iq, ik, iw, dqkv, db, da, dz = jnp.split(hn @ w_in, offs, axis=-1)
    aq = _partial_rope(aq.reshape(b, L, A_HEADS, A_HEAD_DIM), pos)
    ak = _partial_rope(ak.reshape(b, L, A_KV_HEADS, A_HEAD_DIM), pos)
    av = av.reshape(b, L, A_KV_HEADS, A_HEAD_DIM)
    iq = _partial_rope(iq.reshape(b, L, IDX_HEADS, IDX_DIM), pos)
    ik = _partial_rope(ik, pos)
    keys = jnp.concatenate([past_k.astype(ak.dtype), ak], axis=1)
    vals = jnp.concatenate([past_v.astype(av.dtype), av], axis=1)
    ikeys = jnp.concatenate([past_ik.astype(ik.dtype), ik], axis=1)
    a_out = _dsa_attention(aq, iq, iw, keys, vals, ikeys, pos, k_sel)
    c, new_buf = _short_conv(dqkv, conv_buf, conv_w)
    dq, dk, dv = jnp.split(c, [DN_QK_W, 2 * DN_QK_W], axis=-1)
    dq = _l2norm(dq.reshape(b, L, DN_HEADS, DN_DK)) * (DN_DK ** -0.5)
    dk = _l2norm(dk.reshape(b, L, DN_HEADS, DN_DK))
    dv = dv.reshape(b, L, DN_HEADS, DN_DV)
    beta = jax.nn.sigmoid(db.astype(jnp.float32))
    g = -jnp.exp(a_log.astype(jnp.float32)) * jax.nn.softplus(da.astype(jnp.float32) + dt_bias.astype(jnp.float32))
    o, s_new = _chunked(_gated_delta_chunks, (dq, dk, dv, g, beta), s0, pad_front, chunk)
    o = _rmsnorm(o.astype(hn.dtype), dn_norm) * jax.nn.silu(dz.reshape(b, L, DN_HEADS, DN_DV))
    mixed = jnp.concatenate([a_out, o.reshape(b, L, DN_V_W)], axis=-1)
    return mixed @ w_out, ak, av, ik, new_buf, s_new

def _odd_mixer(hn, s0, lb, pad_front, chunk, w_in, w_out, hg_norm):
    b, L, _ = hn.shape
    q, f, iv, gz = jnp.split(hn @ w_in, [HG_F, 2 * HG_F, 2 * HG_F + HG_V], axis=-1)
    q = jax.nn.silu(q).reshape(b, L, HG_HEADS, HG_DK)
    ff = f.astype(jnp.float32).reshape(b, L, HG_HEADS, HG_DK)
    lbh = lb.reshape(HG_HEADS, HG_DK)
    logf = jnp.logaddexp(jnp.log(lbh), jnp.log1p(-lbh) + jax.nn.log_sigmoid(ff))
    kk = (1.0 - lbh) * jax.nn.sigmoid(-ff)
    v = iv.reshape(b, L, HG_HEADS, HG_DV)
    o, s_new = _chunked(_hgrn2_chunks, (q, kk, v, logf), s0, pad_front, chunk)
    o = _rmsnorm(o.astype(hn.dtype), hg_norm) * jax.nn.silu(gz.reshape(b, L, HG_HEADS, HG_DV))
    return o.reshape(b, L, HG_V) @ w_out, s_new

def _sq_relu_mlp(x, w_up, w_down):
    return jnp.square(jax.nn.relu(x @ w_up)) @ w_down

def setup_inputs(seed: int = 0) -> dict:
    key = jax.random.key(seed)
    ks = iter(jax.random.split(key, 32))

    def nrm(shape, scale):
        return scale * jax.random.normal(next(ks), shape, jnp.float32)

    n_pages = PAST_LEN // PAGE_SIZE
    n_used = DEC_BATCH * n_pages
    n_pool = n_used + n_used // 4
    page_table = jax.random.permutation(next(ks), n_pool)[:n_used].reshape(DEC_BATCH, n_pages).astype(jnp.int32)
    dn_a_log = jnp.log(jax.random.uniform(next(ks), (N_EVEN, DN_HEADS), jnp.float32, 1.0, 16.0))
    dt = jnp.exp(jax.random.uniform(next(ks), (N_EVEN, DN_HEADS), jnp.float32, math.log(1e-3), math.log(0.1)))
    dn_dt_bias = dt + jnp.log(-jnp.expm1(-dt))
    return {
        'x_prompt': nrm((BATCH, SEQ, D_MODEL), 1.0),
        'x_sample': nrm((DEC_BATCH, DEC_SEQ, D_MODEL), 1.0),
        'cache_k': nrm((N_EVEN, n_pool, PAGE_SIZE, A_KV_HEADS, A_HEAD_DIM), 1.0),
        'cache_v': nrm((N_EVEN, n_pool, PAGE_SIZE, A_KV_HEADS, A_HEAD_DIM), 1.0),
        'cache_ik': nrm((N_EVEN, n_pool, PAGE_SIZE, IDX_DIM), 1.0),
        'state_conv': nrm((N_EVEN, DEC_BATCH, CONV_W - 1, CONV_DIM), 1.0),
        'state_delta': nrm((N_EVEN, DEC_BATCH, DN_HEADS, DN_DK, DN_DV), 0.3),
        'state_hgrn': nrm((N_ODD, DEC_BATCH, HG_HEADS, HG_DK, HG_DV), 0.5),
        'page_table': page_table,
        'meta': nrm((N_META, D_MODEL), 1.0),
        'ln_mix': 1.0 + nrm((DEPTH, D_MODEL), 0.1),
        'ln_ffn': 1.0 + nrm((DEPTH, D_MODEL), 0.1),
        'ln_final': 1.0 + nrm((D_MODEL,), 0.1),
        'w_in_e': nrm((N_EVEN, D_MODEL, EVEN_IN), D_MODEL ** -0.5),
        'w_out_e': nrm((N_EVEN, EVEN_OUT, D_MODEL), EVEN_OUT ** -0.5),
        'dn_conv': nrm((N_EVEN, CONV_W, CONV_DIM), CONV_W ** -0.5),
        'dn_a_log': dn_a_log,
        'dn_dt_bias': dn_dt_bias,
        'dn_norm': 1.0 + nrm((N_EVEN, DN_DV), 0.1),
        'w_in_o': nrm((N_ODD, D_MODEL, ODD_IN), D_MODEL ** -0.5),
        'w_out_o': nrm((N_ODD, HG_V, D_MODEL), HG_V ** -0.5),
        'hg_lb': nrm((DEPTH, HG_F), 0.5),
        'hg_norm': 1.0 + nrm((N_ODD, HG_DV), 0.1),
        'w_up': nrm((DEPTH, D_MODEL, D_FF), D_MODEL ** -0.5),
        'w_down': nrm((DEPTH, D_FF, D_MODEL), D_FF ** -0.5),
    }

def reference(x_prompt, x_sample, cache_k, cache_v, cache_ik, state_conv, state_delta, state_hgrn, page_table,
              meta, ln_mix, ln_ffn, ln_final, w_in_e, w_out_e, dn_conv, dn_a_log, dn_dt_bias, dn_norm,
              w_in_o, w_out_o, hg_lb, hg_norm, w_up, w_down):
    dt = x_prompt.dtype
    bp, seq, _ = x_prompt.shape
    n_new = x_sample.shape[1]
    n_past = page_table.shape[1] * cache_k.shape[2]
    hp = jnp.concatenate([jnp.broadcast_to(meta.astype(dt)[None], (bp, N_META, D_MODEL)), x_prompt], axis=1)
    hs = x_sample
    pos_p = jnp.arange(hp.shape[1], dtype=jnp.int32)
    pos_s = n_past + jnp.arange(n_new, dtype=jnp.int32)
    ksel_p = min(TOPK_MAX, seq // 4)
    ksel_s = min(TOPK_MAX, (n_past + n_new) // 4)
    pad_p = (-N_META) % CHUNK
    chunk_s = min(CHUNK, n_new)
    lb_soft = jax.nn.softmax(hg_lb.astype(jnp.float32), axis=0)
    lb_all = jnp.cumsum(lb_soft, axis=0) - lb_soft[0]
    kp, vp, ikp, cp, dp, hgp = [], [], [], [], [], []
    ks, vs, iks, cs, ds, hgs = [], [], [], [], [], []
    for l in range(DEPTH):
        if l % 2 == 0:
            i = l // 2
            ew = (w_in_e[i], w_out_e[i], dn_conv[i], dn_a_log[i], dn_dt_bias[i], dn_norm[i])
            empty_kv = jnp.zeros((bp, 0, A_KV_HEADS, A_HEAD_DIM), dt)
            empty_ik = jnp.zeros((bp, 0, IDX_DIM), dt)
            conv0 = jnp.zeros((bp, CONV_W - 1, CONV_DIM), dt)
            s0 = jnp.zeros((bp, DN_HEADS, DN_DK, DN_DV), jnp.float32)
            out, k_, v_, ik_, buf, st = _even_mixer(_rmsnorm(hp, ln_mix[l]), pos_p, empty_kv, empty_kv, empty_ik,
                                                    conv0, s0, ksel_p, pad_p, CHUNK, *ew)
            hp = hp + out
            kp.append(k_); vp.append(v_); ikp.append(ik_); cp.append(buf); dp.append(st)
            out, k_, v_, ik_, buf, st = _even_mixer(_rmsnorm(hs, ln_mix[l]), pos_s,
                                                    _gather_pages(cache_k[i], page_table),
                                                    _gather_pages(cache_v[i], page_table),
                                                    _gather_pages(cache_ik[i], page_table),
                                                    state_conv[i], state_delta[i], ksel_s, 0, chunk_s, *ew)
            hs = hs + out
            ks.append(k_); vs.append(v_); iks.append(ik_); cs.append(buf); ds.append(st)
        else:
            j = l // 2
            s0 = jnp.zeros((bp, HG_HEADS, HG_DK, HG_DV), jnp.float32)
            out, st = _odd_mixer(_rmsnorm(hp, ln_mix[l]), s0, lb_all[l], pad_p, CHUNK, w_in_o[j], w_out_o[j], hg_norm[j])
            hp = hp + out
            hgp.append(st)
            out, st = _odd_mixer(_rmsnorm(hs, ln_mix[l]), state_hgrn[j], lb_all[l], 0, chunk_s, w_in_o[j], w_out_o[j], hg_norm[j])
            hs = hs + out
            hgs.append(st)
        hp = hp + _sq_relu_mlp(_rmsnorm(hp, ln_ffn[l]), w_up[l], w_down[l])
        hs = hs + _sq_relu_mlp(_rmsnorm(hs, ln_ffn[l]), w_up[l], w_down[l])
    y_prompt = _rmsnorm(hp, ln_final)[:, N_META:]
    y_sample = _rmsnorm(hs, ln_final)
    return (y_prompt, y_sample,
            jnp.stack(kp).astype(cache_k.dtype), jnp.stack(vp).astype(cache_v.dtype), jnp.stack(ikp).astype(cache_ik.dtype),
            jnp.stack(cp).astype(state_conv.dtype), jnp.stack(dp).astype(state_delta.dtype), jnp.stack(hgp).astype(state_hgrn.dtype),
            jnp.stack(ks).astype(cache_k.dtype), jnp.stack(vs).astype(cache_v.dtype), jnp.stack(iks).astype(cache_ik.dtype),
            jnp.stack(cs).astype(state_conv.dtype), jnp.stack(ds).astype(state_delta.dtype), jnp.stack(hgs).astype(state_hgrn.dtype))


_drawn_inputs = setup_inputs


def setup_inputs(seed=0):
    import zlib

    import numpy as np

    out = dict(_drawn_inputs(seed))
    spreads = {}
    factors = {}
    for name, (base, spread) in spreads.items():
        noise = np.random.default_rng([zlib.crc32(name.encode()), seed]).standard_normal(out[name].shape)
        drawn = base * np.exp(spread * noise) if base else spread * noise
        out[name] = jnp.asarray(drawn.astype(out[name].dtype))
    for name, factor in factors.items():
        out[name] = (out[name] * factor).astype(out[name].dtype)
    return out
```

```python
from contextlib import ExitStack

import numpy as np

import concourse.bass as bass
from concourse import mybir

F32 = mybir.dt.float32
I32 = mybir.dt.int32
ALU = mybir.AluOpType
ACT = mybir.ActivationFunctionType
AX = mybir.AxisListType

P = 128
D = 1024
KT = D // P
NS, QS = 8, 8
SAMP = NS * QS
META = 16
HEAD = SAMP + META
SEQ = 512
T = HEAD + SEQ
HALF = T // 2
NT = 1 + SEQ // P
PAST, PAGE = 256, 128
NPG = PAST // PAGE
NPOOL = 20
GROUP = 8
SLOTS = 4
A_HEADS, KVH, HD = 8, 2, 64
IDX_HEADS = 4
DNH = 4
HGH = 8
CONV_W = 4
NSEG = NS + 1
EPS = 1e-6
NEG = -3.0e38
K_PROMPT = SEQ // 4 - META
K_SAMPLE = (PAST + QS) // 4 - META

U_EVEN, U_OUT_E, U_UP, U_DOWN, U_ODD, U_OUT_O = 24, 8, 32, 32, 32, 8
UNITS = U_EVEN + U_OUT_E + U_UP + U_DOWN + U_ODD + U_OUT_O + U_UP + U_DOWN
Q0, K0, V0, Z0, IK0, AK0, IQ0, AQ0 = 0, 4, 8, 12, 16, 17, 18, 20

SMALL = P + IDX_HEADS + 2 * DNH
O_IW, O_DB, O_DA = P, P + 4, P + 8

ROWS = [HEAD] + [P] * (NT - 1)
COL0 = [0] + [HEAD + P * i for i in range(NT - 1)]
LEVELS = 7
HLEVELS = 6
HC = 64


def constant_table():
    parts = {}
    i = np.arange(P)
    parts["ident"] = np.eye(P)
    parts["ones"] = np.ones((P, P))
    half = HD // 4 // 2
    rot = np.zeros((P, P))
    for b in (0, HD):
        for d in range(half):
            rot[b + d, b + half + d] = -1.0
            rot[b + half + d, b + d] = 1.0
    parts["rotT"] = rot.T
    pos = np.concatenate([PAST + np.tile(np.arange(QS), NS), np.arange(META + SEQ)]).astype(np.float32)
    inv = (np.float32(500000.0) ** (-np.arange(half, dtype=np.float32) / np.float32(half))).astype(np.float32)
    ang = (pos[None, :] * inv[:, None]).astype(np.float32).astype(np.float64)
    cos, sin = np.ones((P, T)), np.zeros((P, T))
    for b in (0, HD):
        for r in (0, half):
            cos[b + r:b + r + half] = np.cos(ang)
            sin[b + r:b + r + half] = np.sin(ang)
    parts["cos"], parts["sin"] = cos, sin
    seg = np.full(P, -1)
    seg[:SAMP] = np.arange(SAMP) // QS
    seg[SAMP:HEAD] = NS
    same = (seg[:, None] == seg[None, :]) & (seg[:, None] >= 0)
    upper = i[:, None] <= i[None, :]
    for n, blk in (("0", same), ("1", np.ones((P, P), bool))):
        parts["cum" + n] = blk & upper
        parts["rest" + n] = blk & ~upper
        parts["decm" + n] = np.where(blk & upper, 0.0, NEG)
    sm = np.zeros((P, NSEG))
    sm[np.arange(HEAD), seg[:HEAD]] = 1
    parts["seg"] = sm
    for l in range(LEVELS):
        b = 1 << l
        parts[f"lev{l}"] = ((i[:, None] // (2 * b) == i[None, :] // (2 * b))
                            & (i[:, None] % (2 * b) < b) & (i[None, :] % (2 * b) >= b))
    parts["causal"] = np.where(i[None, :] <= i[:, None], 0.0, NEG)
    nb = np.full((P, SAMP), NEG)
    s = np.arange(SAMP)
    nb[:SAMP] = np.where((s[:, None] // QS == s[None, :] // QS) & (s[None, :] <= s[:, None]), 0.0, NEG)
    parts["newb"] = nb
    mb = np.full((P, HEAD), NEG)
    mb[:, SAMP:] = np.where(np.arange(META)[None, :] <= (i % META)[:, None], 0.0, NEG)
    parts["metab"] = mb
    ex = np.zeros((P, 2, P))
    for a in range(2):
        for c in range(P):
            ex[(4 * a + c // 32) * QS + c % QS, a, c] = 1
    parts["expand"] = ex.reshape(P, 2 * P)
    keep = np.ones((P, T))
    keep[:, 0:SAMP:QS] = 0
    keep[:, SAMP] = 0
    keep[:, HEAD::HC] = 0
    parts["eps"] = np.full((P, 1), EPS)
    parts["eps128"] = np.full((P, 1), EPS * P)
    parts["one"] = np.ones((P, 1))
    at, cols = {}, 0
    for n, v in parts.items():
        at[n] = (cols, v.shape[1])
        cols += v.shape[1]
    return np.concatenate([v.astype(np.float32) for v in parts.values()], axis=1), at, keep.astype(np.float32)


def hybrid_step(nc, x, consts, keep, at, w, wsmall, vecs, stconv, sdelta, shgrn, kpages, ikpages, vpages, ptab,
                y, krows, vrows, ikrows, convo_p, convo_s, delta_p, delta_s, hgrn_p, hgrn_s):
    ctx = ExitStack()
    with ctx:
        def sb(name, shape, dt=F32):
            return ctx.enter_context(nc.sbuf_tensor(name, shape, dt))

        def sem(name):
            return ctx.enter_context(nc.semaphore(name))

        ps = ctx.enter_context(nc.psum_tensor("ps", [P, 8, 512], F32))
        h = sb("h", [P, KT, T])
        xn = sb("xn", [P, KT, T])
        ring = sb("ring", [P, SLOTS, KT * P])
        cst = sb("cst", [P, consts.shape[1]])
        vec = sb("vec", [P, vecs.shape[1]])
        sq = sb("sq", [P, 2, T])
        rn = sb("rn", [P, T])
        NARENA = 31040
        arena = sb("arena", [P, NARENA])
        tokm = sb("tokm", [P, NT, SMALL])
        gates = sb("gates", [P, 8, NT * 4])
        pt_sb = sb("pt_sb", [1, NS * NPG], I32)

        def C(name):
            a, n = at[name]
            return cst[:, a:a + n]

        def region(a, *dims):
            n = int(np.prod(dims))
            assert a + n <= NARENA, (a, dims)
            v = arena[:, a:a + n]
            if len(dims) == 1:
                return v
            if len(dims) == 2:
                return v.rearrange("p (a b) -> p a b", a=dims[0])
            return v.rearrange("p (a b c) -> p a b c", a=dims[0], b=dims[1])

        V_LN = 0
        V_CONV = 40
        V_DN, V_HGN = 88, 89
        V_DTB, V_ALOG = 90, 94
        V_LB0, V_LB1 = 98, 106
        negA = sb("negA", [P, 4])
        lbv = sb("lbv", [P, 2, 8])

        proj = region(0, 24, T)
        ct = region(24 * T, 12, T)
        B = 36 * T
        kp = region(B, NS, PAST)
        ikp = region(B + NS * PAST, NS, PAST)
        vp = region(B + 2 * NS * PAST, NS * NPG, P)

        S = {}

        def sg(name):
            if name not in S:
                S[name] = sem(name)
            return S[name]

        const_in, x_in, small_in = sg("const_in"), sg("x_in"), sg("small_in")
        w_in = [sg(f"w_in{s}") for s in range(SLOTS)]
        w_used = sg("w_used")
        bank_free = sg("bank_free")
        dve_chain, act_chain, pool_chain = sg("dve_chain"), sg("act_chain"), sg("pool_chain")
        counts = {}

        def linker(eng, chain):
            def link(ins, name=None):
                s_ = sg(name) if name else chain
                counts[s_.name] = counts.get(s_.name, 0) + 1
                ins.then_inc(s_, 1)
                eng.wait_ge(s_, counts[s_.name])
            return link

        dlink = linker(nc.vector, dve_chain)
        alink = linker(nc.scalar, act_chain)
        plink = linker(nc.gpsimd, pool_chain)

        def pairs(v):
            return v.rearrange("p (n c) -> p n c", n=2)

        def heads(v, n=4):
            return v.rearrange("p (h c) -> p h c", h=n)

        class Units:
            even = 0
            out_e = U_EVEN
            up0 = out_e + U_OUT_E
            down0 = up0 + U_UP
            odd = down0 + U_DOWN
            out_o = odd + U_ODD
            up1 = out_o + U_OUT_O
            down1 = up1 + U_UP

        M_EVEN = 0
        M_OUT_E = M_EVEN + 24
        M_UP0 = M_OUT_E + 8
        M_DOWN0 = M_UP0 + 32
        M_ODD = M_DOWN0 + 8
        M_OUT_O = M_ODD + 32
        M_UP1 = M_OUT_O + 8
        M_DOWN1 = M_UP1 + 32


        def act_norm(n):
            for k in range(KT):
                if n == 0:
                    nc.scalar.wait_ge(x_in, 16)
                else:
                    m0 = (M_OUT_E, M_DOWN0, M_OUT_O, M_DOWN1)[n - 1]
                    nc.scalar.wait_ge(bank_free, m0 + k + 3)
                if KT * n + k >= 2:
                    nc.scalar.wait_ge(sg("norm_mm"), KT * n + k - 1)
                nc.scalar.activation(sq[:, k % 2, :], h[:, k, :], ACT.Square).then_inc(sg("norm_sq"), 1)
            nc.scalar.wait_ge(sg("norm_mm"), KT * (n + 1))
            if n:
                nc.scalar.wait_ge(sg("norm_x"), n)
            nc.scalar.activation(pairs(rn[:, :]), ps[:, 6:8, 0:HALF], ACT.Sqrt, scale=1.0 / D,
                                 bias=C("eps")).then_inc(sg("norm_rt"), 1)

        def pe_norm(n):
            for k in range(KT):
                nc.tensor.wait_ge(sg("norm_sq"), KT * n + k + 1)
                if n and k == 0:
                    nc.tensor.wait_ge(sg("norm_rt"), n)
                for e in range(2):
                    mm = nc.tensor.matmul(ps[:, 6 + e, 0:HALF], C("ones"), sq[:, k % 2, e * HALF:(e + 1) * HALF],
                                          start=(k == 0), stop=(k == KT - 1))
                mm.then_inc(sg("norm_mm"), 1)

        def dve_norm(n, dst, link):
            nc.vector.wait_ge(sg("norm_rt"), n + 1)
            link(nc.vector.reciprocal(rn[:, :], rn[:, :]))
            for k in range(KT):
                ins = nc.vector.scalar_tensor_tensor(out=dst[:, k, :], in0=h[:, k, :],
                                                     scalar=vec[:, V_LN + 8 * n + k:V_LN + 8 * n + k + 1],
                                                     in1=rn[:, :], op0=ALU.mult, op1=ALU.mult)
            ins.then_inc(sg("norm_x"), 1)

        def pe_unit(slot, pair, k0, rhs, first, last):
            for k in range(KT):
                for e in range(2):
                    mm = nc.tensor.matmul(ps[:, 2 * pair + e, 0:HALF], ring[:, slot, k * P:(k + 1) * P],
                                          rhs[:, k0 + k, e * HALF:(e + 1) * HALF],
                                          start=(first and k == 0), stop=(last and k == KT - 1))
            mm.then_inc(w_used, 1)

        def pe_dense(groups, u0, m0, rhs):
            with nc.tensor.Fori(0, groups) as i:
                for j in range(GROUP):
                    nc.tensor.wait_ge(w_in[j % SLOTS], 16 * (u0 // SLOTS + GROUP // SLOTS * i + j // SLOTS + 1))
                    nc.tensor.wait_ge(bank_free, m0 + 1 + GROUP * i + j)
                    pe_unit(j % SLOTS, j % 2, 0, rhs, True, True)

        def pe_down(u0, m0, rhs):
            with nc.tensor.Fori(0, U_DOWN // GROUP) as i:
                for j in range(GROUP):
                    nc.tensor.wait_ge(w_in[j % SLOTS], 16 * (u0 // SLOTS + GROUP // SLOTS * i + j // SLOTS + 1))
                    if j % 4 == 0:
                        nc.tensor.wait_ge(bank_free, m0 + 1 + 2 * i + j // 4)
                    pe_unit(j % SLOTS, j // 4, KT * (j % 4), rhs, j % 4 == 0, j % 4 == 3)

        def act_copy_out(groups, u0, dst, func=ACT.Copy):
            with nc.scalar.Fori(0, groups) as i:
                for j in range(GROUP):
                    nc.scalar.wait_ge(w_used, u0 + 1 + GROUP * i + j)
                    nc.scalar.wait_ge(const_in, 32)
                    nc.scalar.activation(pairs(dst[:, GROUP * i + j, :]),
                                         ps[:, 2 * (j % 2):2 * (j % 2) + 2, 0:HALF], func).then_inc(bank_free, 1)

        def dve_square(m0):
            with nc.vector.Fori(0, U_UP // GROUP) as i:
                for j in range(GROUP):
                    nc.vector.wait_ge(bank_free, m0 + 3 + GROUP * i + j)
                    t_ = hid[:, GROUP * i + j, :]
                    nc.vector.tensor_tensor(t_, t_, t_, ALU.mult).then_inc(sg("hid_ready"), 1)

        def act_relu(u0):
            with nc.scalar.Fori(0, U_UP // GROUP) as i:
                for j in range(GROUP):
                    nc.scalar.wait_ge(w_used, u0 + 1 + GROUP * i + j)
                    nc.scalar.wait_ge(const_in, 32)
                    nc.scalar.activation(pairs(hid[:, GROUP * i + j, :]),
                                         ps[:, 2 * (j % 2):2 * (j % 2) + 2, 0:HALF], ACT.Relu).then_inc(bank_free, 1)

        def dve_residual(groups, per, u0):
            n = GROUP // per
            with nc.vector.Fori(0, groups) as i:
                for j in range(n):
                    nc.vector.wait_ge(w_used, u0 + GROUP * i + per * (j + 1))
                    nc.vector.tensor_tensor(pairs(h[:, n * i + j, :]), pairs(h[:, n * i + j, :]),
                                            ps[:, 2 * (j % 2):2 * (j % 2) + 2, 0:HALF], ALU.add)\
                        .then_inc(bank_free, 1)

        hid = region(0, 32, T)

        def pe_small():
            nc.tensor.wait_ge(small_in, 16)
            for t in range(NT):
                if t >= 2:
                    nc.tensor.wait_ge(sg("small_ev"), t - 1)
                for k in range(KT):
                    mm = nc.tensor.matmul(ps[0:ROWS[t], 4 + t % 2, 0:SMALL], xn[:, k, COL0[t]:COL0[t] + ROWS[t]],
                                          wsm[:, k, :], start=(k == 0), stop=(k == KT - 1))
                mm.then_inc(sg("small_mm"), 1)

        wsm = region(B + 3 * NS * PAST, KT, SMALL)

        def G(n):
            return gates[:, n, :].rearrange("p (t h) -> p t h", t=NT)

        def bct(v):
            return v.rearrange("p (o h) -> p o h", o=1).to_broadcast([P, NT, 4])

        G_BETA, G_G, G_IW, G_A, G_B, G_C, G_ED = range(7)

        def dve_small(link):
            link(nc.vector.memset(tokm[:, 0, :], 0.0))
            for t in range(NT):
                nc.vector.wait_ge(sg("small_mm"), t + 1)
                link(nc.vector.tensor_copy(tokm[0:ROWS[t], t, :], ps[0:ROWS[t], 4 + t % 2, 0:SMALL]), "small_ev")
            link(nc.vector.tensor_tensor(G(G_A), tokm[:, :, O_DA:O_DA + 4], bct(vec[:, V_DTB:V_DTB + 4]), ALU.add))
            nc.vector.tensor_scalar(G(G_IW), tokm[:, :, O_IW:O_IW + 4], (IDX_HEADS * HD) ** -0.5, None, ALU.mult)
            link(nc.vector.tensor_scalar(G(G_C), G(G_A), 0.0, None, ALU.max), "gate_z")
            nc.vector.wait_ge(sg("gate_act"), 5)
            link(nc.vector.tensor_tensor(G(G_C), G(G_C), G(G_B), ALU.add))
            link(nc.vector.scalar_tensor_tensor(out=G(G_G), in0=G(G_C), scalar=-1.0,
                                                in1=bct(negA[:, :]), op0=ALU.mult, op1=ALU.mult), "gate_g")

        def act_small():
            nc.scalar.wait_ge(sg("gate_z"), 1)
            nc.scalar.activation(negA[:, :], vec[:, V_ALOG:V_ALOG + 4], ACT.Exp).then_inc(sg("gate_act"), 1)
            nc.scalar.activation(G(G_BETA), tokm[:, :, O_DB:O_DB + 4], ACT.Sigmoid).then_inc(sg("gate_act"), 1)
            nc.scalar.activation(G(G_B), G(G_A), ACT.Abs).then_inc(sg("gate_act"), 1)
            nc.scalar.wait_ge(sg("gate_act"), 3)
            nc.scalar.activation(G(G_B), G(G_B), ACT.Exp, scale=-1.0).then_inc(sg("gate_act"), 1)
            nc.scalar.wait_ge(sg("gate_act"), 4)
            nc.scalar.activation(G(G_B), G(G_B), ACT.Ln, bias=C("one")).then_inc(sg("gate_act"), 1)

        ROPED = list(range(IK0, 24))

        def pe_rope():
            nc.tensor.wait_ge(bank_free, M_OUT_E + 2)
            for n, m in enumerate(ROPED):
                if n >= 2:
                    nc.tensor.wait_ge(sg("rope_s"), n - 1)
                for e in range(2):
                    mm = nc.tensor.matmul(ps[:, 2 * (n % 2) + e, 0:HALF], C("rotT"),
                                          proj[:, m, e * HALF:(e + 1) * HALF], start=True, stop=True)
                mm.then_inc(sg("rope_mm"), 1)

        def pool_rope():
            for n, m in enumerate(ROPED):
                nc.gpsimd.wait_ge(sg("rope_mm"), n + 1)
                nc.gpsimd.tensor_tensor(proj[:, m, :], proj[:, m, :], C("cos"), ALU.mult).then_inc(sg("rope_c"), 1)

        def dve_rope(link):
            for n, m in enumerate(ROPED):
                nc.vector.wait_ge(sg("rope_mm"), n + 1)
                link(nc.vector.tensor_tensor(pairs(sq[:, n % 2, :]), ps[:, 2 * (n % 2):2 * (n % 2) + 2, 0:HALF],
                                             pairs(C("sin")), ALU.mult), "rope_s")
                nc.vector.wait_ge(sg("rope_c"), n + 1)
                nc.vector.tensor_tensor(proj[:, m, :], proj[:, m, :], sq[:, n % 2, :], ALU.add)\
                    .then_inc(sg("roped"), 1)

        hist = region(B + 3 * NS * PAST + KT * SMALL, 12, NS, CONV_W - 1 + QS)

        def pool_conv():
            nc.gpsimd.wait_ge(sg("hist_in"), 16)
            nc.gpsimd.wait_ge(bank_free, M_OUT_E + 2)
            full = hist.rearrange("p m s q -> p m (s q)")
            link = plink
            link(nc.gpsimd.tensor_copy(hist[:, :, :, 3:11],
                                       proj[:, 0:12, 0:SAMP].rearrange("p m (s q) -> p m s q", s=NS)))
            tmp = region(B + 3 * NS * PAST + KT * SMALL + 12 * 88, 12, SAMP)
            t4 = tmp.rearrange("p m (s q) -> p m s q", s=NS)
            c4 = ct[:, :, 0:SAMP].rearrange("p m (s q) -> p m s q", s=NS)
            for m in range(12):
                for j in range(CONV_W):
                    o = c4 if j == 0 else t4
                    wv = vec[:, V_CONV + 4 * m + j:V_CONV + 4 * m + j + 1]
                    ins = nc.gpsimd.tensor_scalar(o[:, m], hist[:, m, :, j:j + QS], wv, None, ALU.mult)
                    link(ins)
                    if j:
                        link(nc.gpsimd.tensor_tensor(c4[:, m], c4[:, m], t4[:, m], ALU.add),
                             "conv_s" if j == CONV_W - 1 else None)

        def dve_conv(link):
            nc.vector.wait_ge(bank_free, M_OUT_E + 2)
            for m in range(12):
                def tap(j):
                    return vec[:, V_CONV + 4 * m + j:V_CONV + 4 * m + j + 1]
                link(nc.vector.tensor_scalar(ct[:, m, SAMP:T], proj[:, m, SAMP:T], tap(3), None, ALU.mult))
                for j in (2, 1, 0):
                    d = 3 - j
                    link(nc.vector.scalar_tensor_tensor(out=ct[:, m, SAMP + d:T], in0=proj[:, m, SAMP:T - d],
                                                        scalar=tap(j), in1=ct[:, m, SAMP + d:T],
                                                        op0=ALU.mult, op1=ALU.add), "conv_p" if j == 0 else None)

        def act_silu():
            for m in range(12):
                nc.scalar.wait_ge(sg("conv_p"), m + 1)
                nc.scalar.wait_ge(sg("conv_s"), m + 1)
                nc.scalar.activation(ct[:, m, :], ct[:, m, :], ACT.Silu).then_inc(sg("silu"), 1)

        def act_l2():
            for n in range(8):
                nc.scalar.wait_ge(sg("silu"), n + 1)
                if n == 0:
                    nc.scalar.wait_ge(sg("roped"), len(ROPED))
                if n >= 2:
                    nc.scalar.wait_ge(sg("l2_mm"), n - 1)
                nc.scalar.activation(sq[:, n % 2, :], ct[:, n, :], ACT.Square).then_inc(sg("l2_sq"), 1)
                if n >= 1:
                    act_l2_root(n - 1)
            act_l2_root(7)

        l2r = [rn[:, :], region(B + 3 * NS * PAST + KT * SMALL + 12 * 88 + 12 * SAMP, T)]

        def act_l2_root(n):
            nc.scalar.wait_ge(sg("l2_mm"), n + 1)
            if n >= 2:
                nc.scalar.wait_ge(sg("l2_done"), n - 1)
            sc, b = (float(P), C("eps128")) if n < 4 else (1.0, C("eps"))
            nc.scalar.activation(pairs(l2r[n % 2]), ps[:, 2 * (n % 2):2 * (n % 2) + 2, 0:HALF], ACT.Sqrt,
                                 scale=sc, bias=b).then_inc(sg("l2_rt"), 1)

        def pe_l2():
            for n in range(8):
                nc.tensor.wait_ge(sg("l2_sq"), n + 1)
                if n == 0:
                    nc.tensor.wait_ge(sg("rope_s"), len(ROPED))
                if n >= 2:
                    nc.tensor.wait_ge(sg("l2_rt"), n - 1)
                for e in range(2):
                    mm = nc.tensor.matmul(ps[:, 2 * (n % 2) + e, 0:HALF], C("ones"),
                                          sq[:, n % 2, e * HALF:(e + 1) * HALF], start=True, stop=True)
                mm.then_inc(sg("l2_mm"), 1)

        def dve_l2(link):
            for n in range(8):
                nc.vector.wait_ge(sg("l2_rt"), n + 1)
                link(nc.vector.reciprocal(l2r[n % 2], l2r[n % 2]))
                nc.vector.tensor_tensor(ct[:, n, :], ct[:, n, :], l2r[n % 2], ALU.mult).then_inc(sg("l2_done"), 1)

        GD = B
        xflat = xn.rearrange("p k t -> p (k t)")

        def in_xn(a):
            return xflat[:, a:a + 512].rearrange("p (h c) -> p h c", h=4)

        Tt = [region(GD + 512 * t, 4, P) for t in range(NT)]
        kd = [region(GD + 2560 + 512 * t, 4, P) for t in range(NT)]
        at_s = [region(GD + 5120, 4, P)] + [in_xn(4 * T + 512 * e) for e in range(4)]
        st = region(GD + 5632, 4, NS * P)
        X = [region(512 * t, 4, P) for t in range(NT)]
        Ti = [region(2560 + 512 * t, 4, P) for t in range(NT)]
        dec = [region(5120 + 512 * e, 4, P) for e in range(2)]
        XL = [region(6144, 4, P), rn[:, 0:512].rearrange("p (h c) -> p h c", h=4)]
        P1 = sq[:, 0, 0:512].rearrange("p (h c) -> p h c", h=4)
        ebc = sq[:, 1, 0:512].rearrange("p (h c) -> p h c", h=4)
        gcol = sb("gcol", [P, NT, 8])
        egl = sb("egl", [P, NT, 4, NSEG])

        def kT(hd, t):
            return ct[:, 4 + hd, COL0[t]:COL0[t] + ROWS[t]]

        def qT(hd, t):
            return ct[:, hd, COL0[t]:COL0[t] + ROWS[t]]

        def bank(b, R=P, C_=P):
            return ps[0:R, b, :].rearrange("p (h c) -> p h c", h=4)[:, :, 0:C_]

        def nseg(t):
            return NSEG if t == 0 else 1

        def pe_gdn_prep():
            nc.tensor.wait_ge(sg("gate_g"), 1)
            nc.tensor.wait_ge(sg("l2_done"), 8)
            nc.tensor.wait_ge(sg("mix_a"), len(DONE))
            for t in range(NT):
                R, v = ROWS[t], "0" if t == 0 else "1"
                g = G(G_G)[0:R, t, :]
                if t:
                    nc.tensor.wait_ge(sg("gd_col"), t)
                    nc.tensor.wait_ge(sg("gd_egl"), t)
                nc.tensor.matmul(ps[0:R, 4, 0:4], C("cum" + v)[0:R, 0:R], g, start=True, stop=True)
                nc.tensor.matmul(ps[0:R, 4, 4:8], C("rest" + v)[0:R, 0:R], g, start=True, stop=True)
                ends = C("seg")[0:R, :] if t == 0 else C("one")[0:R, :]
                for hd in range(DNH):
                    mm = nc.tensor.matmul(ps[:, 4, 16 + NSEG * hd:16 + NSEG * hd + nseg(t)],
                                          g[:, hd:hd + 1].to_broadcast([R, P]), ends, start=True, stop=True)
                mm.then_inc(sg("gd_a"), 1)
                if t:
                    nc.tensor.wait_ge(sg("gd_dec"), t)
                    nc.tensor.wait_ge(sg("gd_ebc"), t)
                for hd in range(DNH):
                    mm = nc.tensor.matmul(bank(5, P, R)[:, hd], g[:, hd:hd + 1].to_broadcast([R, P]),
                                          C("cum" + v)[0:R, 0:R], start=True, stop=True)
                mm.then_inc(sg("gd_b"), 1)
                if t:
                    nc.tensor.wait_ge(sg("gd_attn"), t)
                    nc.tensor.wait_ge(sg("gd_x"), t)
                    nc.tensor.wait_ge(sg("gd_kd"), t)
                for hd in range(DNH):
                    nc.tensor.matmul(bank(6, R, R)[:, hd], kT(hd, t), qT(hd, t), start=True, stop=True)
                    nc.tensor.matmul(bank(7, R, R)[:, hd], kT(hd, t), kT(hd, t), start=True, stop=True)
                    mm = nc.tensor.transpose(bank(0, R)[:, hd], kT(hd, t), C("ident"))
                mm.then_inc(sg("gd_c"), 1)

        def dve_gdn_prep(link):
            for t in range(NT):
                R, v, e = ROWS[t], "0" if t == 0 else "1", t % 2
                nc.vector.wait_ge(sg("gd_a"), t + 1)
                link(nc.vector.tensor_copy(gcol[0:R, t, :], ps[0:R, 4, 0:8]), "gd_col")
                nc.vector.wait_ge(sg("gd_b"), t + 1)
                for hd in range(DNH):
                    ins = nc.vector.scalar_tensor_tensor(out=dec[e][0:R, hd, 0:R], in0=bank(5, R, R)[:, hd],
                                                         scalar=gcol[0:R, t, hd:hd + 1],
                                                         in1=C("decm" + v)[0:R, 0:R], op0=ALU.subtract, op1=ALU.add)
                link(ins, "gd_dec")
                nc.vector.wait_ge(sg("gd_c"), t + 1)
                nc.vector.wait_ge(sg("gd_ex"), t + 1)
                link(nc.vector.tensor_tensor(at_s[t][0:R, :, 0:R], bank(6, R, R), dec[e][0:R, :, 0:R], ALU.mult),
                     "gd_attn")
                for hd in range(DNH):
                    ins = nc.vector.scalar_tensor_tensor(out=X[t][0:R, hd, 0:R], in0=bank(7, R, R)[:, hd],
                                                         scalar=G(G_BETA)[0:R, t, hd:hd + 1],
                                                         in1=dec[e][0:R, hd, 0:R], op0=ALU.mult, op1=ALU.mult)
                link(ins, "gd_x")
                nc.vector.wait_ge(sg("gd_ebc"), t + 1)
                q_, k_ = ct[:, 0:4, COL0[t]:COL0[t] + R], ct[:, 4:8, COL0[t]:COL0[t] + R]
                nc.vector.tensor_tensor(q_, q_, ebc[:, :, 0:R], ALU.mult)
                link(nc.vector.scalar_tensor_tensor(out=k_, in0=k_, scalar=-1.0, in1=ebc[:, :, 0:R],
                                                    op0=ALU.mult, op1=ALU.mult), "gd_qk")

        def act_gdn_prep():
            for t in range(NT):
                R, e = ROWS[t], t % 2
                nc.scalar.wait_ge(sg("gd_col"), t + 1)
                alink(nc.scalar.activation(G(G_ED)[0:R, t, :], gcol[0:R, t, 4:8], ACT.Exp))
                nc.scalar.activation(egl[:, t, :, 0:nseg(t)],
                                     ps[:, 4, 16:16 + 4 * NSEG].rearrange("p (h s) -> p h s", h=4)[:, :, 0:nseg(t)],
                                     ACT.Exp).then_inc(sg("gd_egl"), 1)
                nc.scalar.wait_ge(sg("gd_dec"), t + 1)
                nc.scalar.activation(dec[e][0:R, :, 0:R], dec[e][0:R, :, 0:R], ACT.Exp).then_inc(sg("gd_ex"), 1)
                if t:
                    nc.scalar.wait_ge(sg("gd_qk"), t)
                nc.scalar.activation(ebc[:, :, 0:R], bank(5, P, R), ACT.Exp).then_inc(sg("gd_ebc"), 1)
                nc.scalar.wait_ge(sg("gd_c"), t + 1)
                for hd in range(DNH):
                    ins = nc.scalar.activation(kd[t][0:R, hd, :], bank(0, R)[:, hd], ACT.Copy,
                                               scale=G(G_ED)[0:R, t, hd:hd + 1])
                ins.then_inc(sg("gd_kd"), 1)

        INV = [(l, t) for l in range(LEVELS) for t in range(NT) if t or l < 4]
        LAST = {t: (3 if t == 0 else LEVELS - 1) for t in range(NT)}

        def pool_inv():
            for n, (l, t) in enumerate(INV):
                R = ROWS[t]
                if l == 0:
                    nc.gpsimd.wait_ge(sg("gd_x"), t + 1)
                if n >= 2:
                    nc.gpsimd.wait_ge(sg("inv_used"), n - 1)
                m = C(f"lev{l}")[0:R, 0:R].rearrange("p (o c) -> p o c", o=1).to_broadcast([R, 4, R])
                nc.gpsimd.tensor_tensor(XL[n % 2][0:R, :, 0:R], X[t][0:R, :, 0:R], m, ALU.mult)\
                    .then_inc(sg("inv_xl"), 1)

        def pe_inv():
            n1 = 0
            for n, (l, t) in enumerate(INV):
                R = ROWS[t]
                nc.tensor.wait_ge(sg("inv_xl"), n + 1)
                if n:
                    nc.tensor.wait_ge(sg("inv_used"), n)
                if l == 0:
                    if n == 0:
                        nc.tensor.wait_ge(sg("l2_rt"), 8)
                    for hd in range(DNH):
                        mm = nc.tensor.transpose(bank(2, R, R)[:, hd], XL[n % 2][0:R, hd, 0:R], C("ident")[0:R, 0:R])
                    mm.then_inc(sg("inv_2"), 1)
                    continue
                for hd in range(DNH):
                    mm = nc.tensor.matmul(bank(1, R, R)[:, hd], XL[n % 2][0:R, hd, 0:R], Ti[t][0:R, hd, 0:R],
                                          start=True, stop=True)
                mm.then_inc(sg("inv_1"), 1)
                n1 += 1
                nc.tensor.wait_ge(sg("inv_p1"), n1)
                for hd in range(DNH):
                    if l < LAST[t]:
                        nc.tensor.matmul(bank(2, R, R)[:, hd], Tt[t][0:R, hd, 0:R], P1[0:R, hd, 0:R],
                                         start=True, stop=True)
                    mm = nc.tensor.matmul(bank(3, R, R)[:, hd], P1[0:R, hd, 0:R], Tt[t][0:R, hd, 0:R],
                                          start=True, stop=True)
                mm.then_inc(sg("inv_2"), 1)

        def act_inv():
            n1 = 0
            for n, (l, t) in enumerate(INV):
                R = ROWS[t]
                if l:
                    n1 += 1
                    nc.scalar.wait_ge(sg("inv_1"), n1)
                    nc.scalar.activation(P1[0:R, :, 0:R], bank(1, R, R), ACT.Copy).then_inc(sg("inv_p1"), 1)

        def dve_inv(link):
            for n, (l, t) in enumerate(INV):
                R = ROWS[t]
                nc.vector.wait_ge(sg("inv_2"), n + 1)
                if l == 0:
                    i4 = C("ident")[0:R, 0:R].rearrange("p (o c) -> p o c", o=1).to_broadcast([R, 4, R])
                    nc.vector.wait_ge(sg("inv_xl"), n + 1)
                    nc.vector.tensor_tensor(Ti[t][0:R, :, 0:R], i4, bank(2, R, R), ALU.subtract)
                    link(nc.vector.tensor_tensor(Tt[t][0:R, :, 0:R], i4, XL[n % 2][0:R, :, 0:R], ALU.subtract),
                         "inv_used")
                    continue
                if l < LAST[t]:
                    nc.vector.tensor_tensor(Ti[t][0:R, :, 0:R], Ti[t][0:R, :, 0:R], bank(2, R, R), ALU.subtract)
                link(nc.vector.tensor_tensor(Tt[t][0:R, :, 0:R], Tt[t][0:R, :, 0:R], bank(3, R, R), ALU.subtract),
                     "inv_used")

        RB = 512 * 10
        rbuf = region(RB, 4, P)
        vnew = region(RB + 512, 4, P)
        rT = region(RB + 1024, 4, P)
        sp_st = sb("sp_st", [P, 2, 4, P])
        vmask = region(0, NSEG, P)
        oT = region(2560, 4, T)

        def pe_gdn_scan():
            nc.tensor.wait_ge(sg("inv_used"), len(INV))
            nc.tensor.wait_ge(sg("gd_qk"), NT)
            nc.tensor.wait_ge(sg("st_in"), 16)
            for hd in range(DNH):
                for s in range(NS):
                    mm = nc.tensor.matmul(bank(0, P, HEAD)[:, hd, QS * s:QS * (s + 1)],
                                          st[:, hd, P * s:P * (s + 1)], kT(hd, 0)[:, QS * s:QS * (s + 1)],
                                          start=True, stop=True)
            mm.then_inc(sg("sc_ks"), 1)
            nc.tensor.wait_ge(sg("sc_rt"), 1)
            for hd in range(DNH):
                mm = nc.tensor.transpose(bank(1, HEAD)[:, hd], rT[:, hd, 0:HEAD], C("ident"))
            mm.then_inc(sg("sc_r"), 1)
            for t in range(NT):
                R = ROWS[t]
                if t:
                    nc.tensor.wait_ge(sg("sc_s"), t)
                    for hd in range(DNH):
                        nc.tensor.matmul(bank(1, R)[:, hd], ct[:, 8 + hd, COL0[t]:COL0[t] + R], C("ident"),
                                         start=True, stop=False)
                        mm = nc.tensor.matmul(bank(1, R)[:, hd], kT(hd, t), sp_st[:, t % 2, hd, :],
                                              start=False, stop=True)
                    mm.then_inc(sg("sc_r"), 1)
                nc.tensor.wait_ge(sg("sc_rb"), t + 1)
                for hd in range(DNH):
                    mm = nc.tensor.matmul(bank(2, R)[:, hd], Tt[t][0:R, hd, 0:R], rbuf[0:R, hd, :],
                                          start=True, stop=True)
                mm.then_inc(sg("sc_v"), 1)
                nc.tensor.wait_ge(sg("sc_vn"), t + 1)
                if t:
                    for hd in range(DNH):
                        mm = nc.tensor.matmul(bank(4)[:, hd], kd[t][0:R, hd, :], vnew[0:R, hd, :],
                                              start=True, stop=True)
                    mm.then_inc(sg("sc_kv"), 1)
                    nc.tensor.wait_ge(sg("sc_ob"), t)
                for hd in range(DNH):
                    o = bank(3, P, R)[:, hd]
                    if t:
                        nc.tensor.matmul(o, sp_st[:, t % 2, hd, :], qT(hd, t), start=True, stop=False)
                    else:
                        for s in range(NS):
                            nc.tensor.matmul(o[:, QS * s:QS * (s + 1)], st[:, hd, P * s:P * (s + 1)],
                                             qT(hd, 0)[:, QS * s:QS * (s + 1)], start=(s == 0), stop=False,
                                             skip_group_check=True)
                    mm = nc.tensor.matmul(o, vnew[0:R, hd, :], at_s[t][0:R, hd, 0:R], start=False, stop=True,
                                          skip_group_check=(t == 0))
                mm.then_inc(sg("sc_o"), 1)
                if t == 0:
                    for hd in range(DNH):
                        nc.tensor.wait_ge(sg("sc_vm"), hd + 1)
                        if hd:
                            nc.tensor.wait_ge(sg("sc_kv0"), hd)
                        for b, (a, n) in enumerate(((0, 4), (4, 4), (8, 1))):
                            mm = nc.tensor.matmul(ps[:, 4 + b, 0:n * P], kd[0][0:R, hd, :],
                                                  vmask[0:R, a:a + n, :].rearrange("p s c -> p (s c)"),
                                                  start=True, stop=True)
                        mm.then_inc(sg("sc_kvm"), 1)

        def pool_gdn_scan():
            nc.gpsimd.wait_ge(sg("sc_vn"), 1)
            for hd in range(DNH):
                if hd:
                    nc.gpsimd.wait_ge(sg("sc_kvm"), hd)
                nc.gpsimd.tensor_tensor(vmask[0:HEAD], vnew[0:HEAD, hd:hd + 1, :].to_broadcast([HEAD, NSEG, P]),
                                        C("seg")[0:HEAD, :].rearrange("p (s o) -> p s o", o=1)
                                        .to_broadcast([HEAD, NSEG, P]), ALU.mult).then_inc(sg("sc_vm"), 1)

        def act_gdn_scan():
            for t in range(NT):
                R = ROWS[t]
                nc.scalar.wait_ge(sg("sc_r"), t + 1)
                nc.scalar.activation(rbuf[0:R], bank(1, R), ACT.Copy).then_inc(sg("sc_rb"), 1)
                nc.scalar.wait_ge(sg("sc_v"), t + 1)
                if t == 1:
                    nc.scalar.wait_ge(sg("sc_vm"), DNH)
                if t:
                    nc.scalar.wait_ge(sg("sc_o"), t)
                for hd in range(DNH):
                    ins = nc.scalar.activation(vnew[0:R, hd, :], bank(2, R)[:, hd], ACT.Copy,
                                               scale=G(G_BETA)[0:R, t, hd:hd + 1])
                ins.then_inc(sg("sc_vn"), 1)

        def dve_gdn_scan(link):
            nc.vector.wait_ge(sg("sc_ks"), 1)
            nc.vector.tensor_copy(rT[:, :, SAMP:HEAD], ct[:, 8:12, SAMP:HEAD])
            link(nc.vector.tensor_tensor(rT[:, :, 0:SAMP], ct[:, 8:12, 0:SAMP], bank(0, P, SAMP), ALU.add), "sc_rt")
            for t in range(NT):
                R = ROWS[t]
                if t == 0:
                    nc.vector.wait_ge(sg("sc_o"), 1)
                    nc.vector.tensor_copy(oT[:, :, 0:HEAD], bank(3, P, HEAD)).then_inc(sg("sc_ob"), 1)
                    for hd in range(DNH):
                        nc.vector.wait_ge(sg("sc_kvm"), hd + 1)
                        for s in range(NS):
                            nc.vector.scalar_tensor_tensor(out=st[:, hd, P * s:P * (s + 1)],
                                                           in0=st[:, hd, P * s:P * (s + 1)],
                                                           scalar=egl[:, 0, hd, s:s + 1],
                                                           in1=ps[:, 4 + s // 4, P * (s % 4):P * (s % 4 + 1)],
                                                           op0=ALU.mult, op1=ALU.add)
                        link(nc.vector.tensor_copy(sp_st[:, 1, hd, :], ps[:, 6, 0:P]), "sc_kv0")
                    nc.vector.sem_inc(sg("sc_s"), 1)
                    continue
                nc.vector.wait_ge(sg("sc_kv"), t)
                for hd in range(DNH):
                    ins = nc.vector.scalar_tensor_tensor(out=sp_st[:, (t + 1) % 2, hd, :], in0=sp_st[:, t % 2, hd, :],
                                                         scalar=egl[:, t, hd, 0:1], in1=bank(4)[:, hd],
                                                         op0=ALU.mult, op1=ALU.add)
                link(ins, "sc_s")
                nc.vector.wait_ge(sg("sc_o"), t + 1)
                nc.vector.tensor_copy(oT[:, :, COL0[t]:COL0[t] + R], bank(3, P, R)).then_inc(sg("sc_ob"), 1)

        def gate_norm(eng, nh, o, z, nv, out_, tag, base_bank):
            if eng == "act":
                for n in range(nh):
                    if n == 0:
                        nc.scalar.wait_ge(*o["ready"])
                    if n >= 2:
                        nc.scalar.wait_ge(sg(tag + "_mm"), n - 1)
                    nc.scalar.activation(sq[:, n % 2, :], o["v"](n), ACT.Square).then_inc(sg(tag + "_sq"), 1)
                    nc.scalar.wait_ge(sg(tag + "_mm"), n + 1)
                    if n:
                        nc.scalar.wait_ge(sg(tag + "_x"), n)
                    nc.scalar.activation(pairs(rn[:, :]), ps[:, base_bank:base_bank + 2, 0:HALF], ACT.Sqrt,
                                         scale=1.0 / P, bias=C("eps")).then_inc(sg(tag + "_rt"), 1)
                return
            if eng == "pe":
                for n in range(nh):
                    nc.tensor.wait_ge(sg(tag + "_sq"), n + 1)
                    if n:
                        nc.tensor.wait_ge(sg(tag + "_rt"), n)
                    for e in range(2):
                        mm = nc.tensor.matmul(ps[:, base_bank + e, 0:HALF], C("ones"),
                                              sq[:, n % 2, e * HALF:(e + 1) * HALF], start=True, stop=True)
                    mm.then_inc(sg(tag + "_mm"), 1)
                return
            for n in range(nh):
                nc.vector.wait_ge(sg(tag + "_rt"), n + 1)
                dlink(nc.vector.reciprocal(rn[:, :], rn[:, :]))
                dlink(nc.vector.scalar_tensor_tensor(out=o["v"](n), in0=o["v"](n), scalar=vec[:, nv:nv + 1],
                                                     in1=rn[:, :], op0=ALU.mult, op1=ALU.mult), tag + "_x")
                nc.vector.tensor_tensor(out_(n), o["v"](n), z(n), ALU.mult).then_inc(sg(tag + "_out"), 1)

        O_E = {"ready": (sg("sc_ob"), NT), "v": lambda n: oT[:, n, :]}
        O_O = {"ready": (sg("hp_ob"), SEQ // HC), "v": lambda n: region(0, HGH, T)[:, n, :]}

        def z_e(n):
            return proj[:, Z0 + n, :]

        def z_o(n):
            return proj[:, 16 + n, :]

        def out_e(n):
            return xn[:, 4 + n, :]

        def out_o(n):
            return xn[:, n, :]

        bias = [None] + [region(o, HEAD + P * i) for i, o in ((1, 0), (2, 208), (3, 544), (4, 1008))]
        sbias = region(1600, PAST + HEAD)
        ebias = region(1936, 2, PAST + HEAD)
        sc, wk, gt, eq, cum = [region(2608 + 512 * n, 512) for n in range(5)]
        rel = [region(2608 + 2560 + 512 * n, 512) for n in range(2)]
        qs = region(6192, NS, 4, QS)
        qm = region(6448, 4, META)
        iqpad = region(B + 3 * NS * PAST, 2, NS, SAMP)
        best = sb("best", [P, 8])
        cnt = sb("cnt", [P, 2])
        SEL = [(t, ROWS[t], P * t) for t in range(1, NT)] + [(0, SAMP, PAST + SAMP)]

        def pool_sample_queries():
            nc.gpsimd.wait_ge(sg("roped"), len(ROPED))
            nc.gpsimd.wait_ge(sg("small_mm"), NT)
            nc.gpsimd.wait_ge(sg("silu"), 12)
            nc.gpsimd.wait_ge(sg("conv_out"), 32)
            plink(nc.gpsimd.memset(iqpad, 0.0))
            for s in range(NS):
                c = slice(QS * s, QS * (s + 1))
                ins = nc.gpsimd.tensor_copy(iqpad[:, :, s, c], proj[:, IQ0:IQ0 + 2, c])
            ins.then_inc(sg("sq_ready"), 1)
            nc.gpsimd.tensor_copy(qs.rearrange("p s h q -> p h s q"),
                                  proj[:, AQ0:AQ0 + 4, 0:SAMP].rearrange("p h (s q) -> p h s q", s=NS))\
                .then_inc(sg("sq_ready"), 1)
            nc.gpsimd.tensor_copy(qm, proj[:, AQ0:AQ0 + 4, SAMP:HEAD]).then_inc(sg("sq_ready"), 1)

        def pe_scores():
            nc.tensor.wait_ge(sg("roped"), len(ROPED))
            nc.tensor.wait_ge(sg("l2_rt"), 8)
            n = 0
            for t, R, W in SEL:
                for hd in range(IDX_HEADS):
                    b = HD * (hd % 2)
                    q = proj[b:b + HD, IQ0 + hd // 2, COL0[t]:COL0[t] + R]
                    if n >= 4:
                        nc.tensor.wait_ge(sg("idx_rel"), n - 3)
                    if t:
                        mm = nc.tensor.matmul(ps[:, n % 4, 0:W], q, proj[b:b + HD, IK0, HEAD:HEAD + W],
                                              start=True, stop=True)
                    else:
                        if hd == 0:
                            nc.tensor.wait_ge(sg("pages_in"), 16 * 4 * NS * NPG)
                            nc.tensor.wait_ge(sg("sq_ready"), 3)
                        for s in range(NS):
                            nc.tensor.matmul(ps[0:SAMP, n % 4, 0:PAST], iqpad[b:b + HD, hd // 2, s, :],
                                             ikp[b:b + HD, s, :], start=(s == 0), stop=(s == NS - 1))
                        mm = nc.tensor.matmul(ps[0:SAMP, n % 4, PAST:PAST + SAMP], q, proj[b:b + HD, IK0, 0:SAMP],
                                              start=True, stop=True)
                    mm.then_inc(sg("idx_mm"), 1)
                    n += 1

        def act_scores():
            n = 0
            for t, R, W in SEL:
                for hd in range(IDX_HEADS):
                    nc.scalar.wait_ge(sg("idx_mm"), n + 1)
                    if n >= 2:
                        nc.scalar.wait_ge(sg("idx_acc"), n - 1)
                    if n == 0:
                        nc.scalar.wait_ge(sg("silu"), 12)
                    nc.scalar.activation(rel[n % 2][0:R, 0:W], ps[0:R, n % 4, 0:W], ACT.Relu)\
                        .then_inc(sg("idx_rel"), 1)
                    n += 1

        def dve_select(link):
            n = 0
            nc.vector.wait_ge(sg("silu"), 12)
            for t, R, W in SEL:
                v = slice(0, R)
                for hd in range(IDX_HEADS):
                    nc.vector.wait_ge(sg("idx_rel"), n + 1)
                    wv = G(G_IW)[v, t, hd:hd + 1]
                    if hd == 0:
                        link(nc.vector.tensor_scalar(sc[v, 0:W], rel[n % 2][v, 0:W], wv, None, ALU.mult), "idx_acc")
                    else:
                        link(nc.vector.scalar_tensor_tensor(out=sc[v, 0:W], in0=rel[n % 2][v, 0:W], scalar=wv,
                                                            in1=sc[v, 0:W], op0=ALU.mult, op1=ALU.add), "idx_acc")
                    n += 1
                last = slice(W - P, W) if t else slice(PAST, PAST + SAMP)
                hide = C("causal") if t else C("newb")[v]
                link(nc.vector.tensor_tensor(sc[v, last], sc[v, last], hide, ALU.add))
                a, K = (0, K_PROMPT) if t else (META, K_SAMPLE)
                s_, k_, g_, e_, c_ = (u[v, a:W] for u in (sc, wk, gt, eq, cum))
                link(nc.vector.max(best[v, :], s_))
                for r in range(1, -(-K // 8)):
                    link(nc.vector.match_replace(out=k_, in_to_replace=best[v, :], in_values=s_ if r == 1 else k_,
                                                 imm_value=NEG))
                    link(nc.vector.max(best[v, :], k_))
                thr = best[v, (K - 1) % 8:(K - 1) % 8 + 1]
                link(nc.vector.tensor_scalar(g_, s_, thr, 0.0, ALU.is_gt, ALU.add, accum_out=cnt[v, 0:1]))
                link(nc.vector.tensor_scalar(e_, s_, thr, None, ALU.is_equal))
                link(nc.vector.tensor_scalar(cnt[v, 1:2], cnt[v, 0:1], -1.0, float(K), ALU.mult, ALU.add))
                link(nc.vector.tensor_tensor_scan(c_, C("one")[v].to_broadcast([R, W - a]), e_, 0.0,
                                                  ALU.mult, ALU.add))
                link(nc.vector.scalar_tensor_tensor(out=c_, in0=c_, scalar=cnt[v, 1:2], in1=e_,
                                                    op0=ALU.is_le, op1=ALU.mult))
                link(nc.vector.tensor_tensor(g_, g_, c_, ALU.add))
                if t:
                    out_ = bias[t]
                    nc.vector.memset(out_[:, 0:SAMP], NEG)
                    nc.vector.memset(out_[:, SAMP:HEAD], 0.0)
                    link(nc.vector.tensor_scalar(out_[:, HEAD:HEAD + W], g_, -1.0, -NEG, ALU.add, ALU.mult))
                    d = out_[:, HEAD + W - P:HEAD + W]
                    link(nc.vector.tensor_tensor(d, d, C("causal"), ALU.min), "chosen")
                else:
                    nc.vector.memset(sbias[v, 0:META], 0.0)
                    nc.vector.memset(sbias[v, PAST + SAMP:PAST + HEAD], NEG)
                    link(nc.vector.tensor_scalar(sbias[v, META:W], g_, -1.0, -NEG, ALU.add, ALU.mult))
                    d = sbias[v, PAST:PAST + SAMP]
                    link(nc.vector.tensor_tensor(d, d, C("newb")[v], ALU.min), "chosen")
            nc.vector.wait_ge(sg("ex_mm"), 1)
            for a in range(2):
                ins = nc.vector.tensor_copy(ebias[:, a, :], ps[:, 4 + a, 0:PAST + HEAD])
            link(ins, "chosen")

        def pe_expand():
            nc.tensor.wait_ge(sg("chosen"), NT)
            for a in range(2):
                mm = nc.tensor.matmul(ps[:, 4 + a, 0:PAST + HEAD], C("expand")[0:SAMP, P * a:P * (a + 1)],
                                      sbias[0:SAMP, :], start=True, stop=True)
            mm.then_inc(sg("ex_mm"), 1)

        ITEMS = [("p", t, hd) for t in range(1, NT) for hd in range(A_HEADS)]
        ITEMS += [("s", g, a) for g in range(KVH) for a in range(2)] + [("m", 0, 0)]
        lm = [region(2608 + T * e, T) for e in range(2)]
        pT = [region(2608 + 2 * T + 640 * e, 5, P) for e in range(2)]
        on = region(2608 + 2 * T + 1280, 512)
        mx = sb("mx", [P, 2])
        rsum = sb("rsum", [P, 3, 8])

        def width(it):
            return {"p": HEAD + P * it[1], "s": PAST + HEAD, "m": HEAD}[it[0]]

        def logits(n):
            W, pr = width(ITEMS[n]), 2 * (n % 2)
            return ps[:, pr, 0:W] if W <= 512 else ps[:, pr:pr + 2, 0:W // 2]

        def as_logits(v):
            return v if v.shape[1] <= 512 else pairs(v)

        def key_tiles(it):
            if it[0] == "p":
                return [(ROWS[u], COL0[u]) for u in range(it[1] + 1)]
            if it[0] == "s":
                return [(P, 0), (P, P), (HEAD, PAST)]
            return [(HEAD, 0)]

        def pe_logits(n):
            it = ITEMS[n]
            W = width(it)
            if n >= 2:
                nc.tensor.wait_ge(sg("lg_max"), n - 1)
            if it[0] == "p":
                g, j = it[2] // 4, it[2] % 4
                q = proj[HD * g:HD * (g + 1), AQ0 + j, COL0[it[1]]:COL0[it[1]] + P]
                k = proj[HD * g:HD * (g + 1), AK0, :]
                if W <= 512:
                    mm = nc.tensor.matmul(ps[:, 2 * (n % 2), 0:W], q, k[:, 0:W], start=True, stop=True)
                else:
                    for e in range(2):
                        mm = nc.tensor.matmul(ps[:, 2 * (n % 2) + e, 0:W // 2], q, k[:, e * W // 2:(e + 1) * W // 2],
                                              start=True, stop=True)
            elif it[0] == "s":
                g, a = it[1:]
                b = slice(HD * g, HD * (g + 1))
                qa = qs[b, 4 * a:4 * a + 4].rearrange("p s h q -> p (s h q)")
                for s in range(4):
                    nc.tensor.matmul(ps[32 * s:32 * (s + 1), 2 * (n % 2), 0:PAST], qa[:, 32 * s:32 * (s + 1)],
                                     kp[b, 4 * a + s, :], start=True, stop=True)
                mm = nc.tensor.matmul(ps[:, 2 * (n % 2), PAST:PAST + HEAD], qa, proj[b, AK0, 0:HEAD],
                                      start=True, stop=True)
            else:
                for g in range(KVH):
                    b = slice(HD * g, HD * (g + 1))
                    mm = nc.tensor.matmul(ps[b, 2 * (n % 2), 0:HEAD], qm[b].rearrange("p h q -> p (h q)"),
                                          proj[b, AK0, 0:HEAD], start=True, stop=True)
            mm.then_inc(sg("lg_mm"), 1)

        def turned(it, u):
            if it[0] == "p":
                return (5, P * (u // 4)) if u % 4 == 0 else (4, P * (u - 1))
            return (5, 0) if it[0] == "m" or u == 2 else (4, P * u)

        def pe_turn(n):
            it = ITEMS[n]
            nc.tensor.wait_ge(sg("pr_exp"), n + 1)
            if n:
                nc.tensor.wait_ge(sg("pr_ev_a"), n)
                nc.tensor.wait_ge(sg("pr_ev_d"), n)
            for u, (K, c) in enumerate(key_tiles(it)):
                tb, tc = turned(it, u)
                mm = nc.tensor.transpose(ps[0:K, tb, tc:tc + P], lm[n % 2][:, c:c + K], C("ident"))
            mm.then_inc(sg("pr_tr"), 1)

        def pe_values(n):
            it = ITEMS[n]
            tiles = key_tiles(it)
            nc.tensor.wait_ge(sg("pr_ev_a"), n + 1)
            nc.tensor.wait_ge(sg("pr_ev_d"), n + 1)
            if it[0] == "p":
                hd = it[2]
                if hd == 0 and it[1] > 1:
                    nc.tensor.wait_ge(sg("o_ev"), it[1] - 1)
                for u, (K, c) in enumerate(tiles):
                    mm = nc.tensor.matmul(ps[:, 6, HD * hd:HD * (hd + 1)], pT[n % 2][0:K, u, :],
                                          tokm[0:K, u, HD * (hd // 4):HD * (hd // 4 + 1)],
                                          start=(u == 0), stop=(u == len(tiles) - 1))
            else:
                nc.tensor.wait_ge(sg("o_ev"), NT - 1 + ITEMS_S.index(n))
                if it[0] == "s":
                    g, a = it[1:]
                    for s in range(4):
                        for u, (K, c) in enumerate(tiles):
                            vv = vp[:, NPG * (4 * a + s) + u, HD * g:HD * (g + 1)] if u < NPG else \
                                tokm[0:K, 0, HD * g:HD * (g + 1)]
                            mm = nc.tensor.matmul(ps[32 * s:32 * (s + 1), 6, 0:HD],
                                                  pT[n % 2][0:K, u, 32 * s:32 * (s + 1)], vv,
                                                  start=(u == 0), stop=(u == len(tiles) - 1))
                else:
                    for g in range(KVH):
                        mm = nc.tensor.matmul(ps[HD * g:HD * (g + 1), 6, 0:HD],
                                              pT[n % 2][0:HEAD, 0, HD * g:HD * (g + 1)],
                                              tokm[0:HEAD, 0, HD * g:HD * (g + 1)], start=True, stop=True)
            mm.then_inc(sg("o_mm"), 1)

        ITEMS_S = [n for n, it in enumerate(ITEMS) if it[0] != "p"]
        DONE = [n for n, it in enumerate(ITEMS) if it[0] != "p" or it[2] == A_HEADS - 1]

        def pe_o_turn(n):
            d = DONE.index(n)
            nc.tensor.wait_ge(sg("o_ev"), d + 1)
            if d:
                nc.tensor.wait_ge(sg("mix_a"), d)
            if ITEMS[n][0] == "p":
                for u in range(4):
                    mm = nc.tensor.transpose(ps[:, 7, P * u:P * (u + 1)], on[:, P * u:P * (u + 1)], C("ident"))
            else:
                mm = nc.tensor.transpose(ps[0:HD, 7, 0:P], on[:, 0:HD], C("ident"))
            mm.then_inc(sg("o_tr"), 1)

        def pe_attention():
            nc.tensor.wait_ge(sg("sq_ready"), 3)
            nc.tensor.wait_ge(sg("pages_in"), 16 * 4 * NS * NPG)
            nc.tensor.wait_ge(sg("idx_rel"), IDX_HEADS * NT)
            nc.tensor.wait_ge(sg("chosen"), NT + 1)
            pe_logits(0)
            for n in range(len(ITEMS)):
                if n + 1 < len(ITEMS):
                    pe_logits(n + 1)
                pe_turn(n)
                pe_values(n)
                if n in DONE:
                    pe_o_turn(n)

        def dve_attention(link):
            for n in range(len(ITEMS) + 1):
                if n < len(ITEMS):
                    it = ITEMS[n]
                    W = width(it)
                    b = bias[it[1]] if it[0] == "p" else ebias[:, it[2], :] if it[0] == "s" else C("metab")
                    nc.vector.wait_ge(sg("lg_mm"), n + 1)
                    if n >= 2:
                        nc.vector.wait_ge(sg("pr_tr"), n - 1)
                    link(nc.vector.tensor_tensor_reduce(
                        out=as_logits(lm[n % 2][:, 0:W]), in0=logits(n), in1=as_logits(b[:, 0:W]), scale=1.0,
                        scalar=NEG, op0=ALU.add, op1=ALU.max, accum_out=mx[:, n % 2:n % 2 + 1]))
                    link(nc.vector.tensor_scalar(mx[:, n % 2:n % 2 + 1], mx[:, n % 2:n % 2 + 1], -HD ** -0.5, None,
                                                 ALU.mult), "lg_max")
                if n == 0:
                    continue
                m = n - 1
                it = ITEMS[m]
                nc.vector.wait_ge(sg("pr_tr"), m + 1)
                if m >= 2:
                    nc.vector.wait_ge(sg("o_mm"), m - 1)
                u = 2 if it[0] == "s" else 0
                ins = nc.vector.tensor_copy(pT[m % 2][0:HEAD, u, :], ps[0:HEAD, 5, 0:P])
                if it[0] == "p" and it[1] == 4:
                    ins = nc.vector.tensor_copy(pT[m % 2][:, 4, :], ps[:, 5, P:2 * P])
                ins.then_inc(sg("pr_ev_d"), 1)
                if m in DONE:
                    d = DONE.index(m)
                    nc.vector.wait_ge(sg("o_mm"), m + 1)
                    if d:
                        nc.vector.wait_ge(sg("o_tr"), d)
                    if it[0] == "p":
                        rs = rsum[:, it[1] % 2, :]
                        link(nc.vector.reciprocal(rs, rs))
                        link(nc.vector.tensor_tensor(on.rearrange("p (h c) -> p h c", h=8),
                                                     ps[:, 6, :].rearrange("p (h c) -> p h c", h=8),
                                                     rs.rearrange("p (h o) -> p h o", o=1)
                                                     .to_broadcast([P, 8, HD]), ALU.mult), "o_ev")
                    else:
                        rs = rsum[:, 2, m - len(ITEMS) + 5:m - len(ITEMS) + 6]
                        link(nc.vector.reciprocal(rs, rs))
                        link(nc.vector.tensor_scalar(on[:, 0:HD], ps[:, 6, 0:HD], rs, None, ALU.mult), "o_ev")

        def act_attention():
            for n in range(len(ITEMS) + 1):
                if n < len(ITEMS):
                    it = ITEMS[n]
                    nc.scalar.wait_ge(sg("lg_max"), n + 1)
                    if it[0] == "p":
                        rs = rsum[:, it[1] % 2, it[2]:it[2] + 1]
                        if it[2] == 0 and it[1] >= 3:
                            nc.scalar.wait_ge(sg("o_ev"), it[1] - 2)
                    else:
                        rs = rsum[:, 2, n - len(ITEMS) + 5:n - len(ITEMS) + 6]
                    p = lm[n % 2][:, 0:width(it)]
                    nc.scalar.activation(p, p, ACT.Exp, scale=HD ** -0.5, bias=mx[:, n % 2:n % 2 + 1], accum_out=rs)\
                        .then_inc(sg("pr_exp"), 1)
                if n == 0:
                    continue
                m = n - 1
                it = ITEMS[m]
                nc.scalar.wait_ge(sg("pr_tr"), m + 1)
                if m >= 2:
                    nc.scalar.wait_ge(sg("o_mm"), m - 1)
                if it[0] == "p":
                    N = min(it[1], 3)
                    ins = nc.scalar.activation(pT[m % 2][:, 1:1 + N, :].rearrange("p u c -> p (u c)"),
                                               ps[:, 4, 0:P * N], ACT.Copy)
                    ins.then_inc(sg("pr_ev_a"), 1)
                elif it[0] == "s":
                    nc.scalar.activation(pT[m % 2][:, 0:2, :].rearrange("p u c -> p (u c)"), ps[:, 4, 0:2 * P],
                                         ACT.Copy).then_inc(sg("pr_ev_a"), 1)
                else:
                    nc.scalar.sem_inc(sg("pr_ev_a"), 1)
                if m in DONE:
                    nc.scalar.wait_ge(sg("o_tr"), DONE.index(m) + 1)
                    if it[0] == "p":
                        nc.scalar.activation(xn[:, 0:4, COL0[it[1]]:COL0[it[1]] + P],
                                             ps[:, 7, :].rearrange("p (u c) -> p u c", u=4), ACT.Copy)\
                            .then_inc(sg("mix_a"), 1)
                        continue
                    for e in range(2):
                        if it[0] == "s":
                            g, a = it[1:]
                            src = ps[0:HD, 7, 0:P].rearrange("p (s h q) -> p h s q", s=4, h=4)[:, e::2]
                            dst = xn[HD * e:HD * (e + 1), 2 * g:2 * g + 2, 32 * a:32 * (a + 1)]\
                                .rearrange("p h (s q) -> p h s q", s=4)
                        else:
                            src = ps[0:HD, 7, 0:P].rearrange("p (h q) -> p h q", h=8)[:, e::2]
                            dst = xn[HD * e:HD * (e + 1), 0:4, SAMP:HEAD]
                        ins = nc.scalar.activation(dst, src, ACT.Copy)
                    ins.then_inc(sg("mix_a"), 1)

        v5 = region(24 * T, NT, HGH * P)
        kd5 = region(24 * T + 5120, NT, HGH * P)
        at5 = region(24 * T + 10240, HGH, NT, P)
        hmask = region(24 * T + 15360, NSEG, P)
        xt = [xn[:, k, :] for k in range(KT)]
        cb, lg, kk, dd, ee, kdT = xt[0], xt[1], xt[2], xt[3], (xt[4], xt[5]), xt[6]
        xe = [sq[:, 0, :], sq[:, 1, :]]
        hst = [xflat[:, 4 * T + 1024 * e:4 * T + 1024 * (e + 1)].rearrange("p (s c) -> p s c", s=NS) for e in range(2)]
        hp_st = [xflat[:, 1024 * e:1024 * (e + 1)].rearrange("p (h c) -> p h c", h=HGH) for e in range(2)]
        oT5 = region(0, HGH, T)
        ecl = sb("ecl", [P, HGH, NSEG + SEQ // HC])
        FROM = [0, 0, 0, SAMP, HEAD, HEAD]

        def pe_values5():
            for j in range(GROUP):
                u, m = Units.odd + 24 + j, M_ODD + 24 + j
                nc.tensor.wait_ge(w_in[j % SLOTS], 16 * (u // SLOTS + 1))
                nc.tensor.wait_ge(bank_free, m + 1)
                b = 2 * (j % 2)
                for t in range(NT):
                    o = ps[0:ROWS[t], b + 1, 0:P] if t == 0 else ps[:, b, P * (t - 1):P * t]
                    for k in range(KT):
                        mm = nc.tensor.matmul(o, xn[:, k, COL0[t]:COL0[t] + ROWS[t]],
                                              ring[:, j % SLOTS, P * k:P * (k + 1)],
                                              start=(k == 0), stop=(k == KT - 1))
                mm.then_inc(w_used, 1)

        def act_values5():
            for j in range(GROUP):
                nc.scalar.wait_ge(w_used, Units.odd + 24 + j + 1)
                b = 2 * (j % 2)
                nc.scalar.activation(v5[:, 1:NT, P * j:P * (j + 1)], ps[:, b, :].rearrange("p (t c) -> p t c", t=4),
                                     ACT.Copy)
                nc.scalar.activation(v5[0:HEAD, 0, P * j:P * (j + 1)], ps[0:HEAD, b + 1, 0:P], ACT.Copy)\
                    .then_inc(bank_free, 1)

        def lower_bounds():
            dlink(nc.vector.tensor_tensor(lbv[:, 0, :], vec[:, V_LB1:V_LB1 + 8], vec[:, V_LB0:V_LB0 + 8],
                                          ALU.subtract))
            dlink(nc.vector.tensor_scalar(lbv[:, 1, :], lbv[:, 0, :], -1.0, None, ALU.mult), "lb_diff")

        def blocks(v, l):
            b = 1 << l
            return v[:, FROM[l]:T].rearrange("p (n o b) -> p n o b", o=2, b=b)

        NL = HLEVELS + 1

        def ends(v):
            out = []
            for a, n, c in ((0, NS, QS), (SAMP, 1, META), (HEAD, SEQ // HC, HC)):
                w_ = v[:, a:a + n * c].rearrange("p (n c) -> p n c", c=c)
                out.append((w_, w_[:, :, c - 1:c]))
            return out

        def act_hgrn():
            nc.scalar.wait_ge(sg("lb_diff"), 1)
            alink(nc.scalar.activation(lbv[:, :, :], lbv[:, :, :], ACT.Sigmoid), "lb")
            for hd in range(HGH):
                if hd:
                    nc.scalar.wait_ge(sg("hg_done"), hd)
                    nc.scalar.wait_ge(sg("hg_kdt"), hd)
                nc.scalar.activation(kk, proj[:, hd, :], ACT.Sigmoid, scale=-1.0).then_inc(sg("hg_sig"), 1)
                nc.scalar.activation(lg, proj[:, hd, :], ACT.Sigmoid).then_inc(sg("hg_sig"), 1)
                nc.scalar.wait_ge(sg("hg_f"), hd + 1)
                nc.scalar.activation(lg, lg, ACT.Ln).then_inc(sg("hg_ln"), 1)
                for e in range(HLEVELS + 2):
                    n = (HLEVELS + 2) * hd + e
                    if e == 1:
                        nc.scalar.wait_ge(sg("hg_cb"), hd + 1)
                        nc.scalar.activation(lg, cb, ACT.Exp).then_inc(sg("hg_ecb"), 1)
                        continue
                    i = (HLEVELS + 1) * hd + (0 if e == 0 else e - 1)
                    nc.scalar.wait_ge(sg("hg_dif"), i + 1)
                    if i >= 2:
                        nc.scalar.wait_ge(sg("hg_mul"), i - 1)
                    a = 0 if e == 0 else FROM[e - 2]
                    nc.scalar.activation(ee[i % 2][:, a:T], dd[:, a:T], ACT.Exp).then_inc(sg("hg_exp"), 1)
                nc.scalar.wait_ge(sg("hg_kt"), hd + 1)
                nc.scalar.activation(kd5[:, 1:NT, P * hd:P * (hd + 1)],
                                     ps[:, 4, :].rearrange("p (t c) -> p t c", t=4), ACT.Copy)
                nc.scalar.activation(kd5[0:HEAD, 0, P * hd:P * (hd + 1)], ps[0:HEAD, 5, 0:P], ACT.Copy)\
                    .then_inc(sg("hg_kdt"), 1)

        def pool_hgrn():
            nc.gpsimd.memset(at5, 0.0).then_inc(sg("hg_zero"), 1)
            for hd in range(HGH):
                nc.gpsimd.wait_ge(sg("hg_cb"), hd + 1)
                i = (HLEVELS + 1) * hd
                if i:
                    nc.gpsimd.wait_ge(sg("hg_exp"), i)
                for (w_, l_), (o_, _) in zip(ends(cb), ends(dd)):
                    ins = nc.gpsimd.tensor_tensor(o_, l_.to_broadcast(list(w_.shape)), w_, ALU.subtract)
                ins.then_inc(sg("hg_dif"), 1)
                for l in range(HLEVELS):
                    nc.gpsimd.wait_ge(sg("hg_exp"), i + l + 1)
                    b = 1 << l
                    c_, d_ = blocks(cb, l), blocks(dd, l)
                    mid = c_[:, :, 0, b - 1:b].to_broadcast([P, c_.shape[1], b])
                    nc.gpsimd.tensor_tensor(d_[:, :, 0, :], mid, c_[:, :, 0, :], ALU.subtract)
                    nc.gpsimd.tensor_tensor(d_[:, :, 1, :], c_[:, :, 1, :], mid, ALU.subtract)\
                        .then_inc(sg("hg_dif"), 1)

        def dve_hgrn(link):
            nc.vector.wait_ge(sg("hg_zero"), 1)
            nc.vector.wait_ge(sg("lb"), 1)
            nc.vector.wait_ge(sg("keep_in"), 16)
            for hd in range(HGH):
                i = (HLEVELS + 1) * hd
                q = proj[:, 8 + hd, :]
                nc.vector.wait_ge(sg("hg_sig"), 2 * hd + 2)
                nc.vector.tensor_scalar(kk, kk, lbv[:, 1, hd:hd + 1], None, ALU.mult)
                link(nc.vector.tensor_scalar(lg, lg, lbv[:, 1, hd:hd + 1], lbv[:, 0, hd:hd + 1], ALU.mult, ALU.add),
                     "hg_f")
                nc.vector.wait_ge(sg("hg_ln"), hd + 1)
                if hd:
                    nc.vector.wait_ge(sg("hg_dif"), i)
                link(nc.vector.tensor_tensor_scan(cb, C("sin"), lg, 0.0, ALU.mult, ALU.add), "hg_cb")
                nc.vector.wait_ge(sg("hg_exp"), i + 1)
                if hd:
                    nc.vector.wait_ge(sg("hg_kt"), hd)
                nc.vector.tensor_tensor(kdT, kk, ee[i % 2], ALU.mult).then_inc(sg("hg_mul"), 1)
                for l in range(HLEVELS):
                    n = NL * hd + l
                    nc.vector.wait_ge(sg("hg_exp"), i + l + 2)
                    if n >= 2:
                        nc.vector.wait_ge(sg("hg_g"), xe_reader(hd, l))
                    e_, x_ = blocks(ee[(i + l + 1) % 2], l), blocks(xe[l % 2], l)
                    nc.vector.tensor_tensor(x_[:, :, 0, :], blocks(kk, l)[:, :, 0, :], e_[:, :, 0, :], ALU.mult)
                    nc.vector.tensor_tensor(x_[:, :, 1, :], blocks(q, l)[:, :, 1, :], e_[:, :, 1, :], ALU.mult)\
                        .then_inc(sg("hg_mul"), 1)
                    if l:
                        take(hd, l - 1)
                take(hd, HLEVELS - 1)
                take(hd, HLEVELS)
                nc.vector.wait_ge(sg("hg_ecb"), hd + 1)
                link(nc.vector.tensor_tensor(q, q, lg, ALU.mult))
                a = 0
                for _, l_ in ends(lg):
                    n = l_.shape[1]
                    ins = nc.vector.tensor_copy(ecl[:, hd, a:a + n].rearrange("p (n o) -> p n o", o=1), l_)
                    a += n
                link(ins, "hg_done")

        def xe_reader(hd, l):
            return NL * hd + l - 1 if l >= 2 else NL * (hd - 1) + HLEVELS - 1 + (l % 2)

        def take(hd, l):
            n = NL * hd + l
            m = C("ident" if l == HLEVELS else f"lev{l}").bitcast(I32)
            nc.vector.wait_ge(sg("hg_g"), n + 1)
            b = 2 * (n % 2)
            nc.vector.copy_predicated(at5[:, hd, 1:NT, :], m.rearrange("p (o c) -> p o c", o=1).to_broadcast([P, 4, P]),
                                      ps[:, b, :].rearrange("p (t c) -> p t c", t=4))
            r = slice(0, HEAD) if l < 3 or l == HLEVELS else slice(SAMP, HEAD)
            if l <= 3 or l == HLEVELS:
                ins = nc.vector.copy_predicated(at5[r, hd, 0, r], m[r, r], ps[r, b + 1, r])
                dlink(ins, "hg_take")
            else:
                dlink(nc.vector.memset(cnt[:, 0:1], 0.0), "hg_take")

        def pe_hgrn():
            for hd in range(HGH):
                for l in range(NL):
                    n = NL * hd + l
                    i = (HLEVELS + 1) * hd
                    if n >= 2:
                        nc.tensor.wait_ge(sg("hg_take"), n - 1)
                    nc.tensor.wait_ge(sg("hg_mul"), i + min(l + 2, HLEVELS + 1))
                    b = 2 * (n % 2)
                    x_ = xe[l % 2]
                    for t in range(NT):
                        c = slice(COL0[t], COL0[t] + ROWS[t])
                        o = ps[0:HEAD, b + 1, 0:HEAD] if t == 0 else ps[:, b, P * (t - 1):P * t]
                        if l == HLEVELS:
                            mm = nc.tensor.matmul(o, kk[:, c], proj[:, 8 + hd, c], start=True, stop=True)
                        elif t or l < 3:
                            mm = nc.tensor.matmul(o, x_[:, c], x_[:, c], start=True, stop=True)
                        elif l == 3:
                            c = slice(SAMP, HEAD)
                            mm = nc.tensor.matmul(ps[c, b + 1, c], x_[:, c], x_[:, c], start=True, stop=True)
                    mm.then_inc(sg("hg_g"), 1)
                    if l == 0:
                        if hd:
                            nc.tensor.wait_ge(sg("hg_kdt"), hd)
                        for t in range(NT):
                            c = slice(COL0[t], COL0[t] + ROWS[t])
                            o = ps[0:HEAD, 5, 0:P] if t == 0 else ps[:, 4, P * (t - 1):P * t]
                            mm = nc.tensor.transpose(o, kdT[:, c], C("ident"))
                        mm.then_inc(sg("hg_kt"), 1)

        def pe_hgrn_scan():
            nc.tensor.wait_ge(sg("hg_done"), HGH)
            nc.tensor.wait_ge(sg("hg_kdt"), HGH)
            for hd in range(HGH):
                nc.tensor.wait_ge(sg("hs_in" + str(hd % 2)), 16 * (hd // 2 + 1))
                if hd:
                    nc.tensor.wait_ge(sg("hs_ob"), hd)
                o = ps[:, 0, 0:HEAD]
                for s in range(NS):
                    c = slice(QS * s, QS * (s + 1))
                    nc.tensor.matmul(ps[:, 0, c], hst[hd % 2][:, s, :], proj[:, 8 + hd, c], start=(s == 0),
                                     stop=False, skip_group_check=True)
                mm = nc.tensor.matmul(o, v5[0:HEAD, 0, P * hd:P * (hd + 1)], at5[0:HEAD, hd, 0, 0:HEAD],
                                      start=False, stop=True, skip_group_check=True)
                mm.then_inc(sg("hs_o"), 1)
                nc.tensor.wait_ge(sg("hs_vm"), hd + 1)
                if hd:
                    nc.tensor.wait_ge(sg("hs_s"), hd)
                for b, (a, n) in enumerate(((0, 4), (4, 4), (8, 1))):
                    mm = nc.tensor.matmul(ps[:, 1 + b, 0:n * P], kd5[0:HEAD, 0, P * hd:P * (hd + 1)],
                                          hmask[0:HEAD, a:a + n, :].rearrange("p s c -> p (s c)"),
                                          start=True, stop=True)
                mm.then_inc(sg("hs_kv"), 1)
            nc.tensor.wait_ge(sg("hs_ob"), HGH)
            nc.tensor.wait_ge(sg("hs_s"), HGH)
            for c in range(SEQ // HC):
                t, r = 1 + c // 2, slice(HC * (c % 2), HC * (c % 2) + HC)
                c0 = HEAD + HC * c
                kv = 2 + 2 * (c % 2)
                if c >= 2:
                    nc.tensor.wait_ge(sg("hp_s"), c - 1)
                for hd in range(HGH):
                    mm = nc.tensor.matmul(ps[:, kv + hd // 4, P * (hd % 4):P * (hd % 4 + 1)],
                                          kd5[r, t, P * hd:P * (hd + 1)], v5[r, t, P * hd:P * (hd + 1)],
                                          start=True, stop=True)
                mm.then_inc(sg("hp_kv"), 1)
                if c:
                    nc.tensor.wait_ge(sg("hp_s"), c)
                if c >= 2:
                    nc.tensor.wait_ge(sg("hp_ob"), c - 1)
                for hd in range(HGH):
                    o = ps[:, c % 2, HC * hd:HC * (hd + 1)]
                    nc.tensor.matmul(o, v5[r, t, P * hd:P * (hd + 1)], at5[r, hd, t, r], start=True, stop=False)
                    mm = nc.tensor.matmul(o, hp_st[c % 2][:, hd, :], proj[:, 8 + hd, c0:c0 + HC],
                                          start=False, stop=True)
                mm.then_inc(sg("hp_o"), 1)

        def pool_hgrn_scan():
            for hd in range(HGH):
                if hd == 0:
                    nc.gpsimd.wait_ge(sg("hg_done"), HGH)
                    nc.gpsimd.wait_ge(sg("hg_kt"), HGH)
                if hd >= 2:
                    nc.gpsimd.wait_ge(sg("hs_out" + str(hd % 2)), 16 * (hd // 2))
                nc.gpsimd.dma_start(hst[hd % 2], shgrn[:, hd]).then_inc(sg("hs_in" + str(hd % 2)), 16)
                if hd:
                    nc.gpsimd.wait_ge(sg("hs_kv"), hd)
                nc.gpsimd.tensor_tensor(hmask[0:HEAD], v5[0:HEAD, 0:1, P * hd:P * (hd + 1)]
                                        .to_broadcast([HEAD, NSEG, P]),
                                        C("seg")[0:HEAD, :].rearrange("p (s o) -> p s o", o=1)
                                        .to_broadcast([HEAD, NSEG, P]), ALU.mult).then_inc(sg("hs_vm"), 1)
                if hd:
                    pool_state_out(hd - 1)
            pool_state_out(HGH - 1)
            nc.gpsimd.wait_ge(sg("hp_s"), SEQ // HC)
            nc.gpsimd.dma_start(hgrn_p, hp_st[0]).then_inc(sg("hp_out"), 16)

        def pool_state_out(hd):
            nc.gpsimd.wait_ge(sg("hs_s"), hd + 1)
            nc.gpsimd.dma_start(hgrn_s[:, hd], hst[hd % 2]).then_inc(sg("hs_out" + str(hd % 2)), 16)

        def dve_hgrn_scan(link):
            for hd in range(HGH):
                nc.vector.wait_ge(sg("hs_kv"), hd + 1)
                for s in range(NS):
                    nc.vector.scalar_tensor_tensor(out=hst[hd % 2][:, s, :], in0=hst[hd % 2][:, s, :],
                                                   scalar=ecl[:, hd, s:s + 1],
                                                   in1=ps[:, 1 + s // 4, P * (s % 4):P * (s % 4 + 1)],
                                                   op0=ALU.mult, op1=ALU.add)
                link(nc.vector.tensor_copy(hp_st[0][:, hd, :], ps[:, 3, 0:P]), "hs_s")
            for c in range(SEQ // HC):
                nc.vector.wait_ge(sg("hp_kv"), c + 1)
                if c:
                    nc.vector.wait_ge(sg("hp_o"), c)
                kv = 2 + 2 * (c % 2)
                for hd in range(HGH):
                    ins = nc.vector.scalar_tensor_tensor(out=hp_st[(c + 1) % 2][:, hd, :], in0=hp_st[c % 2][:, hd, :],
                                                         scalar=ecl[:, hd, NSEG + c:NSEG + c + 1],
                                                         in1=ps[:, kv + hd // 4, P * (hd % 4):P * (hd % 4 + 1)],
                                                         op0=ALU.mult, op1=ALU.add)
                link(ins, "hp_s")

        def act_hgrn_scan():
            for hd in range(HGH):
                nc.scalar.wait_ge(sg("hs_o"), hd + 1)
                nc.scalar.activation(oT5[:, hd, 0:HEAD], ps[:, 0, 0:HEAD], ACT.Copy).then_inc(sg("hs_ob"), 1)
            for c in range(SEQ // HC):
                nc.scalar.wait_ge(sg("hp_o"), c + 1)
                nc.scalar.activation(oT5[:, :, HEAD + HC * c:HEAD + HC * (c + 1)],
                                     ps[:, c % 2, :].rearrange("p (h c) -> p h c", h=HGH), ACT.Copy)\
                    .then_inc(sg("hp_ob"), 1)

        block = ctx.enter_context(nc.Block())

        @block.sync
        def _(sp):
            sp.dma_start(h[:, :, :], x).then_inc(x_in, 16)
            for s in range(SLOTS):
                sp.dma_start(ring[:, s, :], w[s]).then_inc(w_in[s], 16)
            with sp.Fori(0, UNITS // SLOTS - 1) as i:
                for s in range(SLOTS):
                    sp.wait_ge(w_used, SLOTS * i + s + 1)
                    sp.dma_start(ring[:, s, :], w[SLOTS * i + (SLOTS + s)]).then_inc(w_in[s], 16)
            sp.wait_ge(sg("norm_x"), 5)
            sp.dma_start(y, xn[:, :, :]).then_inc(sg("y_out"), 16)
            sp.wait_ge(sg("y_out"), 16)
            sp.wait_ge(sg("hs_out0"), 16 * (HGH // 2))
            sp.wait_ge(sg("hs_out1"), 16 * (HGH // 2))
            sp.wait_ge(sg("hp_out"), 16)

        @block.gpsimd
        def _(pool):
            pool.dma_start(pt_sb[:, :], ptab).then_inc(sg("pt_in"), 16)
            pool.dma_start(hist[:, :, :, 0:CONV_W - 1], stconv).then_inc(sg("hist_in"), 16)
            pool.wait_ge(sg("pt_in"), 16)
            for s in range(NS):
                for g in range(NPG):
                    pg = pool.value_load(pt_sb[0:1, NPG * s + g:NPG * s + g + 1], min_val=0, max_val=NPOOL - 1)
                    c = slice(PAGE * g, PAGE * (g + 1))
                    pool.dma_start(kp[:, s, c], kpages[pg]).then_inc(sg("pages_in"), 16)
                    for b in (0, HD):
                        pool.dma_start(ikp[b:b + HD, s, c], ikpages[pg]).then_inc(sg("pages_in"), 16)
                    pool.dma_start(vp[:, NPG * s + g, :], vpages[pg]).then_inc(sg("pages_in"), 16)
            pool_rope()
            pool_conv()
            pool.wait_ge(sg("roped"), len(ROPED))
            pool.dma_start(C("sin"), keep).then_inc(sg("keep_in"), 16)
            pool.dma_start(krows, proj[:, AK0, :]).then_inc(sg("rows_out"), 16)
            pool.dma_start(ikrows, proj[0:HD, IK0, :]).then_inc(sg("rows_out"), 16)
            pool.dma_start(vrows, tokm[:, :, 0:P]).then_inc(sg("rows_out"), 16)
            pool.dma_start(convo_p, proj[:, 0:12, T - 3:T]).then_inc(sg("conv_out"), 16)
            pool.dma_start(convo_s, hist).then_inc(sg("conv_out"), 16)
            pool_sample_queries()
            pool.wait_ge(sg("conv_out"), 32)
            pool.wait_ge(sg("l2_done"), 8)
            pool.wait_ge(sg("mix_a"), len(DONE))
            pool.dma_start(st, sdelta).then_inc(sg("st_in"), 16)
            pool_inv()
            pool_gdn_scan()
            pool.wait_ge(sg("sc_kv0"), DNH)
            pool.wait_ge(sg("sc_s"), NT)
            pool.dma_start(delta_s, st).then_inc(sg("state_out"), 16)
            pool.dma_start(delta_p, sp_st[:, NT % 2]).then_inc(sg("state_out"), 16)
            pool.wait_ge(bank_free, M_OUT_O + 2)
            pool_hgrn()
            pool_hgrn_scan()

        @block.scalar
        def _(act):
            act.dma_start(cst[:, :], consts).then_inc(const_in, 16)
            act.dma_start(vec[:, :], vecs).then_inc(const_in, 16)
            act.dma_start(wsm, wsmall).then_inc(small_in, 16)
            act.wait_ge(const_in, 32)
            act_norm(0)
            act_copy_out(3, Units.even, proj)
            act_small()
            act_silu()
            act_l2()
            act_scores()
            act_attention()
            nc.scalar.activation(proj[:, Z0:Z0 + 4, :], proj[:, Z0:Z0 + 4, :], ACT.Silu).then_inc(sg("z_gate"), 1)
            act_gdn_prep()
            act_inv()
            act_gdn_scan()
            gate_norm("act", DNH, O_E, z_e, V_DN, out_e, "ge", 6)
            act_norm(1)
            act.wait_ge(sg("rows_out"), 48)
            act.wait_ge(sg("state_out"), 32)
            act_relu(Units.up0)
            act_norm(2)
            act_copy_out(1, Units.odd, proj)
            act_copy_out(2, Units.odd + 8, region(8 * T, 16, T), ACT.Silu)
            act_values5()
            act_hgrn()
            act_hgrn_scan()
            gate_norm("act", HGH, O_O, z_o, V_HGN, out_o, "go", 6)
            act_norm(3)
            act_relu(Units.up1)
            act_norm(4)

        @block.vector
        def _(dve):
            dve.wait_ge(const_in, 32)
            dlink(nc.vector.memset(mx[:, :], 0.0), "bank_free")
            dlink(nc.vector.memset(mx[:, :], 0.0), "bank_free")
            dve_norm(0, xn, dlink)
            dve_small(dlink)
            dve_rope(dlink)
            dve_conv(dlink)
            dve_l2(dlink)
            nc.vector.wait_ge(sg("conv_out"), 32)
            dve_select(dlink)
            dve_attention(dlink)
            dve_gdn_prep(dlink)
            dve_inv(dlink)
            dve_gdn_scan(dlink)
            gate_norm("dve", DNH, O_E, z_e, V_DN, out_e, "ge", 6)
            dve_residual(1, 1, Units.out_e)
            dve_norm(1, xn, dlink)
            dve_square(M_UP0)
            dve_residual(4, 4, Units.down0)
            dve_norm(2, xn, dlink)
            lower_bounds()
            dve.wait_ge(bank_free, M_OUT_O + 2)
            dve_hgrn(dlink)
            dve_hgrn_scan(dlink)
            dve.wait_ge(sg("hs_out0"), 16 * (HGH // 2))
            dve.wait_ge(sg("hs_out1"), 16 * (HGH // 2))
            dve.wait_ge(sg("hp_out"), 16)
            gate_norm("dve", HGH, O_O, z_o, V_HGN, out_o, "go", 6)
            dve_residual(1, 1, Units.out_o)
            dve_norm(3, xn, dlink)
            dve_square(M_UP1)
            dve_residual(4, 4, Units.down1)
            dve_norm(4, xn, dlink)

        @block.tensor
        def _(pe):
            pe.wait_ge(const_in, 32)
            pe_norm(0)
            pe.wait_ge(sg("norm_x"), 1)
            pe_dense(3, Units.even, M_EVEN, xn)
            pe_small()
            pe_rope()
            pe_l2()
            pe_scores()
            pe_expand()
            pe_attention()
            pe_gdn_prep()
            pe_inv()
            pe_gdn_scan()
            gate_norm("pe", DNH, O_E, z_e, V_DN, out_e, "ge", 6)
            pe.wait_ge(sg("ge_out"), DNH)
            pe.wait_ge(sg("mix_a"), len(DONE))
            pe_dense(1, Units.out_e, M_OUT_E, xn)
            pe_norm(1)
            pe.wait_ge(sg("norm_x"), 2)
            pe_dense(4, Units.up0, M_UP0, xn)
            pe.wait_ge(sg("hid_ready"), 32)
            pe_down(Units.down0, M_DOWN0, hid)
            pe_norm(2)
            pe.wait_ge(sg("norm_x"), 3)
            pe_dense(3, Units.odd, M_ODD, xn)
            pe_values5()
            pe.wait_ge(bank_free, M_OUT_O + 2)
            pe_hgrn()
            pe_hgrn_scan()
            gate_norm("pe", HGH, O_O, z_o, V_HGN, out_o, "go", 6)
            pe.wait_ge(sg("go_out"), HGH)
            pe_dense(1, Units.out_o, M_OUT_O, xn)
            pe_norm(3)
            pe.wait_ge(sg("norm_x"), 4)
            pe_dense(4, Units.up1, M_UP1, xn)
            pe.wait_ge(sg("hid_ready"), 64)
            pe_down(Units.down1, M_DOWN1, hid)
            pe_norm(4)


def unit_columns():
    dq = 1092
    cols = [np.arange(dq + P * m, dq + P * (m + 1)) for m in range(12)]
    cols += [np.arange(2636 + P * m, 2636 + P * (m + 1)) for m in range(4)]
    ik = np.arange(1024, 1088)
    cols += [np.concatenate([ik, ik]), np.arange(512, 640)]
    cols += [np.arange(768 + P * m, 768 + P * (m + 1)) for m in range(2)]
    cols += [np.concatenate([np.arange(HD * j, HD * j + HD), np.arange(HD * (j + 4), HD * (j + 5))]) for j in range(4)]
    return np.concatenate(cols)


def units_up(w):
    n = w.shape[1] // P
    return w.reshape(KT, P, n, P).transpose(2, 1, 0, 3).reshape(n, P, KT * P)


def units_down(w):
    return w.reshape(4, KT, P, KT, P).transpose(3, 0, 2, 1, 4).reshape(32, P, KT * P)


def kernel(x_prompt, x_sample, cache_k, cache_v, cache_ik, state_conv, state_delta, state_hgrn, page_table,
           meta, ln_mix, ln_ffn, ln_final, w_in_e, w_out_e, dn_conv, dn_a_log, dn_dt_bias, dn_norm,
           w_in_o, w_out_o, hg_lb, hg_norm, w_up, w_down):
    import concourse.bacc as _bacc
    from concourse.bass_utils import run_bass_kernel_spmd as _run

    A = np.asarray

    def fm(v):
        return A(v).reshape(-1, KT, P).transpose(2, 1, 0)

    def cols(v):
        return A(v).reshape(-1, P).T

    table, at, keep = constant_table()
    wi = A(w_in_e)[0]
    wo = A(w_in_o)[0]
    fq = np.concatenate([wo[:, D:2 * D], wo[:, 0:D], wo[:, 3 * D:4 * D], wo[:, 2 * D:3 * D]], axis=1)
    units = np.concatenate([
        units_up(wi[:, unit_columns()]), units_up(A(w_out_e)[0]), units_up(A(w_up)[0]), units_down(A(w_down)[0]),
        units_up(fq), units_up(A(w_out_o)[0]), units_up(A(w_up)[1]), units_down(A(w_down)[1])])
    small = wi[:, np.concatenate([np.arange(640, 768), np.arange(1088, 1092), np.arange(2628, 2636)])]
    lb = A(hg_lb)
    vecs = np.concatenate([
        cols(A(ln_mix)[0]), cols(A(ln_ffn)[0]), cols(A(ln_mix)[1]), cols(A(ln_ffn)[1]), cols(ln_final),
        A(dn_conv)[0].reshape(CONV_W, 12, P).transpose(2, 1, 0).reshape(P, 48),
        cols(A(dn_norm)[0]), cols(A(hg_norm)[0]),
        np.broadcast_to(A(dn_dt_bias)[0], (P, 4)), np.broadcast_to(A(dn_a_log)[0], (P, 4)),
        cols(lb[0]), cols(lb[1])], axis=1)
    ins = {
        "x": np.concatenate([fm(A(x_sample).reshape(SAMP, D)), fm(meta), fm(A(x_prompt)[0])], axis=2),
        "consts": table, "keep": keep, "w": units,
        "wsmall": small.reshape(KT, P, SMALL).transpose(1, 0, 2),
        "vecs": vecs,
        "stconv": A(state_conv)[0].reshape(NS, 3, 12, P).transpose(3, 2, 0, 1),
        "sdelta": A(state_delta)[0].transpose(2, 1, 0, 3).reshape(P, DNH, NS * P),
        "shgrn": A(state_hgrn)[0].transpose(2, 1, 0, 3),
        "kpages": A(cache_k)[0].reshape(NPOOL, PAGE, P).transpose(0, 2, 1),
        "ikpages": A(cache_ik)[0].transpose(0, 2, 1),
        "vpages": A(cache_v)[0].reshape(NPOOL, PAGE, P),
        "ptab": A(page_table).reshape(1, NS * NPG),
    }
    outs = {
        "y": (P, KT, T), "krows": (P, T), "vrows": (P, NT, P), "ikrows": (HD, T), "convo_p": (P, 12, 3),
        "convo_s": (P, 12, NS, 11), "delta_p": (P, DNH, P), "delta_s": (P, DNH, NS * P),
        "hgrn_p": (P, HGH, P), "hgrn_s": (P, HGH, NS, P),
    }
    nc = _bacc.Bacc("TRN2", target_bir_lowering=False, num_devices=1)
    arrays, args = {}, {}
    for name, a in ins.items():
        a = np.ascontiguousarray(a)
        arrays["in_" + name] = a
        args[name] = nc.dram_tensor("in_" + name, a.shape, mybir.dt.from_np(a.dtype), kind="ExternalInput").ap()
    for name, shape in outs.items():
        args[name] = nc.dram_tensor("out_" + name, shape, F32, kind="ExternalOutput").ap()
    hybrid_step(nc, at=at, **args)
    r = _run(nc, [arrays], core_ids=[0]).results[0]
    o = {name: A(r["out_" + name]).reshape(shape) for name, shape in outs.items()}

    y = o["y"].transpose(2, 1, 0).reshape(T, D)
    kr, ikr = o["krows"].T, o["ikrows"].T
    vr = np.concatenate([o["vrows"][0:HEAD, 0]] + [o["vrows"][:, t] for t in range(1, NT)])
    cs = o["convo_s"][:, :, :, 8:11].transpose(2, 3, 1, 0).reshape(1, NS, 3, 12 * P)
    return (
        y[None, HEAD:], y[:SAMP].reshape(NS, QS, D),
        kr[SAMP:].reshape(1, 1, META + SEQ, KVH, HD), vr[SAMP:].reshape(1, 1, META + SEQ, KVH, HD),
        ikr[SAMP:].reshape(1, 1, META + SEQ, HD),
        o["convo_p"].transpose(2, 1, 0).reshape(1, 1, 3, 12 * P),
        o["delta_p"].transpose(1, 0, 2)[None, None],
        o["hgrn_p"].transpose(1, 0, 2)[None, None],
        kr[:SAMP].reshape(1, NS, QS, KVH, HD), vr[:SAMP].reshape(1, NS, QS, KVH, HD),
        ikr[:SAMP].reshape(1, NS, QS, HD), cs,
        o["delta_s"].reshape(P, DNH, NS, P).transpose(2, 1, 0, 3)[None],
        o["hgrn_s"].transpose(2, 1, 0, 3)[None],
    )
```

```python
from contextlib import ExitStack

import numpy as np

import concourse.bass as bass
from concourse import mybir

F32 = mybir.dt.float32
F32R = mybir.dt.float32r
I32 = mybir.dt.int32
ALU = mybir.AluOpType
ACT = mybir.ActivationFunctionType
AX = mybir.AxisListType

P = 128
D = 1024
KT = D // P
NS, QS = 8, 8
SAMP = NS * QS
META = 16
HEAD = SAMP + META
SEQ = 512
T = HEAD + SEQ
HALF = T // 2
NT = 1 + SEQ // P
PAST, PAGE = 256, 128
NPG = PAST // PAGE
NPOOL = 20
GROUP = 8
SLOTS = 4
A_HEADS, KVH, HD = 8, 2, 64
IDX_HEADS = 4
DNH = 4
HGH = 8
CONV_W = 4
NSEG = NS + 1
EPS = 1e-6
NEG = -3.0e38
K_PROMPT = SEQ // 4 - META
K_SAMPLE = (PAST + QS) // 4 - META

U_EVEN, U_OUT_E, U_FFN, U_ODD, U_OUT_O = 24, 8, 64, 32, 8
VUNITS = 8
UNITS = U_EVEN + U_OUT_E + U_FFN + U_ODD + U_OUT_O + U_FFN
Q0, K0, V0, Z0, IK0, AK0, IQ0, AQ0 = 0, 4, 8, 12, 16, 17, 18, 20

SMALL = P + IDX_HEADS + 2 * DNH
O_IW, O_DB, O_DA = P, P + 4, P + 8

ROWS = [HEAD] + [P] * (NT - 1)
COL0 = [0] + [HEAD + P * i for i in range(NT - 1)]
LEVELS = 7
HLEVELS = 6
HC = 64


def constant_table():
    parts = {}
    i = np.arange(P)
    parts["ident"] = np.eye(P)
    parts["ones"] = np.ones((P, P))
    half = HD // 4 // 2
    rot = np.zeros((P, P))
    for b in (0, HD):
        for d in range(half):
            rot[b + d, b + half + d] = -1.0
            rot[b + half + d, b + d] = 1.0
    parts["rotT"] = rot.T
    pos = np.concatenate([PAST + np.tile(np.arange(QS), NS), np.arange(META + SEQ)]).astype(np.float32)
    inv = (np.float32(500000.0) ** (-np.arange(half, dtype=np.float32) / np.float32(half))).astype(np.float32)
    ang = (pos[None, :] * inv[:, None]).astype(np.float32).astype(np.float64)
    cos, sin = np.ones((P, T)), np.zeros((P, T))
    for b in (0, HD):
        for r in (0, half):
            cos[b + r:b + r + half] = np.cos(ang)
            sin[b + r:b + r + half] = np.sin(ang)
    parts["cos"], parts["sin"] = cos, sin
    seg = np.full(P, -1)
    seg[:SAMP] = np.arange(SAMP) // QS
    seg[SAMP:HEAD] = NS
    same = (seg[:, None] == seg[None, :]) & (seg[:, None] >= 0)
    upper = i[:, None] <= i[None, :]
    for n, blk in (("0", same), ("1", np.ones((P, P), bool))):
        parts["cum" + n] = blk & upper
        parts["rest" + n] = blk & ~upper
        parts["decm" + n] = np.where(blk & upper, 0.0, NEG)
    sm = np.zeros((P, NSEG))
    sm[np.arange(HEAD), seg[:HEAD]] = 1
    parts["seg"] = sm
    for l in range(LEVELS):
        b = 1 << l
        parts[f"lev{l}"] = ((i[:, None] // (2 * b) == i[None, :] // (2 * b))
                            & (i[:, None] % (2 * b) < b) & (i[None, :] % (2 * b) >= b))
    parts["causal"] = np.where(i[None, :] <= i[:, None], 0.0, NEG)
    nb = np.full((P, SAMP), NEG)
    s = np.arange(SAMP)
    nb[:SAMP] = np.where((s[:, None] // QS == s[None, :] // QS) & (s[None, :] <= s[:, None]), 0.0, NEG)
    parts["newb"] = nb
    mb = np.full((P, HEAD), NEG)
    mb[:, SAMP:] = np.where(np.arange(META)[None, :] <= (i % META)[:, None], 0.0, NEG)
    parts["metab"] = mb
    ex = np.zeros((P, 2, P))
    for a in range(2):
        for c in range(P):
            ex[(4 * a + c // 32) * QS + c % QS, a, c] = 1
    parts["expand"] = ex.reshape(P, 2 * P)
    keep = np.ones((P, T))
    keep[:, 0:SAMP:QS] = 0
    keep[:, SAMP] = 0
    keep[:, HEAD::HC] = 0
    parts["eps"] = np.full((P, 1), EPS)
    parts["eps128"] = np.full((P, 1), EPS * P)
    parts["one"] = np.ones((P, 1))
    at, cols = {}, 0
    for n, v in parts.items():
        at[n] = (cols, v.shape[1])
        cols += v.shape[1]
    return np.concatenate([v.astype(np.float32) for v in parts.values()], axis=1), at, keep.astype(np.float32)


def hybrid_step(nc, x, consts, keep, at, w, wsmall, vecs, stconv, sdelta, shgrn, kpages, ikpages, vpages, ptab,
                y, krows, vrows, ikrows, convo_p, convo_s, delta_p, delta_s, hgrn_p, hgrn_s):
    ctx = ExitStack()
    with ctx:
        def sb(name, shape, dt=F32):
            return ctx.enter_context(nc.sbuf_tensor(name, shape, dt))

        def sem(name):
            return ctx.enter_context(nc.semaphore(name))

        ps = ctx.enter_context(nc.psum_tensor("ps", [P, 8, 512], F32))
        def overlay(*parts):
            with ExitStack() as inner:
                return [inner.enter_context(nc.sbuf_tensor(*a)) for a in parts]

        NARENA = 31040
        NSPLIT, NX = 2 * 2 * KT * P, KT * T
        x_lo, hid, _, wsp, x_hi = overlay(("x_lo", [P, KT, T], F32R), ("hid", [P, 2, GROUP, T], F32R),
                                          ("gap", [P, NARENA - NX - NSPLIT - 2 * GROUP * T], F32),
                                          ("wsp", [P, 2, 2, KT * P], F32R), ("x_hi", [P, KT, T], F32R))
        xn = sb("xn", [P, KT, T])
        arena = sb("arena", [P, NARENA])
        h = sb("h", [P, KT, T])
        ring = sb("ring", [P, SLOTS, KT * P])
        cst = sb("cst", [P, consts.shape[1]])
        vec = sb("vec", [P, vecs.shape[1]])
        sq = sb("sq", [P, 2, T])
        rn = sb("rn", [P, T])
        NARENA = 31040
        tokm = sb("tokm", [P, NT, SMALL])
        gates = sb("gates", [P, 8, NT * 4])
        pt_sb = sb("pt_sb", [1, NS * NPG], I32)

        def C(name):
            a, n = at[name]
            return cst[:, a:a + n]

        def region(a, *dims):
            n = int(np.prod(dims))
            assert a + n <= NARENA, (a, dims)
            v = arena[:, a:a + n]
            if len(dims) == 1:
                return v
            if len(dims) == 2:
                return v.rearrange("p (a b) -> p a b", a=dims[0])
            return v.rearrange("p (a b c) -> p a b c", a=dims[0], b=dims[1])

        V_LN = 0
        V_CONV = 40
        V_DN, V_HGN = 88, 89
        V_DTB, V_ALOG = 90, 94
        V_LB0, V_LB1 = 98, 106
        negA = sb("negA", [P, 4])
        lbv = sb("lbv", [P, 2, 8])

        proj = region(0, 24, T)
        ct = region(24 * T, 12, T)
        B = 36 * T
        kp = region(B, NS, PAST)
        ikp = region(B + NS * PAST, NS, PAST)
        vp = region(B + 2 * NS * PAST, NS * NPG, P)

        S = {}

        def sg(name):
            if name not in S:
                S[name] = sem(name)
            return S[name]

        const_in, x_in, small_in = sg("const_in"), sg("x_in"), sg("small_in")
        w_in = [sg(f"w_in{s}") for s in range(SLOTS)]
        w_hi, w_lo, w_used = sg("w_hi"), sg("w_lo"), sg("w_used")
        bank_free = sg("bank_free")
        dve_chain, act_chain, pool_chain = sg("dve_chain"), sg("act_chain"), sg("pool_chain")
        counts = {}

        def linker(eng, chain):
            def link(ins, name=None):
                s_ = sg(name) if name else chain
                counts[s_.name] = counts.get(s_.name, 0) + 1
                ins.then_inc(s_, 1)
                eng.wait_ge(s_, counts[s_.name])
            return link

        dlink = linker(nc.vector, dve_chain)
        alink = linker(nc.scalar, act_chain)
        plink = linker(nc.gpsimd, pool_chain)

        def pairs(v):
            return v.rearrange("p (n c) -> p n c", n=2)

        def heads(v, n=4):
            return v.rearrange("p (h c) -> p h c", h=n)

        class Units:
            even = 0
            out_e = U_EVEN
            ffn0 = out_e + U_OUT_E
            odd = ffn0 + U_FFN
            values = odd + 24
            out_o = values + VUNITS
            ffn1 = out_o + U_OUT_O

        M_OUT_O = Units.out_o - VUNITS

        def act_norm(n):
            for k in range(KT):
                if n == 0:
                    nc.scalar.wait_ge(x_in, 16)
                else:
                    m0 = (Units.out_e, Units.odd - 8, M_OUT_O, UNITS - VUNITS - 8)[n - 1]
                    nc.scalar.wait_ge(bank_free, m0 + k + 3)
                if KT * n + k >= 2:
                    nc.scalar.wait_ge(sg("norm_mm"), KT * n + k - 1)
                nc.scalar.activation(sq[:, k % 2, :], h[:, k, :], ACT.Square).then_inc(sg("norm_sq"), 1)
            nc.scalar.wait_ge(sg("norm_mm"), KT * (n + 1))
            if n:
                nc.scalar.wait_ge(sg("x_f"), KT * n)
            act_root(rn[:, :], ps[:, 6:8, 0:HALF], 1.0 / D, C("eps"), "norm_ln", "norm_rt")
            if n < 4:
                for k in range(KT):
                    act_x_hi(xn if n else xn0, k, "x_f", KT * n + k + 1)

        def act_root(dst, sums, scale, bias, logs, roots):
            nc.scalar.activation(pairs(dst), sums, ACT.Ln, scale=scale, bias=bias).then_inc(sg(logs), 1)
            counts[logs] = counts.get(logs, 0) + 1
            nc.scalar.wait_ge(sg(logs), counts[logs])
            nc.scalar.activation(dst, dst, ACT.Exp, scale=-0.5).then_inc(sg(roots), 1)

        def pe_norm(n):
            for k in range(KT):
                nc.tensor.wait_ge(sg("norm_sq"), KT * n + k + 1)
                if n and k == 0:
                    nc.tensor.wait_ge(sg("norm_ln"), n)
                for e in range(2):
                    mm = nc.tensor.matmul(ps[:, 6 + e, 0:HALF], C("ones"), sq[:, k % 2, e * HALF:(e + 1) * HALF],
                                          start=(k == 0), stop=(k == KT - 1))
                mm.then_inc(sg("norm_mm"), 1)

        def dve_norm(n, dst):
            nc.vector.wait_ge(sg("norm_rt"), n + 1)
            for k in range(KT + 1):
                if k < KT:
                    ins = nc.vector.scalar_tensor_tensor(out=dst[:, k, :], in0=h[:, k, :],
                                                         scalar=vec[:, V_LN + 8 * n + k:V_LN + 8 * n + k + 1],
                                                         in1=rn[:, :], op0=ALU.mult, op1=ALU.mult)
                    ins.then_inc(sg("x_f"), 1)
                if k and n < 4:
                    dve_x_lo(dst, k - 1)
            
        def act_x_hi(src, k, ready, n):
            nc.scalar.wait_ge(sg(ready), n)
            nc.scalar.activation(x_hi[:, k, :], src[:, k, :], ACT.Copy).then_inc(sg("x_hi"), 1)

        split_count = [0]

        def dve_x_lo(src, k):
            split_count[0] += 1
            nc.vector.wait_ge(sg("x_hi"), split_count[0])
            nc.vector.tensor_tensor(x_lo[:, k, :], src[:, k, :], x_hi[:, k, :].bitcast(F32), ALU.subtract)\
                .then_inc(sg("x_split"), 1)

        def loaded(base, per, i, j):
            return 16 * (base // SLOTS + per // SLOTS * i + j // SLOTS + 1)

        def act_w_hi(base, per, i, j):
            nc.scalar.wait_ge(w_in[j % SLOTS], loaded(base, per, i, j))
            if not (base == 0 and j < 2 and isinstance(i, int) and i == 0):
                nc.scalar.wait_ge(w_used, base + per * i + j - 1)
            nc.scalar.activation(wsp[:, j % 2, 0, :], ring[:, j % SLOTS, :], ACT.Copy).then_inc(w_hi, 1)

        def dve_w_lo(base, per, i, j):
            nc.vector.wait_ge(w_hi, base + per * i + j + 1)
            nc.vector.tensor_tensor(wsp[:, j % 2, 1, :], ring[:, j % SLOTS, :], wsp[:, j % 2, 0, :].bitcast(F32),
                                    ALU.subtract).then_inc(w_lo, 1)

        def pe_unit(base, per, i, j, x, first=None):
            nc.tensor.wait_ge(w_lo, base + per * i + j + 1)
            m0 = base if base < Units.out_o else base - VUNITS
            nc.tensor.wait_ge(bank_free, m0 + 1 + per * i + j)
            wh, wl = wsp[:, j % 2, 0, :], wsp[:, j % 2, 1, :]
            for k in range(KT):
                if first:
                    first(k)
                for a, b in ((wh, x[0]), (wh, x[1]), (wl, x[0])):
                    for e in range(2):
                        mm = nc.tensor.matmul(ps[:, 2 * (j % 2) + e, 0:HALF], a[:, k * P:(k + 1) * P],
                                              b[:, k, e * HALF:(e + 1) * HALF],
                                              start=(k == 0 and a is wh and b is x[0]),
                                              stop=(k == KT - 1 and a is wl))
            mm.then_inc(w_used, 1)

        X_SPLIT = (x_hi, x_lo)
        HID = (hid[:, 0], hid[:, 1])

        def x_tiles(n):
            return lambda k: nc.tensor.wait_ge(sg("x_split"), KT * n + k + 1)

        def pe_dense(groups, u0, n):
            with nc.tensor.Fori(0, groups) as i:
                for j in range(GROUP):
                    pe_unit(u0, GROUP, i, j, X_SPLIT, x_tiles(n) if j == 0 else None)

        def act_evacuate(base, i, j, dst, func):
            nc.scalar.wait_ge(w_used, base + GROUP * i + j + 1)
            if not isinstance(i, int):
                nc.scalar.wait_ge(const_in, 32)
            nc.scalar.activation(pairs(dst), ps[:, 2 * (j % 2):2 * (j % 2) + 2, 0:HALF], func).then_inc(bank_free, 1)

        def act_dense(groups, u0, dst, func, more=True):
            def step(i, last):
                for j in range(GROUP):
                    if j < GROUP - 2 or not last:
                        act_w_hi(u0, GROUP, i, j + 2)
                    act_evacuate(u0, i, j, dst[:, GROUP * i + j, :], func)
            with nc.scalar.Fori(0, groups if more else groups - 1) as i:
                step(i, False)
            if not more:
                step(groups - 1, True)

        def dve_w_los(groups, u0, more=True):
            def step(i, last):
                for j in range(GROUP):
                    if j < GROUP - 2 or not last:
                        dve_w_lo(u0, GROUP, i, j + 2)
            with nc.vector.Fori(0, groups if more else groups - 1) as i:
                step(i, False)
            if not more:
                step(groups - 1, True)

        def act_out(u0):
            for j in range(GROUP):
                act_w_hi(u0, GROUP, 0, j + 2)

        def dve_residual(base, per, i, j, k):
            nc.vector.wait_ge(w_used, base + per * i + j + 1)
            nc.vector.tensor_tensor(pairs(h[:, k, :]), pairs(h[:, k, :]), ps[:, 2 * (j % 2):2 * (j % 2) + 2, 0:HALF],
                                    ALU.add).then_inc(bank_free, 1)

        def dve_out(u0):
            for j in range(GROUP):
                dve_residual(u0, GROUP, 0, j, j)
                dve_w_lo(u0, GROUP, 0, j + 2)

        STEP, STEPS = 2 * GROUP, U_FFN // (2 * GROUP)

        def pe_ffn(n, u0):
            with nc.tensor.Fori(0, STEPS) as i:
                for j in range(GROUP):
                    pe_unit(u0, STEP, i, j, X_SPLIT, x_tiles(3 * n + 2) if j == 0 else None)
                for j in range(GROUP, STEP):
                    pe_unit(u0, STEP, i, j, HID, (lambda k: nc.tensor.wait_ge(
                        sg("hid_split"), 4 * GROUP * n + GROUP * i + k + 1)) if j == GROUP else None)

        def ffn_steps(eng, step, more):
            with eng.Fori(0, STEPS if more else STEPS - 1) as i:
                step(i, False)
            if not more:
                step(STEPS - 1, True)

        def act_ffn(n, u0, more=True):
            def step(i, last):
                for j in range(STEP):
                    if j < STEP - 2 or not last:
                        act_w_hi(u0, STEP, i, j + 2)
                    if j < GROUP:
                        nc.scalar.wait_ge(sg("hid_sq"), 4 * GROUP * n + GROUP * i + j + 1)
                        nc.scalar.activation(hid[:, 0, j, :], sq[:, j % 2, :], ACT.Copy).then_inc(sg("hid_hi"), 1)
            ffn_steps(nc.scalar, step, more)

        def dve_ffn(n, u0, more=True):
            def step(i, last):
                for j in range(STEP):
                    if j < GROUP:
                        nc.vector.wait_ge(w_used, u0 + STEP * i + j + 1)
                        pr = ps[:, 2 * (j % 2):2 * (j % 2) + 2, 0:HALF]
                        nc.vector.tensor_scalar(pairs(sq[:, j % 2, :]), pr, 0.0, None, ALU.max).then_inc(bank_free, 1)
                        nc.vector.wait_ge(bank_free, u0 - VUNITS * n + STEP * i + j + 3)
                        nc.vector.tensor_tensor(sq[:, j % 2, :], sq[:, j % 2, :], sq[:, j % 2, :], ALU.mult)\
                            .then_inc(sg("hid_sq"), 1)
                    else:
                        dve_residual(u0, STEP, i, j, j - GROUP)
                    if j < STEP - 2 or not last:
                        dve_w_lo(u0, STEP, i, j + 2)
                    if j < GROUP:
                        nc.vector.wait_ge(sg("hid_hi"), 4 * GROUP * n + GROUP * i + j + 1)
                        nc.vector.tensor_tensor(hid[:, 1, j, :], sq[:, j % 2, :], hid[:, 0, j, :].bitcast(F32),
                                                ALU.subtract).then_inc(sg("hid_split"), 1)
            ffn_steps(nc.vector, step, more)

        def pe_small():
            nc.tensor.wait_ge(small_in, 16)
            nc.tensor.wait_ge(sg("x_f"), KT)
            for t in range(NT):
                if t >= 2:
                    nc.tensor.wait_ge(sg("small_ev"), t - 1)
                for k in range(KT):
                    mm = nc.tensor.matmul(ps[0:ROWS[t], 4 + t % 2, 0:SMALL], xn0[:, k, COL0[t]:COL0[t] + ROWS[t]],
                                          wsm[:, k, :], start=(k == 0), stop=(k == KT - 1))
                mm.then_inc(sg("small_mm"), 1)

        xn0 = region(24 * T, KT, T)
        wsm = region(32 * T, KT, SMALL)

        def G(n):
            return gates[:, n, :].rearrange("p (t h) -> p t h", t=NT)

        def bct(v):
            return v.rearrange("p (o h) -> p o h", o=1).to_broadcast([P, NT, 4])

        G_BETA, G_G, G_IW, G_A, G_B, G_C, G_ED = range(7)

        def dve_small(link):
            link(nc.vector.memset(tokm[:, 0, :], 0.0))
            for t in range(NT):
                nc.vector.wait_ge(sg("small_mm"), t + 1)
                link(nc.vector.tensor_copy(tokm[0:ROWS[t], t, :], ps[0:ROWS[t], 4 + t % 2, 0:SMALL]), "small_ev")
            link(nc.vector.tensor_tensor(G(G_A), tokm[:, :, O_DA:O_DA + 4], bct(vec[:, V_DTB:V_DTB + 4]), ALU.add))
            nc.vector.tensor_scalar(G(G_IW), tokm[:, :, O_IW:O_IW + 4], (IDX_HEADS * HD) ** -0.5, None, ALU.mult)
            link(nc.vector.tensor_scalar(G(G_C), G(G_A), 0.0, None, ALU.max), "gate_z")
            nc.vector.wait_ge(sg("gate_act"), 5)
            link(nc.vector.tensor_tensor(G(G_C), G(G_C), G(G_B), ALU.add))
            link(nc.vector.scalar_tensor_tensor(out=G(G_G), in0=G(G_C), scalar=-1.0,
                                                in1=bct(negA[:, :]), op0=ALU.mult, op1=ALU.mult), "gate_g")

        def act_small():
            nc.scalar.wait_ge(sg("gate_z"), 1)
            nc.scalar.activation(negA[:, :], vec[:, V_ALOG:V_ALOG + 4], ACT.Exp).then_inc(sg("gate_act"), 1)
            nc.scalar.activation(G(G_BETA), tokm[:, :, O_DB:O_DB + 4], ACT.Sigmoid).then_inc(sg("gate_act"), 1)
            nc.scalar.activation(G(G_B), G(G_A), ACT.Abs).then_inc(sg("gate_act"), 1)
            nc.scalar.wait_ge(sg("gate_act"), 3)
            nc.scalar.activation(G(G_B), G(G_B), ACT.Exp, scale=-1.0).then_inc(sg("gate_act"), 1)
            nc.scalar.wait_ge(sg("gate_act"), 4)
            nc.scalar.activation(G(G_B), G(G_B), ACT.Ln, bias=C("one")).then_inc(sg("gate_act"), 1)

        ROPED = list(range(IK0, 24))

        def pe_rope():
            nc.tensor.wait_ge(bank_free, Units.out_e + 2)
            for n, m in enumerate(ROPED):
                if n >= 2:
                    nc.tensor.wait_ge(sg("rope_s"), n - 1)
                for e in range(2):
                    mm = nc.tensor.matmul(ps[:, 2 * (n % 2) + e, 0:HALF], C("rotT"),
                                          proj[:, m, e * HALF:(e + 1) * HALF], start=True, stop=True)
                mm.then_inc(sg("rope_mm"), 1)

        def pool_rope():
            for n, m in enumerate(ROPED):
                nc.gpsimd.wait_ge(sg("rope_mm"), n + 1)
                nc.gpsimd.tensor_tensor(proj[:, m, :], proj[:, m, :], C("cos"), ALU.mult).then_inc(sg("rope_c"), 1)

        def dve_rope(link):
            for n, m in enumerate(ROPED):
                nc.vector.wait_ge(sg("rope_mm"), n + 1)
                link(nc.vector.tensor_tensor(pairs(sq[:, n % 2, :]), ps[:, 2 * (n % 2):2 * (n % 2) + 2, 0:HALF],
                                             pairs(C("sin")), ALU.mult), "rope_s")
                nc.vector.wait_ge(sg("rope_c"), n + 1)
                nc.vector.tensor_tensor(proj[:, m, :], proj[:, m, :], sq[:, n % 2, :], ALU.add)\
                    .then_inc(sg("roped"), 1)

        hist = region(B + 3 * NS * PAST + KT * SMALL, 12, NS, CONV_W - 1 + QS)

        def pool_conv():
            nc.gpsimd.wait_ge(sg("hist_in"), 16)
            nc.gpsimd.wait_ge(bank_free, Units.out_e + 2)
            full = hist.rearrange("p m s q -> p m (s q)")
            link = plink
            link(nc.gpsimd.tensor_copy(hist[:, :, :, 3:11],
                                       proj[:, 0:12, 0:SAMP].rearrange("p m (s q) -> p m s q", s=NS)))
            tmp = region(B + 3 * NS * PAST + KT * SMALL + 12 * 88, 12, SAMP)
            t4 = tmp.rearrange("p m (s q) -> p m s q", s=NS)
            c4 = ct[:, :, 0:SAMP].rearrange("p m (s q) -> p m s q", s=NS)
            for m in range(12):
                for j in range(CONV_W):
                    o = c4 if j == 0 else t4
                    wv = vec[:, V_CONV + 4 * m + j:V_CONV + 4 * m + j + 1]
                    ins = nc.gpsimd.tensor_scalar(o[:, m], hist[:, m, :, j:j + QS], wv, None, ALU.mult)
                    link(ins)
                    if j:
                        link(nc.gpsimd.tensor_tensor(c4[:, m], c4[:, m], t4[:, m], ALU.add),
                             "conv_s" if j == CONV_W - 1 else None)

        def dve_conv(link):
            nc.vector.wait_ge(bank_free, Units.out_e + 2)
            for m in range(12):
                def tap(j):
                    return vec[:, V_CONV + 4 * m + j:V_CONV + 4 * m + j + 1]
                link(nc.vector.tensor_scalar(ct[:, m, SAMP:T], proj[:, m, SAMP:T], tap(3), None, ALU.mult))
                for j in (2, 1, 0):
                    d = 3 - j
                    link(nc.vector.scalar_tensor_tensor(out=ct[:, m, SAMP + d:T], in0=proj[:, m, SAMP:T - d],
                                                        scalar=tap(j), in1=ct[:, m, SAMP + d:T],
                                                        op0=ALU.mult, op1=ALU.add), "conv_p" if j == 0 else None)

        def act_silu():
            for m in range(12):
                nc.scalar.wait_ge(sg("conv_p"), m + 1)
                nc.scalar.wait_ge(sg("conv_s"), m + 1)
                nc.scalar.activation(ct[:, m, :], ct[:, m, :], ACT.Silu).then_inc(sg("silu"), 1)

        def act_l2():
            for n in range(8):
                nc.scalar.wait_ge(sg("silu"), n + 1)
                if n == 0:
                    nc.scalar.wait_ge(sg("roped"), len(ROPED))
                if n >= 2:
                    nc.scalar.wait_ge(sg("l2_mm"), n - 1)
                nc.scalar.activation(sq[:, n % 2, :], ct[:, n, :], ACT.Square).then_inc(sg("l2_sq"), 1)
                if n >= 1:
                    act_l2_root(n - 1)
            act_l2_root(7)

        l2r = [rn[:, :], region(B + 3 * NS * PAST + KT * SMALL + 12 * 88 + 12 * SAMP, T)]

        def act_l2_root(n):
            nc.scalar.wait_ge(sg("l2_mm"), n + 1)
            if n >= 2:
                nc.scalar.wait_ge(sg("l2_done"), n - 1)
            sc, b = (float(P), C("eps128")) if n < 4 else (1.0, C("eps"))
            act_root(l2r[n % 2], ps[:, 2 * (n % 2):2 * (n % 2) + 2, 0:HALF], sc, b, "l2_ln", "l2_rt")

        def pe_l2():
            for n in range(8):
                nc.tensor.wait_ge(sg("l2_sq"), n + 1)
                if n == 0:
                    nc.tensor.wait_ge(sg("rope_s"), len(ROPED))
                if n >= 2:
                    nc.tensor.wait_ge(sg("l2_rt"), n - 1)
                for e in range(2):
                    mm = nc.tensor.matmul(ps[:, 2 * (n % 2) + e, 0:HALF], C("ones"),
                                          sq[:, n % 2, e * HALF:(e + 1) * HALF], start=True, stop=True)
                mm.then_inc(sg("l2_mm"), 1)

        def dve_l2(link):
            for n in range(8):
                nc.vector.wait_ge(sg("l2_rt"), n + 1)
                nc.vector.tensor_tensor(ct[:, n, :], ct[:, n, :], l2r[n % 2], ALU.mult).then_inc(sg("l2_done"), 1)

        GD = B
        xflat = xn.rearrange("p k t -> p (k t)")

        def in_xn(a):
            return xflat[:, a:a + 512].rearrange("p (h c) -> p h c", h=4)

        Tt = [region(GD + 512 * t, 4, P) for t in range(NT)]
        kd = [region(GD + 2560 + 512 * t, 4, P) for t in range(NT)]
        at_s = [region(GD + 5120, 4, P)] + [in_xn(4 * T + 512 * e) for e in range(4)]
        st = region(16 * T, 4, NS * P)
        X = [region(512 * t, 4, P) for t in range(NT)]
        Ti = [region(2560 + 512 * t, 4, P) for t in range(NT)]
        dec = [region(5120 + 512 * e, 4, P) for e in range(2)]
        XL = [region(6144, 4, P), rn[:, 0:512].rearrange("p (h c) -> p h c", h=4)]
        P1 = [sq[:, e, 0:512].rearrange("p (h c) -> p h c", h=4) for e in range(2)]
        ebc = sq[:, 1, 0:512].rearrange("p (h c) -> p h c", h=4)
        gcol = sb("gcol", [P, NT, 8])
        egl = sb("egl", [P, NT, 4, NSEG])

        def kT(hd, t):
            return ct[:, 4 + hd, COL0[t]:COL0[t] + ROWS[t]]

        def qT(hd, t):
            return ct[:, hd, COL0[t]:COL0[t] + ROWS[t]]

        def bank(b, R=P, C_=P):
            return ps[0:R, b, :].rearrange("p (h c) -> p h c", h=4)[:, :, 0:C_]

        def nseg(t):
            return NSEG if t == 0 else 1

        def pe_gdn_prep():
            nc.tensor.wait_ge(sg("gate_g"), 1)
            nc.tensor.wait_ge(sg("l2_done"), 8)
            nc.tensor.wait_ge(sg("mix_a"), len(DONE))
            for t in range(NT):
                R, v = ROWS[t], "0" if t == 0 else "1"
                g = G(G_G)[0:R, t, :]
                if t:
                    nc.tensor.wait_ge(sg("gd_col"), t)
                    nc.tensor.wait_ge(sg("gd_egl"), t)
                nc.tensor.matmul(ps[0:R, 4, 0:4], C("cum" + v)[0:R, 0:R], g, start=True, stop=True)
                nc.tensor.matmul(ps[0:R, 4, 4:8], C("rest" + v)[0:R, 0:R], g, start=True, stop=True)
                ends = C("seg")[0:R, :] if t == 0 else C("one")[0:R, :]
                for hd in range(DNH):
                    mm = nc.tensor.matmul(ps[:, 4, 16 + NSEG * hd:16 + NSEG * hd + nseg(t)],
                                          g[:, hd:hd + 1].to_broadcast([R, P]), ends, start=True, stop=True)
                mm.then_inc(sg("gd_a"), 1)
                if t:
                    nc.tensor.wait_ge(sg("gd_dec"), t)
                    nc.tensor.wait_ge(sg("gd_ebc"), t)
                for hd in range(DNH):
                    mm = nc.tensor.matmul(bank(5, P, R)[:, hd], g[:, hd:hd + 1].to_broadcast([R, P]),
                                          C("cum" + v)[0:R, 0:R], start=True, stop=True)
                mm.then_inc(sg("gd_b"), 1)
                if t:
                    nc.tensor.wait_ge(sg("gd_attn"), t)
                    nc.tensor.wait_ge(sg("gd_x"), t)
                    nc.tensor.wait_ge(sg("gd_kd"), t)
                for hd in range(DNH):
                    nc.tensor.matmul(bank(6, R, R)[:, hd], kT(hd, t), qT(hd, t), start=True, stop=True)
                    nc.tensor.matmul(bank(7, R, R)[:, hd], kT(hd, t), kT(hd, t), start=True, stop=True)
                    mm = nc.tensor.transpose(bank(0, R)[:, hd], kT(hd, t), C("ident"))
                mm.then_inc(sg("gd_c"), 1)

        def dve_gdn_prep(link):
            for t in range(NT):
                R, v, e = ROWS[t], "0" if t == 0 else "1", t % 2
                nc.vector.wait_ge(sg("gd_a"), t + 1)
                link(nc.vector.tensor_copy(gcol[0:R, t, :], ps[0:R, 4, 0:8]), "gd_col")
                nc.vector.wait_ge(sg("gd_b"), t + 1)
                for hd in range(DNH):
                    ins = nc.vector.scalar_tensor_tensor(out=dec[e][0:R, hd, 0:R], in0=bank(5, R, R)[:, hd],
                                                         scalar=gcol[0:R, t, hd:hd + 1],
                                                         in1=C("decm" + v)[0:R, 0:R], op0=ALU.subtract, op1=ALU.add)
                link(ins, "gd_dec")
                nc.vector.wait_ge(sg("gd_c"), t + 1)
                nc.vector.wait_ge(sg("gd_ex"), t + 1)
                link(nc.vector.tensor_tensor(at_s[t][0:R, :, 0:R], bank(6, R, R), dec[e][0:R, :, 0:R], ALU.mult),
                     "gd_attn")
                for hd in range(DNH):
                    ins = nc.vector.scalar_tensor_tensor(out=X[t][0:R, hd, 0:R], in0=bank(7, R, R)[:, hd],
                                                         scalar=G(G_BETA)[0:R, t, hd:hd + 1],
                                                         in1=dec[e][0:R, hd, 0:R], op0=ALU.mult, op1=ALU.mult)
                link(ins, "gd_x")
                nc.vector.wait_ge(sg("gd_ebc"), t + 1)
                q_, k_ = ct[:, 0:4, COL0[t]:COL0[t] + R], ct[:, 4:8, COL0[t]:COL0[t] + R]
                nc.vector.tensor_tensor(q_, q_, ebc[:, :, 0:R], ALU.mult)
                link(nc.vector.scalar_tensor_tensor(out=k_, in0=k_, scalar=-1.0, in1=ebc[:, :, 0:R],
                                                    op0=ALU.mult, op1=ALU.mult), "gd_qk")

        def act_gdn_prep():
            for t in range(NT):
                R, e = ROWS[t], t % 2
                nc.scalar.wait_ge(sg("gd_col"), t + 1)
                alink(nc.scalar.activation(G(G_ED)[0:R, t, :], gcol[0:R, t, 4:8], ACT.Exp))
                nc.scalar.activation(egl[:, t, :, 0:nseg(t)],
                                     ps[:, 4, 16:16 + 4 * NSEG].rearrange("p (h s) -> p h s", h=4)[:, :, 0:nseg(t)],
                                     ACT.Exp).then_inc(sg("gd_egl"), 1)
                nc.scalar.wait_ge(sg("gd_dec"), t + 1)
                nc.scalar.activation(dec[e][0:R, :, 0:R], dec[e][0:R, :, 0:R], ACT.Exp).then_inc(sg("gd_ex"), 1)
                if t:
                    nc.scalar.wait_ge(sg("gd_qk"), t)
                nc.scalar.activation(ebc[:, :, 0:R], bank(5, P, R), ACT.Exp).then_inc(sg("gd_ebc"), 1)
                nc.scalar.wait_ge(sg("gd_c"), t + 1)
                for hd in range(DNH):
                    ins = nc.scalar.activation(kd[t][0:R, hd, :], bank(0, R)[:, hd], ACT.Copy,
                                               scale=G(G_ED)[0:R, t, hd:hd + 1])
                ins.then_inc(sg("gd_kd"), 1)

        INV = [(l, t) for l in range(LEVELS) for t in range(NT) if t or l < 4]
        LAST = {t: (3 if t == 0 else LEVELS - 1) for t in range(NT)}

        def pool_inv():
            for n, (l, t) in enumerate(INV):
                R = ROWS[t]
                if l == 0:
                    nc.gpsimd.wait_ge(sg("gd_x"), t + 1)
                if n >= 2 and INV[n - 2][0] == 0:
                    nc.gpsimd.wait_ge(sg("inv_used"), n - 1)
                elif n >= 2:
                    nc.gpsimd.wait_ge(sg("inv_1"), n - 1 - NT)
                m = C(f"lev{l}")[0:R, 0:R].rearrange("p (o c) -> p o c", o=1).to_broadcast([R, 4, R])
                nc.gpsimd.tensor_tensor(XL[n % 2][0:R, :, 0:R], X[t][0:R, :, 0:R], m, ALU.mult)\
                    .then_inc(sg("inv_xl"), 1)

        def pe_inv():
            nc.tensor.wait_ge(sg("l2_rt"), 8)
            nc.tensor.wait_ge(sg("gd_kd"), NT)
            for n in range(len(INV) + 1):
                if n < len(INV):
                    l, t = INV[n]
                    R = ROWS[t]
                    nc.tensor.wait_ge(sg("inv_xl"), n + 1)
                    if l:
                        nc.tensor.wait_ge(sg("inv_used"), INV.index((l - 1, t)) + 1)
                        if n >= 2 + NT:
                            nc.tensor.wait_ge(sg("inv_p1"), n - 1 - NT)
                        for hd in range(DNH):
                            mm = nc.tensor.matmul(bank(n % 2, R, R)[:, hd], XL[n % 2][0:R, hd, 0:R],
                                                  Ti[t][0:R, hd, 0:R], start=True, stop=True)
                        mm.then_inc(sg("inv_1"), 1)
                    else:
                        if n >= 2:
                            nc.tensor.wait_ge(sg("inv_used"), n - 1)
                        for hd in range(DNH):
                            mm = nc.tensor.transpose(bank(2 + 2 * (n % 2), R, R)[:, hd], XL[n % 2][0:R, hd, 0:R],
                                                     C("ident")[0:R, 0:R])
                        mm.then_inc(sg("inv_2"), 1)
                m = n - 1
                if m < NT:
                    continue
                l, t = INV[m]
                R = ROWS[t]
                nc.tensor.wait_ge(sg("inv_p1"), m + 1 - NT)
                nc.tensor.wait_ge(sg("inv_used"), m - 1)
                for hd in range(DNH):
                    if l < LAST[t]:
                        nc.tensor.matmul(bank(2 + 2 * (m % 2), R, R)[:, hd], Tt[t][0:R, hd, 0:R],
                                         P1[m % 2][0:R, hd, 0:R], start=True, stop=True)
                    mm = nc.tensor.matmul(bank(3 + 2 * (m % 2), R, R)[:, hd], P1[m % 2][0:R, hd, 0:R],
                                          Tt[t][0:R, hd, 0:R], start=True, stop=True)
                mm.then_inc(sg("inv_2"), 1)

        def act_inv():
            nc.scalar.wait_ge(sg("gd_qk"), NT)
            for n, (l, t) in enumerate(INV):
                R = ROWS[t]
                if l:
                    nc.scalar.wait_ge(sg("inv_1"), n + 1 - NT)
                    if n >= 2 + NT:
                        nc.scalar.wait_ge(sg("inv_2"), n - 1)
                    nc.scalar.activation(P1[n % 2][0:R, :, 0:R], bank(n % 2, R, R), ACT.Copy)\
                        .then_inc(sg("inv_p1"), 1)

        def dve_inv(link):
            for n, (l, t) in enumerate(INV):
                R = ROWS[t]
                nc.vector.wait_ge(sg("inv_2"), n + 1)
                if l == 0:
                    i4 = C("ident")[0:R, 0:R].rearrange("p (o c) -> p o c", o=1).to_broadcast([R, 4, R])
                    nc.vector.wait_ge(sg("inv_xl"), n + 1)
                    nc.vector.tensor_tensor(Ti[t][0:R, :, 0:R], i4, bank(2 + 2 * (n % 2), R, R), ALU.subtract)
                    link(nc.vector.tensor_tensor(Tt[t][0:R, :, 0:R], i4, XL[n % 2][0:R, :, 0:R], ALU.subtract),
                         "inv_used")
                    continue
                if l < LAST[t]:
                    nc.vector.tensor_tensor(Ti[t][0:R, :, 0:R], Ti[t][0:R, :, 0:R], bank(2 + 2 * (n % 2), R, R),
                                            ALU.subtract)
                link(nc.vector.tensor_tensor(Tt[t][0:R, :, 0:R], Tt[t][0:R, :, 0:R],
                                             bank(3 + 2 * (n % 2), R, R), ALU.subtract),
                     "inv_used")

        RB = 512 * 10
        rbuf = region(RB, 4, P)
        vnew = region(RB + 512, 4, P)
        rT = region(RB + 1024, 4, P)
        sp_st = sb("sp_st", [P, 2, 4, P])
        vmask = region(0, NSEG, P)
        oT = region(2560, 4, T)

        def pe_gdn_scan():
            nc.tensor.wait_ge(sg("inv_used"), len(INV))
            nc.tensor.wait_ge(sg("gd_qk"), NT)
            nc.tensor.wait_ge(sg("st_in"), 16)
            for hd in range(DNH):
                for s in range(NS):
                    mm = nc.tensor.matmul(bank(0, P, HEAD)[:, hd, QS * s:QS * (s + 1)],
                                          st[:, hd, P * s:P * (s + 1)], kT(hd, 0)[:, QS * s:QS * (s + 1)],
                                          start=True, stop=True)
            mm.then_inc(sg("sc_ks"), 1)
            nc.tensor.wait_ge(sg("sc_rt"), 1)
            for hd in range(DNH):
                mm = nc.tensor.transpose(bank(1, HEAD)[:, hd], rT[:, hd, 0:HEAD], C("ident"))
            mm.then_inc(sg("sc_r"), 1)
            for t in range(NT):
                R = ROWS[t]
                if t:
                    nc.tensor.wait_ge(sg("sc_s"), t)
                    for hd in range(DNH):
                        nc.tensor.matmul(bank(1, R)[:, hd], ct[:, 8 + hd, COL0[t]:COL0[t] + R], C("ident"),
                                         start=True, stop=False)
                        mm = nc.tensor.matmul(bank(1, R)[:, hd], kT(hd, t), sp_st[:, t % 2, hd, :],
                                              start=False, stop=True)
                    mm.then_inc(sg("sc_r"), 1)
                nc.tensor.wait_ge(sg("sc_rb"), t + 1)
                for hd in range(DNH):
                    mm = nc.tensor.matmul(bank(2, R)[:, hd], Tt[t][0:R, hd, 0:R], rbuf[0:R, hd, :],
                                          start=True, stop=True)
                mm.then_inc(sg("sc_v"), 1)
                nc.tensor.wait_ge(sg("sc_vn"), t + 1)
                if t:
                    for hd in range(DNH):
                        mm = nc.tensor.matmul(bank(4)[:, hd], kd[t][0:R, hd, :], vnew[0:R, hd, :],
                                              start=True, stop=True)
                    mm.then_inc(sg("sc_kv"), 1)
                    nc.tensor.wait_ge(sg("sc_ob"), t)
                for hd in range(DNH):
                    o = bank(3, P, R)[:, hd]
                    if t:
                        nc.tensor.matmul(o, sp_st[:, t % 2, hd, :], qT(hd, t), start=True, stop=False)
                    else:
                        for s in range(NS):
                            nc.tensor.matmul(o[:, QS * s:QS * (s + 1)], st[:, hd, P * s:P * (s + 1)],
                                             qT(hd, 0)[:, QS * s:QS * (s + 1)], start=(s == 0), stop=False,
                                             skip_group_check=True)
                    mm = nc.tensor.matmul(o, vnew[0:R, hd, :], at_s[t][0:R, hd, 0:R], start=False, stop=True,
                                          skip_group_check=(t == 0))
                mm.then_inc(sg("sc_o"), 1)
                if t == 0:
                    for hd in range(DNH):
                        nc.tensor.wait_ge(sg("sc_vm"), hd + 1)
                        if hd:
                            nc.tensor.wait_ge(sg("sc_kv0"), hd)
                        for b, (a, n) in enumerate(((0, 4), (4, 4), (8, 1))):
                            mm = nc.tensor.matmul(ps[:, 4 + b, 0:n * P], kd[0][0:R, hd, :],
                                                  vmask[0:R, a:a + n, :].rearrange("p s c -> p (s c)"),
                                                  start=True, stop=True)
                        mm.then_inc(sg("sc_kvm"), 1)

        def pool_gdn_scan():
            nc.gpsimd.wait_ge(sg("sc_vn"), 1)
            for hd in range(DNH):
                if hd:
                    nc.gpsimd.wait_ge(sg("sc_kvm"), hd)
                nc.gpsimd.tensor_tensor(vmask[0:HEAD], vnew[0:HEAD, hd:hd + 1, :].to_broadcast([HEAD, NSEG, P]),
                                        C("seg")[0:HEAD, :].rearrange("p (s o) -> p s o", o=1)
                                        .to_broadcast([HEAD, NSEG, P]), ALU.mult).then_inc(sg("sc_vm"), 1)

        def act_gdn_scan():
            for t in range(NT):
                R = ROWS[t]
                nc.scalar.wait_ge(sg("sc_r"), t + 1)
                nc.scalar.activation(rbuf[0:R], bank(1, R), ACT.Copy).then_inc(sg("sc_rb"), 1)
                nc.scalar.wait_ge(sg("sc_v"), t + 1)
                if t == 1:
                    nc.scalar.wait_ge(sg("sc_vm"), DNH)
                if t:
                    nc.scalar.wait_ge(sg("sc_o"), t)
                for hd in range(DNH):
                    ins = nc.scalar.activation(vnew[0:R, hd, :], bank(2, R)[:, hd], ACT.Copy,
                                               scale=G(G_BETA)[0:R, t, hd:hd + 1])
                ins.then_inc(sg("sc_vn"), 1)

        def dve_gdn_scan(link):
            nc.vector.wait_ge(sg("sc_ks"), 1)
            nc.vector.tensor_copy(rT[:, :, SAMP:HEAD], ct[:, 8:12, SAMP:HEAD])
            link(nc.vector.tensor_tensor(rT[:, :, 0:SAMP], ct[:, 8:12, 0:SAMP], bank(0, P, SAMP), ALU.add), "sc_rt")
            for t in range(NT):
                R = ROWS[t]
                if t == 0:
                    nc.vector.wait_ge(sg("sc_o"), 1)
                    nc.vector.tensor_copy(oT[:, :, 0:HEAD], bank(3, P, HEAD)).then_inc(sg("sc_ob"), 1)
                    for hd in range(DNH):
                        nc.vector.wait_ge(sg("sc_kvm"), hd + 1)
                        for s in range(NS):
                            nc.vector.scalar_tensor_tensor(out=st[:, hd, P * s:P * (s + 1)],
                                                           in0=st[:, hd, P * s:P * (s + 1)],
                                                           scalar=egl[:, 0, hd, s:s + 1],
                                                           in1=ps[:, 4 + s // 4, P * (s % 4):P * (s % 4 + 1)],
                                                           op0=ALU.mult, op1=ALU.add)
                        link(nc.vector.tensor_copy(sp_st[:, 1, hd, :], ps[:, 6, 0:P]), "sc_kv0")
                    nc.vector.sem_inc(sg("sc_s"), 1)
                    continue
                nc.vector.wait_ge(sg("sc_kv"), t)
                for hd in range(DNH):
                    ins = nc.vector.scalar_tensor_tensor(out=sp_st[:, (t + 1) % 2, hd, :], in0=sp_st[:, t % 2, hd, :],
                                                         scalar=egl[:, t, hd, 0:1], in1=bank(4)[:, hd],
                                                         op0=ALU.mult, op1=ALU.add)
                link(ins, "sc_s")
                nc.vector.wait_ge(sg("sc_o"), t + 1)
                nc.vector.tensor_copy(oT[:, :, COL0[t]:COL0[t] + R], bank(3, P, R)).then_inc(sg("sc_ob"), 1)

        def gate_norm(eng, nh, o, z, nv, tag, base_bank):
            if eng == "act":
                for n in range(nh):
                    if n == 0:
                        nc.scalar.wait_ge(*o["ready"])
                    if n >= 2:
                        nc.scalar.wait_ge(sg(tag + "_mm"), n - 1)
                    nc.scalar.activation(sq[:, n % 2, :], o["v"](n), ACT.Square).then_inc(sg(tag + "_sq"), 1)
                    nc.scalar.wait_ge(sg(tag + "_mm"), n + 1)
                    if n:
                        nc.scalar.wait_ge(sg(tag + "_x"), n)
                    act_root(rn[:, :], ps[:, base_bank:base_bank + 2, 0:HALF], 1.0 / P, C("eps"), tag + "_ln",
                             tag + "_rt")
                    if n:
                        act_x_hi(xn, KT - nh + n - 1, tag + "_out", n)
                act_x_hi(xn, KT - 1, tag + "_out", nh)
                return
            if eng == "pe":
                for n in range(nh):
                    nc.tensor.wait_ge(sg(tag + "_sq"), n + 1)
                    if n:
                        nc.tensor.wait_ge(sg(tag + "_ln"), n)
                    for e in range(2):
                        mm = nc.tensor.matmul(ps[:, base_bank + e, 0:HALF], C("ones"),
                                              sq[:, n % 2, e * HALF:(e + 1) * HALF], start=True, stop=True)
                    mm.then_inc(sg(tag + "_mm"), 1)
                return
            for n in range(nh):
                nc.vector.wait_ge(sg(tag + "_rt"), n + 1)
                dlink(nc.vector.scalar_tensor_tensor(out=o["v"](n), in0=o["v"](n), scalar=vec[:, nv:nv + 1],
                                                     in1=rn[:, :], op0=ALU.mult, op1=ALU.mult), tag + "_x")
                nc.vector.tensor_tensor(xn[:, KT - nh + n, :], o["v"](n), z(n), ALU.mult).then_inc(sg(tag + "_out"), 1)
                if n:
                    dve_x_lo(xn, KT - nh + n - 1)
            dve_x_lo(xn, KT - 1)

        O_E = {"ready": (sg("sc_ob"), NT), "v": lambda n: oT[:, n, :]}

        def z_e(n):
            return proj[:, Z0 + n, :]

        bias = [None] + [region(o, HEAD + P * i) for i, o in ((1, 0), (2, 208), (3, 544), (4, 1008))]
        sbias = region(1600, PAST + HEAD)
        ebias = region(1936, 2, PAST + HEAD)
        sc, wk, gt, eq, cum = [region(2608 + 512 * n, 512) for n in range(5)]
        rel = [region(2608 + 2560 + 512 * n, 512) for n in range(2)]
        qs = region(6192, NS, 4, QS)
        qm = region(6448, 4, META)
        iqpad = region(B + 3 * NS * PAST, 2, NS, SAMP)
        best = sb("best", [P, 8])
        cnt = sb("cnt", [P, 2])
        SEL = [(t, ROWS[t], P * t) for t in range(1, NT)] + [(0, SAMP, PAST + SAMP)]

        def pool_sample_queries():
            nc.gpsimd.wait_ge(sg("roped"), len(ROPED))
            nc.gpsimd.wait_ge(sg("small_mm"), NT)
            nc.gpsimd.wait_ge(sg("silu"), 12)
            nc.gpsimd.wait_ge(sg("conv_out"), 32)
            plink(nc.gpsimd.memset(iqpad, 0.0))
            for s in range(NS):
                c = slice(QS * s, QS * (s + 1))
                ins = nc.gpsimd.tensor_copy(iqpad[:, :, s, c], proj[:, IQ0:IQ0 + 2, c])
            ins.then_inc(sg("sq_ready"), 1)
            nc.gpsimd.tensor_copy(qs.rearrange("p s h q -> p h s q"),
                                  proj[:, AQ0:AQ0 + 4, 0:SAMP].rearrange("p h (s q) -> p h s q", s=NS))\
                .then_inc(sg("sq_ready"), 1)
            nc.gpsimd.tensor_copy(qm, proj[:, AQ0:AQ0 + 4, SAMP:HEAD]).then_inc(sg("sq_ready"), 1)

        def pe_scores():
            nc.tensor.wait_ge(sg("roped"), len(ROPED))
            nc.tensor.wait_ge(sg("l2_rt"), 8)
            n = 0
            for t, R, W in SEL:
                for hd in range(IDX_HEADS):
                    b = HD * (hd % 2)
                    q = proj[b:b + HD, IQ0 + hd // 2, COL0[t]:COL0[t] + R]
                    if n >= 4:
                        nc.tensor.wait_ge(sg("idx_rel"), n - 3)
                    if t:
                        mm = nc.tensor.matmul(ps[:, n % 4, 0:W], q, proj[b:b + HD, IK0, HEAD:HEAD + W],
                                              start=True, stop=True)
                    else:
                        if hd == 0:
                            nc.tensor.wait_ge(sg("pages_in"), 16 * 4 * NS * NPG)
                            nc.tensor.wait_ge(sg("sq_ready"), 3)
                        for s in range(NS):
                            nc.tensor.matmul(ps[0:SAMP, n % 4, 0:PAST], iqpad[b:b + HD, hd // 2, s, :],
                                             ikp[b:b + HD, s, :], start=(s == 0), stop=(s == NS - 1))
                        mm = nc.tensor.matmul(ps[0:SAMP, n % 4, PAST:PAST + SAMP], q, proj[b:b + HD, IK0, 0:SAMP],
                                              start=True, stop=True)
                    mm.then_inc(sg("idx_mm"), 1)
                    n += 1

        def act_scores():
            n = 0
            for t, R, W in SEL:
                for hd in range(IDX_HEADS):
                    nc.scalar.wait_ge(sg("idx_mm"), n + 1)
                    if n >= 2:
                        nc.scalar.wait_ge(sg("idx_acc"), n - 1)
                    if n == 0:
                        nc.scalar.wait_ge(sg("silu"), 12)
                    nc.scalar.activation(rel[n % 2][0:R, 0:W], ps[0:R, n % 4, 0:W], ACT.Relu)\
                        .then_inc(sg("idx_rel"), 1)
                    n += 1

        def dve_select(link):
            n = 0
            nc.vector.wait_ge(sg("silu"), 12)
            for t, R, W in SEL:
                v = slice(0, R)
                for hd in range(IDX_HEADS):
                    nc.vector.wait_ge(sg("idx_rel"), n + 1)
                    wv = G(G_IW)[v, t, hd:hd + 1]
                    if hd == 0:
                        link(nc.vector.tensor_scalar(sc[v, 0:W], rel[n % 2][v, 0:W], wv, None, ALU.mult), "idx_acc")
                    else:
                        link(nc.vector.scalar_tensor_tensor(out=sc[v, 0:W], in0=rel[n % 2][v, 0:W], scalar=wv,
                                                            in1=sc[v, 0:W], op0=ALU.mult, op1=ALU.add), "idx_acc")
                    n += 1
                last = slice(W - P, W) if t else slice(PAST, PAST + SAMP)
                hide = C("causal") if t else C("newb")[v]
                link(nc.vector.tensor_tensor(sc[v, last], sc[v, last], hide, ALU.add))
                a, K = (0, K_PROMPT) if t else (META, K_SAMPLE)
                s_, k_, g_, e_, c_ = (u[v, a:W] for u in (sc, wk, gt, eq, cum))
                link(nc.vector.max(best[v, :], s_))
                for r in range(1, -(-K // 8)):
                    link(nc.vector.match_replace(out=k_, in_to_replace=best[v, :], in_values=s_ if r == 1 else k_,
                                                 imm_value=NEG))
                    link(nc.vector.max(best[v, :], k_))
                thr = best[v, (K - 1) % 8:(K - 1) % 8 + 1]
                link(nc.vector.tensor_scalar(g_, s_, thr, 0.0, ALU.is_gt, ALU.add, accum_out=cnt[v, 0:1]))
                link(nc.vector.tensor_scalar(e_, s_, thr, None, ALU.is_equal))
                link(nc.vector.tensor_scalar(cnt[v, 1:2], cnt[v, 0:1], -1.0, float(K), ALU.mult, ALU.add))
                link(nc.vector.tensor_tensor_scan(c_, C("one")[v].to_broadcast([R, W - a]), e_, 0.0,
                                                  ALU.mult, ALU.add))
                link(nc.vector.scalar_tensor_tensor(out=c_, in0=c_, scalar=cnt[v, 1:2], in1=e_,
                                                    op0=ALU.is_le, op1=ALU.mult))
                link(nc.vector.tensor_tensor(g_, g_, c_, ALU.add))
                if t:
                    out_ = bias[t]
                    nc.vector.memset(out_[:, 0:SAMP], NEG)
                    nc.vector.memset(out_[:, SAMP:HEAD], 0.0)
                    link(nc.vector.tensor_scalar(out_[:, HEAD:HEAD + W], g_, -1.0, -NEG, ALU.add, ALU.mult))
                    d = out_[:, HEAD + W - P:HEAD + W]
                    link(nc.vector.tensor_tensor(d, d, C("causal"), ALU.min), "chosen")
                else:
                    nc.vector.memset(sbias[v, 0:META], 0.0)
                    nc.vector.memset(sbias[v, PAST + SAMP:PAST + HEAD], NEG)
                    link(nc.vector.tensor_scalar(sbias[v, META:W], g_, -1.0, -NEG, ALU.add, ALU.mult))
                    d = sbias[v, PAST:PAST + SAMP]
                    link(nc.vector.tensor_tensor(d, d, C("newb")[v], ALU.min), "chosen")
            nc.vector.wait_ge(sg("ex_mm"), 1)
            for a in range(2):
                ins = nc.vector.tensor_copy(ebias[:, a, :], ps[:, 4 + a, 0:PAST + HEAD])
            link(ins, "chosen")

        def pe_expand():
            nc.tensor.wait_ge(sg("chosen"), NT)
            for a in range(2):
                mm = nc.tensor.matmul(ps[:, 4 + a, 0:PAST + HEAD], C("expand")[0:SAMP, P * a:P * (a + 1)],
                                      sbias[0:SAMP, :], start=True, stop=True)
            mm.then_inc(sg("ex_mm"), 1)

        ITEMS = [("p", t, hd) for t in range(1, NT) for hd in range(A_HEADS)]
        ITEMS += [("s", g, a) for g in range(KVH) for a in range(2)] + [("m", 0, 0)]
        lm = [region(2608 + T * e, T) for e in range(2)]
        pT = [region(2608 + 2 * T + 640 * e, 5, P) for e in range(2)]
        on = region(2608 + 2 * T + 1280, 512)
        mx = sb("mx", [P, 2])
        rsum = sb("rsum", [P, 3, 8])

        def width(it):
            return {"p": HEAD + P * it[1], "s": PAST + HEAD, "m": HEAD}[it[0]]

        def logits(n):
            W, pr = width(ITEMS[n]), 2 * (n % 2)
            return ps[:, pr, 0:W] if W <= 512 else ps[:, pr:pr + 2, 0:W // 2]

        def as_logits(v):
            return v if v.shape[1] <= 512 else pairs(v)

        def key_tiles(it):
            if it[0] == "p":
                return [(ROWS[u], COL0[u]) for u in range(it[1] + 1)]
            if it[0] == "s":
                return [(P, 0), (P, P), (HEAD, PAST)]
            return [(HEAD, 0)]

        def pe_logits(n):
            it = ITEMS[n]
            W = width(it)
            if n >= 2:
                nc.tensor.wait_ge(sg("lg_max"), n - 1)
            if it[0] == "p":
                g, j = it[2] // 4, it[2] % 4
                q = proj[HD * g:HD * (g + 1), AQ0 + j, COL0[it[1]]:COL0[it[1]] + P]
                k = proj[HD * g:HD * (g + 1), AK0, :]
                if W <= 512:
                    mm = nc.tensor.matmul(ps[:, 2 * (n % 2), 0:W], q, k[:, 0:W], start=True, stop=True)
                else:
                    for e in range(2):
                        mm = nc.tensor.matmul(ps[:, 2 * (n % 2) + e, 0:W // 2], q, k[:, e * W // 2:(e + 1) * W // 2],
                                              start=True, stop=True)
            elif it[0] == "s":
                g, a = it[1:]
                b = slice(HD * g, HD * (g + 1))
                qa = qs[b, 4 * a:4 * a + 4].rearrange("p s h q -> p (s h q)")
                for s in range(4):
                    nc.tensor.matmul(ps[32 * s:32 * (s + 1), 2 * (n % 2), 0:PAST], qa[:, 32 * s:32 * (s + 1)],
                                     kp[b, 4 * a + s, :], start=True, stop=True)
                mm = nc.tensor.matmul(ps[:, 2 * (n % 2), PAST:PAST + HEAD], qa, proj[b, AK0, 0:HEAD],
                                      start=True, stop=True)
            else:
                for g in range(KVH):
                    b = slice(HD * g, HD * (g + 1))
                    mm = nc.tensor.matmul(ps[b, 2 * (n % 2), 0:HEAD], qm[b].rearrange("p h q -> p (h q)"),
                                          proj[b, AK0, 0:HEAD], start=True, stop=True)
            mm.then_inc(sg("lg_mm"), 1)

        def turned(it, u):
            if it[0] == "p":
                return (5, P * (u // 4)) if u % 4 == 0 else (4, P * (u - 1))
            return (5, 0) if it[0] == "m" or u == 2 else (4, P * u)

        def pe_turn(n):
            it = ITEMS[n]
            nc.tensor.wait_ge(sg("pr_exp"), n + 1)
            if n:
                nc.tensor.wait_ge(sg("pr_ev_a"), n)
                nc.tensor.wait_ge(sg("pr_ev_d"), n)
            for u, (K, c) in enumerate(key_tiles(it)):
                tb, tc = turned(it, u)
                mm = nc.tensor.transpose(ps[0:K, tb, tc:tc + P], lm[n % 2][:, c:c + K], C("ident"))
            mm.then_inc(sg("pr_tr"), 1)

        def pe_values(n):
            it = ITEMS[n]
            tiles = key_tiles(it)
            nc.tensor.wait_ge(sg("pr_ev_a"), n + 1)
            nc.tensor.wait_ge(sg("pr_ev_d"), n + 1)
            if it[0] == "p":
                hd = it[2]
                if hd == 0 and it[1] > 1:
                    nc.tensor.wait_ge(sg("o_ev"), it[1] - 1)
                for u, (K, c) in enumerate(tiles):
                    mm = nc.tensor.matmul(ps[:, 6, HD * hd:HD * (hd + 1)], pT[n % 2][0:K, u, :],
                                          tokm[0:K, u, HD * (hd // 4):HD * (hd // 4 + 1)],
                                          start=(u == 0), stop=(u == len(tiles) - 1))
            else:
                nc.tensor.wait_ge(sg("o_ev"), NT - 1 + ITEMS_S.index(n))
                if it[0] == "s":
                    g, a = it[1:]
                    for s in range(4):
                        for u, (K, c) in enumerate(tiles):
                            vv = vp[:, NPG * (4 * a + s) + u, HD * g:HD * (g + 1)] if u < NPG else \
                                tokm[0:K, 0, HD * g:HD * (g + 1)]
                            mm = nc.tensor.matmul(ps[32 * s:32 * (s + 1), 6, 0:HD],
                                                  pT[n % 2][0:K, u, 32 * s:32 * (s + 1)], vv,
                                                  start=(u == 0), stop=(u == len(tiles) - 1))
                else:
                    for g in range(KVH):
                        mm = nc.tensor.matmul(ps[HD * g:HD * (g + 1), 6, 0:HD],
                                              pT[n % 2][0:HEAD, 0, HD * g:HD * (g + 1)],
                                              tokm[0:HEAD, 0, HD * g:HD * (g + 1)], start=True, stop=True)
            mm.then_inc(sg("o_mm"), 1)

        ITEMS_S = [n for n, it in enumerate(ITEMS) if it[0] != "p"]
        DONE = [n for n, it in enumerate(ITEMS) if it[0] != "p" or it[2] == A_HEADS - 1]

        def pe_o_turn(n):
            d = DONE.index(n)
            nc.tensor.wait_ge(sg("o_ev"), d + 1)
            if d:
                nc.tensor.wait_ge(sg("mix_a"), d)
            if ITEMS[n][0] == "p":
                for u in range(4):
                    mm = nc.tensor.transpose(ps[:, 7, P * u:P * (u + 1)], on[:, P * u:P * (u + 1)], C("ident"))
            else:
                mm = nc.tensor.transpose(ps[0:HD, 7, 0:P], on[:, 0:HD], C("ident"))
            mm.then_inc(sg("o_tr"), 1)

        def pe_attention():
            nc.tensor.wait_ge(sg("sq_ready"), 3)
            nc.tensor.wait_ge(sg("pages_in"), 16 * 4 * NS * NPG)
            nc.tensor.wait_ge(sg("idx_rel"), IDX_HEADS * NT)
            nc.tensor.wait_ge(sg("chosen"), NT + 1)
            pe_logits(0)
            for n in range(len(ITEMS) + 2):
                if n + 1 < len(ITEMS):
                    pe_logits(n + 1)
                if n < len(ITEMS):
                    pe_turn(n)
                if 1 <= n <= len(ITEMS):
                    pe_values(n - 1)
                if n - 2 in DONE:
                    pe_o_turn(n - 2)

        def dve_attention(link):
            for n in range(len(ITEMS) + 2):
                if n < len(ITEMS):
                    it = ITEMS[n]
                    W = width(it)
                    b = bias[it[1]] if it[0] == "p" else ebias[:, it[2], :] if it[0] == "s" else C("metab")
                    nc.vector.wait_ge(sg("lg_mm"), n + 1)
                    if n >= 2:
                        nc.vector.wait_ge(sg("pr_tr"), n - 1)
                    link(nc.vector.tensor_tensor_reduce(
                        out=as_logits(lm[n % 2][:, 0:W]), in0=logits(n), in1=as_logits(b[:, 0:W]), scale=1.0,
                        scalar=NEG, op0=ALU.add, op1=ALU.max, accum_out=mx[:, n % 2:n % 2 + 1]))
                    link(nc.vector.tensor_scalar(mx[:, n % 2:n % 2 + 1], mx[:, n % 2:n % 2 + 1], -HD ** -0.5, None,
                                                 ALU.mult), "lg_max")
                if 1 <= n <= len(ITEMS):
                    m = n - 1
                    it = ITEMS[m]
                    nc.vector.wait_ge(sg("pr_tr"), m + 1)
                    if m >= 2:
                        nc.vector.wait_ge(sg("o_mm"), m - 1)
                    u = 2 if it[0] == "s" else 0
                    ins = nc.vector.tensor_copy(pT[m % 2][0:HEAD, u, :], ps[0:HEAD, 5, 0:P])
                    if it[0] == "p" and it[1] == 4:
                        ins = nc.vector.tensor_copy(pT[m % 2][:, 4, :], ps[:, 5, P:2 * P])
                    ins.then_inc(sg("pr_ev_d"), 1)
                if n - 2 in DONE:
                    m = n - 2
                    it, d = ITEMS[m], DONE.index(m)
                    nc.vector.wait_ge(sg("o_mm"), m + 1)
                    if d:
                        nc.vector.wait_ge(sg("o_tr"), d)
                    if it[0] == "p":
                        rs = rsum[:, it[1] % 2, :]
                        link(nc.vector.reciprocal(rs, rs))
                        link(nc.vector.tensor_tensor(on.rearrange("p (h c) -> p h c", h=8),
                                                     ps[:, 6, :].rearrange("p (h c) -> p h c", h=8),
                                                     rs.rearrange("p (h o) -> p h o", o=1)
                                                     .to_broadcast([P, 8, HD]), ALU.mult), "o_ev")
                    else:
                        rs = rsum[:, 2, m - len(ITEMS) + 5:m - len(ITEMS) + 6]
                        link(nc.vector.reciprocal(rs, rs))
                        link(nc.vector.tensor_scalar(on[:, 0:HD], ps[:, 6, 0:HD], rs, None, ALU.mult), "o_ev")

        def act_attention():
            for n in range(len(ITEMS) + 2):
                if n < len(ITEMS):
                    it = ITEMS[n]
                    nc.scalar.wait_ge(sg("lg_max"), n + 1)
                    if it[0] == "p":
                        rs = rsum[:, it[1] % 2, it[2]:it[2] + 1]
                        if it[2] == 0 and it[1] >= 3:
                            nc.scalar.wait_ge(sg("o_ev"), it[1] - 2)
                    else:
                        rs = rsum[:, 2, n - len(ITEMS) + 5:n - len(ITEMS) + 6]
                    p = lm[n % 2][:, 0:width(it)]
                    nc.scalar.activation(p, p, ACT.Exp, scale=HD ** -0.5, bias=mx[:, n % 2:n % 2 + 1], accum_out=rs)\
                        .then_inc(sg("pr_exp"), 1)
                if 1 <= n <= len(ITEMS):
                    m = n - 1
                    it = ITEMS[m]
                    nc.scalar.wait_ge(sg("pr_tr"), m + 1)
                    if m >= 2:
                        nc.scalar.wait_ge(sg("o_mm"), m - 1)
                    if it[0] == "m":
                        nc.scalar.sem_inc(sg("pr_ev_a"), 1)
                    else:
                        u, N = (1, min(it[1], 3)) if it[0] == "p" else (0, 2)
                        nc.scalar.activation(pT[m % 2][:, u:u + N, :].rearrange("p u c -> p (u c)"),
                                             ps[:, 4, 0:P * N], ACT.Copy).then_inc(sg("pr_ev_a"), 1)
                if n - 2 in DONE:
                    it, d = ITEMS[n - 2], DONE.index(n - 2)
                    nc.scalar.wait_ge(sg("o_tr"), d + 1)
                    if it[0] == "p":
                        nc.scalar.activation(xn[:, 0:4, COL0[it[1]]:COL0[it[1]] + P],
                                             ps[:, 7, :].rearrange("p (u c) -> p u c", u=4), ACT.Copy)\
                            .then_inc(sg("mix_a"), 1)
                        continue
                    for e in range(2):
                        if it[0] == "s":
                            g, a = it[1:]
                            src = ps[0:HD, 7, 0:P].rearrange("p (s h q) -> p h s q", s=4, h=4)[:, e::2]
                            dst = xn[HD * e:HD * (e + 1), 2 * g:2 * g + 2, 32 * a:32 * (a + 1)]\
                                .rearrange("p h (s q) -> p h s q", s=4)
                        else:
                            src = ps[0:HD, 7, 0:P].rearrange("p (h q) -> p h q", h=8)[:, e::2]
                            dst = xn[HD * e:HD * (e + 1), 0:4, SAMP:HEAD]
                        ins = nc.scalar.activation(dst, src, ACT.Copy)
                    ins.then_inc(sg("mix_a"), 1)

        v5 = region(24 * T, NT, HGH * P)
        HB = 24 * T + NT * HGH * P
        at5 = [region(HB + NT * P * e, NT, P) for e in range(2)]
        kd5 = region(HB + 2 * NT * P, NT, P)
        hsp = region(HB + 3 * NT * P, SEQ // HC, P)
        HC0 = HB + 3 * NT * P + SEQ // HC * P
        hmask = region(HC0, NSEG, P)
        kkall = region(HC0 + NSEG * P, HGH, T)
        hst = [region(HC0 + NSEG * P + HGH * T + NS * P * e, NS, P) for e in range(2)]
        qe = region(HC0 + NSEG * P + HGH * T + 2 * NS * P, T)
        xt = [xn[:, k, :] for k in range(KT)]
        cb, dd, ee, kdT = (xt[0], xt[1]), (xt[2], xt[3]), (xt[4], xt[5]), (xt[6], xt[7])
        xe = [sq[:, 0, :], sq[:, 1, :]]
        hp_fin = sp_st.rearrange("p a h c -> p (a h) c")
        oT5 = region(0, HGH, T)
        ecl = sb("ecl", [P, 2, NSEG + SEQ // HC])
        FROM = [0, 0, 0, SAMP, HEAD, HEAD]

        def v_bank(a, t):
            return (NT * a + t) % 8

        def pe_values5():
            for j in range(VUNITS):
                a, q = j // 4, j % 4
                nc.tensor.wait_ge(w_lo, Units.values + j + 1)
                nc.tensor.wait_ge(bank_free, Units.values + 2)
                wh, wl = wsp[:, j % 2, 0, :], wsp[:, j % 2, 1, :]
                for t in range(NT):
                    if a and q == 0 and v_bank(a, t) < NT:
                        nc.tensor.wait_ge(sg("v_out"), v_bank(a, t) + 1)
                    c = slice(COL0[t], COL0[t] + ROWS[t])
                    for k in range(2):
                        for x, w_ in ((x_hi, wh), (x_hi, wl), (x_lo, wh)):
                            mm = nc.tensor.matmul(ps[0:ROWS[t], v_bank(a, t), :], x[:, 2 * q + k, c],
                                                  w_[:, 512 * k:512 * (k + 1)],
                                                  start=(q == 0 and k == 0 and x is x_hi and w_ is wh),
                                                  stop=(q == 3 and k == 1 and x is x_lo))
                mm.then_inc(w_used, 1)

        def act_values5():
            for j in range(VUNITS):
                if j < VUNITS - 2:
                    act_w_hi(Units.values, VUNITS, 0, j + 2)
                a, q = j // 4, j % 4
                if q == 3:
                    nc.scalar.wait_ge(w_used, Units.values + j + 1)
                    for t in range(NT):
                        nc.scalar.activation(v5[0:ROWS[t], t, 512 * a:512 * (a + 1)], ps[0:ROWS[t], v_bank(a, t), :],
                                             ACT.Copy).then_inc(sg("v_out"), 1)

        def lower_bounds():
            dlink(nc.vector.tensor_tensor(lbv[:, 0, :], vec[:, V_LB1:V_LB1 + 8], vec[:, V_LB0:V_LB0 + 8],
                                          ALU.subtract))
            dlink(nc.vector.tensor_scalar(lbv[:, 1, :], lbv[:, 0, :], -1.0, None, ALU.mult), "lb_diff")

        def blocks(v, l):
            b = 1 << l
            return v[:, FROM[l]:T].rearrange("p (n o b) -> p n o b", o=2, b=b)

        NL = HLEVELS + 1

        def ends(v):
            out = []
            for a, n, c in ((0, NS, QS), (SAMP, 1, META), (HEAD, SEQ // HC, HC)):
                w_ = v[:, a:a + n * c].rearrange("p (n c) -> p n c", c=c)
                out.append((w_, w_[:, :, c - 1:c]))
            return out

        PERIODS = range(HGH + 2)

        def dec_no(hd, l):
            return NL * hd + 1 + l

        def act_hgrn():
            nc.scalar.wait_ge(sg("lb_diff"), 1)
            nc.scalar.wait_ge(sg("v_out"), 2 * NT)
            nc.scalar.activation(lbv[:, :, :], lbv[:, :, :], ACT.Sigmoid).then_inc(sg("lb"), 1)
            for hd in range(HGH):
                nc.scalar.activation(kkall[:, hd], proj[:, hd, :], ACT.Sigmoid, scale=-1.0)\
                    .then_inc(sg("hg_sig"), 1)
                nc.scalar.activation(proj[:, hd, :], proj[:, hd, :], ACT.Sigmoid).then_inc(sg("hg_sig"), 1)
            nc.scalar.preload_act_table_set("natural_log_exp_and_others")
            act_front_ln(0)
            act_decay(dec_no(0, -1), 0)
            for hd in PERIODS:
                for l in range(NL):
                    if hd < HGH and l < HLEVELS:
                        act_decay(dec_no(hd, l), FROM[l])
                    if 0 <= hd - 1 < HGH:
                        act_hgrn_post(hd - 1, l)
                    if l == 1 and 0 <= hd - 2:
                        nc.scalar.wait_ge(sg("go_mm"), hd - 1)
                        act_root(rn[:, :], ps[:, 6:8, 0:HALF], 1.0 / P, C("eps"), "go_ln", "go_rt")
                    if l == 3 and hd + 1 < HGH:
                        act_front_ln(hd + 1)
                    if l == 5:
                        if hd + 1 < HGH:
                            act_decay(dec_no(hd + 1, -1), 0)
                        if hd < HGH:
                            if hd:
                                nc.scalar.wait_ge(sg("hg_done"), hd)
                            nc.scalar.activation(qe, cb[hd % 2], ACT.Exp).then_inc(sg("hg_qe"), 1)

        def act_front_ln(hd):
            nc.scalar.wait_ge(sg("hg_f"), hd + 1)
            nc.scalar.activation(proj[:, hd, :], proj[:, hd, :], ACT.Ln).then_inc(sg("hg_ln"), 1)

        def act_decay(i, a):
            nc.scalar.wait_ge(sg("hg_dif"), i + 1)
            if i >= 2:
                nc.scalar.wait_ge(sg("hg_mul"), i - 1)
            nc.scalar.activation(ee[i % 2][:, a:T], dd[i % 2][:, a:T], ACT.Exp).then_inc(sg("hg_exp"), 1)

        def act_hgrn_post(hd, l):
            if l == 0:
                nc.scalar.wait_ge(sg("hg_kt"), hd + 1)
                if hd:
                    nc.scalar.wait_ge(sg("hp_kv"), hd)
                nc.scalar.activation(kd5[:, 1:NT, :], ps[:, 4, :].rearrange("p (t c) -> p t c", t=4), ACT.Copy)
                nc.scalar.activation(kd5[0:HEAD, 0, :], ps[0:HEAD, 5, 0:P], ACT.Copy).then_inc(sg("hg_kdt"), 1)
            if l == 2:
                nc.scalar.wait_ge(sg("hs_o"), hd + 1)
                nc.scalar.activation(oT5[:, hd, 0:HEAD], ps[:, 5, 0:HEAD], ACT.Copy).then_inc(sg("hs_ob"), 1)
            if l == 6:
                nc.scalar.wait_ge(sg("hp_o"), hd + 1)
                nc.scalar.activation(oT5[:, hd, HEAD:T].rearrange("p (n o c) -> p o n c", o=2, c=HC),
                                     ps[:, 4:6, 0:SEQ // 2].rearrange("p o (n c) -> p o n c", c=HC), ACT.Copy)\
                    .then_inc(sg("hp_ob"), 1)
                nc.scalar.wait_ge(sg("hp_ob"), hd + 1)
                if hd:
                    nc.scalar.wait_ge(sg("go_x"), hd)
                nc.scalar.activation(rn[:, :], oT5[:, hd, :], ACT.Square).then_inc(sg("go_sq"), 1)

        def pool_hgrn():
            for e in range(2):
                nc.gpsimd.memset(at5[e], 0.0).then_inc(sg("hg_zero"), 1)
            pool_dif_end(0)
            for hd in range(HGH):
                for l in range(HLEVELS):
                    i = dec_no(hd, l)
                    nc.gpsimd.wait_ge(sg("hg_exp"), i - 1)
                    b = 1 << l
                    c_, d_ = blocks(cb[hd % 2], l), blocks(dd[i % 2], l)
                    mid = c_[:, :, 0, b - 1:b].to_broadcast([P, c_.shape[1], b])
                    nc.gpsimd.tensor_tensor(d_[:, :, 0, :], mid, c_[:, :, 0, :], ALU.subtract)
                    nc.gpsimd.tensor_tensor(d_[:, :, 1, :], c_[:, :, 1, :], mid, ALU.subtract)\
                        .then_inc(sg("hg_dif"), 1)
                    if l == 3:
                        if hd:
                            nc.gpsimd.wait_ge(sg("hs_kv"), hd)
                        nc.gpsimd.tensor_tensor(hmask[0:HEAD], v5[0:HEAD, 0:1, P * hd:P * (hd + 1)]
                                                .to_broadcast([HEAD, NSEG, P]),
                                                C("seg")[0:HEAD, :].rearrange("p (s o) -> p s o", o=1)
                                                .to_broadcast([HEAD, NSEG, P]), ALU.mult).then_inc(sg("hs_vm"), 1)
                if hd + 1 < HGH:
                    pool_dif_end(hd + 1)

        def pool_dif_end(hd):
            i = dec_no(hd, -1)
            nc.gpsimd.wait_ge(sg("hg_cb"), hd + 1)
            if i >= 2:
                nc.gpsimd.wait_ge(sg("hg_exp"), i - 1)
            for (w_, l_), (o_, _) in zip(ends(cb[hd % 2]), ends(dd[i % 2])):
                ins = nc.gpsimd.tensor_tensor(o_, l_.to_broadcast(list(w_.shape)), w_, ALU.subtract)
            ins.then_inc(sg("hg_dif"), 1)

        def dve_front_f(hd):
            nc.vector.wait_ge(sg("hg_sig"), 2 * hd + 2)
            nc.vector.tensor_scalar(kkall[:, hd], kkall[:, hd], lbv[:, 1, hd:hd + 1], None, ALU.mult)
            nc.vector.tensor_scalar(proj[:, hd, :], proj[:, hd, :], lbv[:, 1, hd:hd + 1], lbv[:, 0, hd:hd + 1],
                                    ALU.mult, ALU.add).then_inc(sg("hg_f"), 1)

        def dve_front_scan(hd):
            nc.vector.wait_ge(sg("hg_ln"), hd + 1)
            if hd >= 2:
                nc.vector.wait_ge(sg("hg_qe"), hd - 1)
                nc.vector.wait_ge(sg("hg_dif"), NL * (hd - 1))
            nc.vector.tensor_tensor_scan(cb[hd % 2], C("sin"), proj[:, hd, :], 0.0, ALU.mult, ALU.add)\
                .then_inc(sg("hg_cb"), 1)

        def dve_front_kd(hd):
            i = dec_no(hd, -1)
            nc.vector.wait_ge(sg("hg_exp"), i + 1)
            nc.vector.wait_ge(sg("hg_f"), hd + 1)
            if hd >= 2:
                nc.vector.wait_ge(sg("hg_kt"), hd - 1)
            nc.vector.tensor_tensor(kdT[hd % 2], kkall[:, hd], ee[i % 2], ALU.mult).then_inc(sg("hg_mul"), 1)

        def dve_level(hd, l):
            n, i = NL * hd + l, dec_no(hd, l)
            nc.vector.wait_ge(sg("hg_exp"), i + 1)
            if n >= 2:
                nc.vector.wait_ge(sg("hg_g"), xe_reader(hd, l))
            e_, x_ = blocks(ee[i % 2], l), blocks(xe[l % 2], l)
            nc.vector.tensor_tensor(x_[:, :, 0, :], blocks(kkall[:, hd], l)[:, :, 0, :], e_[:, :, 0, :], ALU.mult)
            nc.vector.tensor_tensor(x_[:, :, 1, :], blocks(proj[:, 8 + hd, :], l)[:, :, 1, :], e_[:, :, 1, :],
                                    ALU.mult).then_inc(sg("hg_mul"), 1)

        def dve_hgrn(link):
            nc.vector.wait_ge(sg("hg_zero"), 2)
            nc.vector.wait_ge(sg("lb"), 1)
            nc.vector.wait_ge(sg("keep_in"), 16)
            nc.vector.wait_ge(sg("state_out"), 32)
            dve_front_f(0)
            dve_front_scan(0)
            dve_front_kd(0)
            for hd in PERIODS:
                for l in range(NL):
                    if hd < HGH and l < HLEVELS:
                        dve_level(hd, l)
                    p_, g_ = hd - 1, hd - 2
                    post = 0 <= p_ < HGH
                    if l == 3 and post:
                        nc.vector.wait_ge(sg("hs_m"), p_ + 1)
                        if hd < HGH:
                            nc.vector.wait_ge(sg("hg_g"), NL * hd + 3)
                        link(nc.vector.tensor_copy(hsp[:, 0, :], ps[:, meta_bank(p_), P:2 * P]), "hs_m0")
                    if l == 0 and post:
                        take(p_, HLEVELS)
                        nc.vector.wait_ge(sg("hg_qe"), p_ + 1)
                        q = proj[:, 8 + p_, :]
                        nc.vector.tensor_tensor(q, q, qe, ALU.mult)
                        a = 0
                        for _, l_ in ends(qe):
                            n = l_.shape[1]
                            ins = nc.vector.tensor_copy(ecl[:, p_ % 2, a:a + n].rearrange("p (n o) -> p n o", o=1), l_)
                            a += n
                        link(ins, "hg_done")
                    if l and hd < HGH:
                        take(hd, l - 1)
                    if l == 1 and hd + 1 < HGH:
                        dve_front_f(hd + 1)
                    if l == 2 and 0 <= g_:
                        o = oT5[:, g_, :]
                        nc.vector.wait_ge(sg("go_rt"), g_ + 1)
                        link(nc.vector.scalar_tensor_tensor(out=o, in0=o, scalar=vec[:, V_HGN:V_HGN + 1],
                                                            in1=rn[:, :], op0=ALU.mult, op1=ALU.mult), "go_x")
                        nc.vector.tensor_tensor(o, o, proj[:, 16 + g_, :], ALU.mult).then_inc(sg("go_out"), 1)
                    if l == 3 and post:
                        nc.vector.wait_ge(sg("hs_kv"), p_ + 1)
                        for s in range(NS):
                            st_ = hst[p_ % 2][:, s, :]
                            ins = nc.vector.scalar_tensor_tensor(out=st_, in0=st_, scalar=ecl[:, p_ % 2, s:s + 1],
                                                                 in1=ps[:, 6 + s // 4, P * (s % 4):P * (s % 4 + 1)],
                                                                 op0=ALU.mult, op1=ALU.add)
                        ins.then_inc(sg("hs_s"), 1)
                    if l == 4 and hd + 1 < HGH:
                        dve_front_scan(hd + 1)
                    if l == 5 and post:
                        nc.vector.wait_ge(sg("hp_kv"), p_ + 1)
                        for c in range(SEQ // HC):
                            dst = hsp[:, c + 1, :] if c + 1 < SEQ // HC else hp_fin[:, p_, :]
                            link(nc.vector.scalar_tensor_tensor(
                                out=dst, in0=hsp[:, c, :], scalar=ecl[:, p_ % 2, NSEG + c:NSEG + c + 1],
                                in1=ps[:, 6 + c % 2, P * (c // 2):P * (c // 2 + 1)], op0=ALU.mult, op1=ALU.add), "hp_s")
                    if l == 6 and hd + 1 < HGH:
                        dve_front_kd(hd + 1)

        def xe_reader(hd, l):
            return NL * hd + l - 1 if l >= 2 else NL * (hd - 1) + HLEVELS - 1 + (l % 2)

        def take(hd, l):
            n = NL * hd + l
            m = C("ident" if l == HLEVELS else f"lev{l}").bitcast(I32)
            nc.vector.wait_ge(sg("hg_g"), n + 1)
            if hd >= 2 and l == 0:
                nc.vector.wait_ge(sg("hp_o"), hd - 1)
            b = 2 * (n % 2)
            a_ = at5[hd % 2]
            ins = nc.vector.copy_predicated(a_[:, 1:NT, :], m.rearrange("p (o c) -> p o c", o=1)
                                            .to_broadcast([P, 4, P]),
                                            ps[:, b, :].rearrange("p (t c) -> p t c", t=4))
            r = slice(0, HEAD) if l < 3 or l == HLEVELS else slice(SAMP, HEAD)
            if l <= 3 or l == HLEVELS:
                ins = nc.vector.copy_predicated(a_[r, 0, r], m[r, r], ps[r, b + 1, r])
            dlink(ins, "hg_take")

        def meta_bank(hd):
            return 2 * ((NL * (hd + 1) + 2) % 2) + 1

        def pe_level(hd, l):
            n = NL * hd + l
            if n >= 2:
                nc.tensor.wait_ge(sg("hg_take"), n - 1)
            if l == HLEVELS:
                nc.tensor.wait_ge(sg("hg_f"), hd + 1)
            else:
                nc.tensor.wait_ge(sg("hg_mul"), dec_no(hd, l) + 1)
            b = 2 * (n % 2)
            x_ = xe[l % 2]
            for t in range(NT):
                c = slice(COL0[t], COL0[t] + ROWS[t])
                o = ps[0:HEAD, b + 1, 0:HEAD] if t == 0 else ps[:, b, P * (t - 1):P * t]
                if l == HLEVELS:
                    mm = nc.tensor.matmul(o, kkall[:, hd, c], proj[:, 8 + hd, c], start=True, stop=True)
                elif t or l < 3:
                    mm = nc.tensor.matmul(o, x_[:, c], x_[:, c], start=True, stop=True)
                elif l == 3:
                    c = slice(SAMP, HEAD)
                    mm = nc.tensor.matmul(ps[c, b + 1, c], x_[:, c], x_[:, c], start=True, stop=True)
            mm.then_inc(sg("hg_g"), 1)

        def pe_hgrn():
            for hd in PERIODS:
                for l in range(NL):
                    p_ = hd - 1
                    post = 0 <= p_ < HGH
                    if l == 2 and post:
                        nc.tensor.wait_ge(sg("hg_kdt"), p_ + 1)
                        nc.tensor.wait_ge(sg("hs_vm"), p_ + 1)
                        nc.tensor.wait_ge(sg("hg_take"), min(NL * hd + 1, NL * HGH))
                        nc.tensor.matmul(ps[:, meta_bank(p_), P:2 * P], kd5[0:HEAD, 0, :], hmask[0:HEAD, NS, :],
                                         start=True, stop=True).then_inc(sg("hs_m"), 1)
                    if hd < HGH:
                        pe_level(hd, l)
                    if l == 0 and 0 <= hd - 2:
                        nc.tensor.wait_ge(sg("go_sq"), hd - 1)
                        nc.tensor.wait_ge(sg("hp_s"), SEQ // HC * (hd - 1))
                        for e in range(2):
                            mm = nc.tensor.matmul(ps[:, 6 + e, 0:HALF], C("ones"), rn[:, e * HALF:(e + 1) * HALF],
                                                  start=True, stop=True)
                        mm.then_inc(sg("go_mm"), 1)
                    if post:
                        pe_hgrn_post(p_, l)

        def pe_hgrn_post(hd, l):
            vh = slice(P * hd, P * (hd + 1))
            if l == 0:
                if hd:
                    nc.tensor.wait_ge(sg("hp_ob"), hd)
                    nc.tensor.wait_ge(sg("hs_ob"), hd)
                for t in range(NT):
                    c = slice(COL0[t], COL0[t] + ROWS[t])
                    o = ps[0:HEAD, 5, 0:P] if t == 0 else ps[:, 4, P * (t - 1):P * t]
                    mm = nc.tensor.transpose(o, kdT[hd % 2][:, c], C("ident"))
                mm.then_inc(sg("hg_kt"), 1)
            if l == 1:
                nc.tensor.wait_ge(sg("hg_kdt"), hd + 1)
                nc.tensor.wait_ge(sg("hg_done"), hd + 1)
                nc.tensor.wait_ge(sg("hs_in" + str(hd % 2)), 16 * (hd // 2 + 1))
                for s in range(NS):
                    c = slice(QS * s, QS * (s + 1))
                    nc.tensor.matmul(ps[:, 5, c], hst[hd % 2][:, s, :], proj[:, 8 + hd, c], start=(s == 0),
                                     stop=False, skip_group_check=True)
                nc.tensor.matmul(ps[:, 5, 0:HEAD], v5[0:HEAD, 0, vh], at5[hd % 2][0:HEAD, 0, 0:HEAD],
                                 start=False, stop=True, skip_group_check=True).then_inc(sg("hs_o"), 1)
            if l == 2:
                if hd:
                    nc.tensor.wait_ge(sg("go_ln"), hd)
                for b in range(2):
                    mm = nc.tensor.matmul(ps[:, 6 + b, :], kd5[0:HEAD, 0, :],
                                          hmask[0:HEAD, 4 * b:4 * b + 4, :].rearrange("p s c -> p (s c)"),
                                          start=True, stop=True)
                mm.then_inc(sg("hs_kv"), 1)
            if l == 4:
                nc.tensor.wait_ge(sg("hs_s"), hd + 1)
                for c in range(SEQ // HC):
                    t, r = 1 + c // 2, slice(HC * (c % 2), HC * (c % 2) + HC)
                    mm = nc.tensor.matmul(ps[:, 6 + c % 2, P * (c // 2):P * (c // 2 + 1)], kd5[r, t, :], v5[r, t, vh],
                                          start=True, stop=True)
                mm.then_inc(sg("hp_kv"), 1)
            if l == 6:
                nc.tensor.wait_ge(sg("hs_ob"), hd + 1)
                nc.tensor.wait_ge(sg("hp_s"), SEQ // HC * (hd + 1) - 1)
                for c in range(SEQ // HC):
                    t, r = 1 + c // 2, slice(HC * (c % 2), HC * (c % 2) + HC)
                    o = ps[:, 4 + c % 2, HC * (c // 2):HC * (c // 2 + 1)]
                    nc.tensor.matmul(o, v5[r, t, vh], at5[hd % 2][r, t, r], start=True, stop=False)
                    mm = nc.tensor.matmul(o, hsp[:, c, :], proj[:, 8 + hd, HEAD + HC * c:HEAD + HC * (c + 1)],
                                          start=False, stop=True)
                mm.then_inc(sg("hp_o"), 1)

        def sp_hgrn_states(sp):
            sp.wait_ge(sg("v_out"), 2 * NT)
            for hd in range(HGH + 2):
                if hd >= 2:
                    sp.wait_ge(sg("hs_s"), hd - 1)
                    sp.dma_start(hgrn_s[:, hd - 2], hst[hd % 2]).then_inc(sg("hs_out" + str(hd % 2)), 16)
                if hd < HGH:
                    if hd >= 2:
                        sp.wait_ge(sg("hs_out" + str(hd % 2)), 16 * (hd // 2))
                    sp.dma_start(hst[hd % 2], shgrn[:, hd]).then_inc(sg("hs_in" + str(hd % 2)), 16)
            sp.wait_ge(sg("hp_s"), SEQ // HC * HGH)
            sp.dma_start(hgrn_p, hp_fin).then_inc(sg("hp_out"), 16)

        def sp_weights(sp, a, b):
            with sp.Fori(0, b - a) as i:
                for s in range(SLOTS):
                    sp.wait_ge(w_lo, SLOTS * i + (SLOTS * a + s + 1))
                    sp.dma_start(ring[:, s, :], w[SLOTS * i + (SLOTS * (a + 1) + s)]).then_inc(w_in[s], 16)

        block = ctx.enter_context(nc.Block())

        @block.sync
        def _(sp):
            sp.dma_start(h[:, :, :], x).then_inc(x_in, 16)
            for s in range(SLOTS):
                sp.dma_start(ring[:, s, :], w[s]).then_inc(w_in[s], 16)
            sp_weights(sp, 0, U_EVEN // SLOTS)
            sp.wait_ge(sg("pt_in"), 16)
            sp.wait_ge(w_used, U_EVEN)
            for s in range(NS):
                for g in range(NPG):
                    pg = sp.value_load(pt_sb[0:1, NPG * s + g:NPG * s + g + 1], min_val=0, max_val=NPOOL - 1)
                    c = slice(PAGE * g, PAGE * (g + 1))
                    sp.dma_start(kp[:, s, c], kpages[pg]).then_inc(sg("pages_in"), 16)
                    for b in (0, HD):
                        sp.dma_start(ikp[b:b + HD, s, c], ikpages[pg]).then_inc(sg("pages_in"), 16)
                    sp.dma_start(vp[:, NPG * s + g, :], vpages[pg]).then_inc(sg("pages_in"), 16)
            sp_weights(sp, U_EVEN // SLOTS, Units.out_o // SLOTS)
            sp_hgrn_states(sp)
            sp_weights(sp, Units.out_o // SLOTS, UNITS // SLOTS - 1)
            sp.wait_ge(sg("x_f"), 5 * KT)
            sp.dma_start(y, xn[:, :, :]).then_inc(sg("y_out"), 16)
            sp.wait_ge(sg("y_out"), 16)
            sp.wait_ge(sg("hs_out0"), 16 * (HGH // 2))
            sp.wait_ge(sg("hs_out1"), 16 * (HGH // 2))
            sp.wait_ge(sg("hp_out"), 16)

        @block.gpsimd
        def _(pool):
            pool.dma_start(pt_sb[:, :], ptab).then_inc(sg("pt_in"), 16)
            pool.wait_ge(w_used, U_EVEN)
            pool.dma_start(hist[:, :, :, 0:CONV_W - 1], stconv).then_inc(sg("hist_in"), 16)
            pool_rope()
            pool_conv()
            pool.wait_ge(sg("roped"), len(ROPED))
            pool.dma_start(C("sin"), keep).then_inc(sg("keep_in"), 16)
            pool.dma_start(krows, proj[:, AK0, :]).then_inc(sg("rows_out"), 16)
            pool.dma_start(ikrows, proj[0:HD, IK0, :]).then_inc(sg("rows_out"), 16)
            pool.dma_start(vrows, tokm[:, :, 0:P]).then_inc(sg("rows_out"), 16)
            pool.dma_start(convo_p, proj[:, 0:12, T - 3:T]).then_inc(sg("conv_out"), 16)
            pool.dma_start(convo_s, hist).then_inc(sg("conv_out"), 16)
            pool_sample_queries()
            pool.wait_ge(sg("conv_out"), 32)
            pool.wait_ge(sg("l2_done"), 8)
            pool.wait_ge(sg("mix_a"), len(DONE))
            pool.wait_ge(sg("rows_out"), 48)
            pool.dma_start(st, sdelta).then_inc(sg("st_in"), 16)
            pool_inv()
            pool_gdn_scan()
            pool.wait_ge(sg("sc_kv0"), DNH)
            pool.wait_ge(sg("sc_s"), NT)
            pool.dma_start(delta_s, st).then_inc(sg("state_out"), 16)
            pool.dma_start(delta_p, sp_st[:, NT % 2]).then_inc(sg("state_out"), 16)
            pool.wait_ge(sg("v_out"), 2 * NT)
            pool_hgrn()

        @block.scalar
        def _(act):
            act.dma_start(cst[:, :], consts).then_inc(const_in, 16)
            act.dma_start(vec[:, :], vecs).then_inc(const_in, 16)
            act.dma_start(wsm, wsmall).then_inc(small_in, 16)
            act.wait_ge(const_in, 32)
            act_w_hi(0, GROUP, 0, 0)
            act_w_hi(0, GROUP, 0, 1)
            act_norm(0)
            act_small()
            act_dense(3, Units.even, proj, ACT.Copy, more=False)
            act_silu()
            act_l2()
            act_scores()
            act_attention()
            nc.scalar.activation(proj[:, Z0:Z0 + 4, :], proj[:, Z0:Z0 + 4, :], ACT.Silu).then_inc(sg("z_gate"), 1)
            act_gdn_prep()
            act_inv()
            act_gdn_scan()
            act.wait_ge(sg("sc_ob"), NT)
            act.wait_ge(sg("conv_out"), 32)
            act_w_hi(Units.out_e, GROUP, 0, 0)
            act_w_hi(Units.out_e, GROUP, 0, 1)
            for k in range(4):
                act_x_hi(xn, k, "mix_a", len(DONE))
            gate_norm("act", DNH, O_E, z_e, V_DN, "ge", 6)
            act_out(Units.out_e)
            act_norm(1)
            act_ffn(0, Units.ffn0)
            act_norm(2)
            act.wait_ge(sg("state_out"), 32)
            act_dense(1, Units.odd, proj, ACT.Copy)
            act_dense(2, Units.odd + 8, region(8 * T, 16, T), ACT.Silu)
            act_values5()
            act_hgrn()
            act.wait_ge(sg("go_mm"), HGH)
            act_w_hi(Units.out_o, GROUP, 0, 0)
            act_w_hi(Units.out_o, GROUP, 0, 1)
            act.wait_ge(sg("hs_out0"), 16 * (HGH // 2))
            act.wait_ge(sg("hs_out1"), 16 * (HGH // 2))
            for k in range(KT):
                act_x_hi(oT5, k, "go_out", k + 1)
            act_out(Units.out_o)
            act_norm(3)
            act_ffn(1, Units.ffn1, more=False)
            act_norm(4)

        @block.vector
        def _(dve):
            dve.wait_ge(const_in, 32)
            dlink(nc.vector.memset(mx[:, :], 0.0), "bank_free")
            dlink(nc.vector.memset(mx[:, :], 0.0), "bank_free")
            dve_w_lo(0, GROUP, 0, 0)
            dve_w_lo(0, GROUP, 0, 1)
            dve_norm(0, xn0)
            dve_small(dlink)
            dve_w_los(3, Units.even, more=False)
            dve_rope(dlink)
            dve_conv(dlink)
            dve_l2(dlink)
            nc.vector.wait_ge(sg("conv_out"), 32)
            dve_select(dlink)
            dve_attention(dlink)
            dve_gdn_prep(dlink)
            dve_inv(dlink)
            dve_gdn_scan(dlink)
            dve_w_lo(Units.out_e, GROUP, 0, 0)
            dve_w_lo(Units.out_e, GROUP, 0, 1)
            for k in range(4):
                dve_x_lo(xn, k)
            gate_norm("dve", DNH, O_E, z_e, V_DN, "ge", 6)
            dve_out(Units.out_e)
            dve_norm(1, xn)
            dve_ffn(0, Units.ffn0)
            dve_norm(2, xn)
            dve_w_los(3, Units.odd)
            for j in range(VUNITS - 2):
                dve_w_lo(Units.values, VUNITS, 0, j + 2)
            lower_bounds()
            dve.wait_ge(sg("v_out"), 2 * NT)
            dve_hgrn(dlink)
            dve_w_lo(Units.out_o, GROUP, 0, 0)
            dve_w_lo(Units.out_o, GROUP, 0, 1)
            for k in range(KT):
                dve_x_lo(oT5, k)
            dve_out(Units.out_o)
            dve_norm(3, xn)
            dve_ffn(1, Units.ffn1, more=False)
            dve_norm(4, xn)

        @block.tensor
        def _(pe):
            pe.wait_ge(const_in, 32)
            pe_norm(0)
            pe_small()
            pe_dense(3, Units.even, 0)
            pe_rope()
            pe_l2()
            pe_scores()
            pe_expand()
            pe_attention()
            pe_gdn_prep()
            pe_inv()
            pe_gdn_scan()
            gate_norm("pe", DNH, O_E, z_e, V_DN, "ge", 6)
            pe_dense(1, Units.out_e, 1)
            pe_norm(1)
            pe_ffn(0, Units.ffn0)
            pe_norm(2)
            pe_dense(3, Units.odd, 3)
            pe_values5()
            pe.wait_ge(sg("v_out"), 2 * NT)
            pe_hgrn()
            pe_dense(1, Units.out_o, 4)
            pe_norm(3)
            pe_ffn(1, Units.ffn1)
            pe_norm(4)


def unit_columns():
    dq = 1092
    cols = [np.arange(dq + P * m, dq + P * (m + 1)) for m in range(12)]
    cols += [np.arange(2636 + P * m, 2636 + P * (m + 1)) for m in range(4)]
    ik = np.arange(1024, 1088)
    cols += [np.concatenate([ik, ik]), np.arange(512, 640)]
    cols += [np.arange(768 + P * m, 768 + P * (m + 1)) for m in range(2)]
    cols += [np.concatenate([np.arange(HD * j, HD * j + HD), np.arange(HD * (j + 4), HD * (j + 5))]) for j in range(4)]
    return np.concatenate(cols)


def units_up(w):
    n = w.shape[1] // P
    return w.reshape(KT, P, n, P).transpose(2, 1, 0, 3).reshape(n, P, KT * P)


def units_ffn(up, down):
    down = down.reshape(4, KT, P, KT, P).transpose(0, 3, 2, 1, 4).reshape(4, GROUP, P, KT * P)
    return np.concatenate([units_up(up).reshape(4, GROUP, P, KT * P), down], axis=1).reshape(U_FFN, P, KT * P)


def units_values(w):
    return w.reshape(4, 2, P, 2, 512).transpose(3, 0, 2, 1, 4).reshape(VUNITS, P, KT * P)


def kernel(x_prompt, x_sample, cache_k, cache_v, cache_ik, state_conv, state_delta, state_hgrn, page_table,
           meta, ln_mix, ln_ffn, ln_final, w_in_e, w_out_e, dn_conv, dn_a_log, dn_dt_bias, dn_norm,
           w_in_o, w_out_o, hg_lb, hg_norm, w_up, w_down):
    import concourse.bacc as _bacc
    from concourse.bass_utils import run_bass_kernel_spmd as _run

    A = np.asarray

    def fm(v):
        return A(v).reshape(-1, KT, P).transpose(2, 1, 0)

    def cols(v):
        return A(v).reshape(-1, P).T

    table, at, keep = constant_table()
    wi = A(w_in_e)[0]
    wo = A(w_in_o)[0]
    fqz = np.concatenate([wo[:, D:2 * D], wo[:, 0:D], wo[:, 3 * D:4 * D]], axis=1)
    units = np.concatenate([
        units_up(wi[:, unit_columns()]), units_up(A(w_out_e)[0]), units_ffn(A(w_up)[0], A(w_down)[0]),
        units_up(fqz), units_values(wo[:, 2 * D:3 * D]), units_up(A(w_out_o)[0]),
        units_ffn(A(w_up)[1], A(w_down)[1])])
    small = wi[:, np.concatenate([np.arange(640, 768), np.arange(1088, 1092), np.arange(2628, 2636)])]
    lb = A(hg_lb)
    vecs = np.concatenate([
        cols(A(ln_mix)[0]), cols(A(ln_ffn)[0]), cols(A(ln_mix)[1]), cols(A(ln_ffn)[1]), cols(ln_final),
        A(dn_conv)[0].reshape(CONV_W, 12, P).transpose(2, 1, 0).reshape(P, 48),
        cols(A(dn_norm)[0]), cols(A(hg_norm)[0]),
        np.broadcast_to(A(dn_dt_bias)[0], (P, 4)), np.broadcast_to(A(dn_a_log)[0], (P, 4)),
        cols(lb[0]), cols(lb[1])], axis=1)
    ins = {
        "x": np.concatenate([fm(A(x_sample).reshape(SAMP, D)), fm(meta), fm(A(x_prompt)[0])], axis=2),
        "consts": table, "keep": keep, "w": units,
        "wsmall": small.reshape(KT, P, SMALL).transpose(1, 0, 2),
        "vecs": vecs,
        "stconv": A(state_conv)[0].reshape(NS, 3, 12, P).transpose(3, 2, 0, 1),
        "sdelta": A(state_delta)[0].transpose(2, 1, 0, 3).reshape(P, DNH, NS * P),
        "shgrn": A(state_hgrn)[0].transpose(2, 1, 0, 3),
        "kpages": A(cache_k)[0].reshape(NPOOL, PAGE, P).transpose(0, 2, 1),
        "ikpages": A(cache_ik)[0].transpose(0, 2, 1),
        "vpages": A(cache_v)[0].reshape(NPOOL, PAGE, P),
        "ptab": A(page_table).reshape(1, NS * NPG),
    }
    outs = {
        "y": (P, KT, T), "krows": (P, T), "vrows": (P, NT, P), "ikrows": (HD, T), "convo_p": (P, 12, 3),
        "convo_s": (P, 12, NS, 11), "delta_p": (P, DNH, P), "delta_s": (P, DNH, NS * P),
        "hgrn_p": (P, HGH, P), "hgrn_s": (P, HGH, NS, P),
    }
    nc = _bacc.Bacc("TRN2", target_bir_lowering=False, num_devices=1)
    arrays, args = {}, {}
    for name, a in ins.items():
        a = np.ascontiguousarray(a)
        arrays["in_" + name] = a
        args[name] = nc.dram_tensor("in_" + name, a.shape, mybir.dt.from_np(a.dtype), kind="ExternalInput").ap()
    for name, shape in outs.items():
        args[name] = nc.dram_tensor("out_" + name, shape, F32, kind="ExternalOutput").ap()
    hybrid_step(nc, at=at, **args)
    r = _run(nc, [arrays], core_ids=[0]).results[0]
    o = {name: A(r["out_" + name]).reshape(shape) for name, shape in outs.items()}

    y = o["y"].transpose(2, 1, 0).reshape(T, D)
    kr, ikr = o["krows"].T, o["ikrows"].T
    vr = np.concatenate([o["vrows"][0:HEAD, 0]] + [o["vrows"][:, t] for t in range(1, NT)])
    cs = o["convo_s"][:, :, :, 8:11].transpose(2, 3, 1, 0).reshape(1, NS, 3, 12 * P)
    return (
        y[None, HEAD:], y[:SAMP].reshape(NS, QS, D),
        kr[SAMP:].reshape(1, 1, META + SEQ, KVH, HD), vr[SAMP:].reshape(1, 1, META + SEQ, KVH, HD),
        ikr[SAMP:].reshape(1, 1, META + SEQ, HD),
        o["convo_p"].transpose(2, 1, 0).reshape(1, 1, 3, 12 * P),
        o["delta_p"].transpose(1, 0, 2)[None, None],
        o["hgrn_p"].transpose(1, 0, 2)[None, None],
        kr[:SAMP].reshape(1, NS, QS, KVH, HD), vr[:SAMP].reshape(1, NS, QS, KVH, HD),
        ikr[:SAMP].reshape(1, NS, QS, HD), cs,
        o["delta_s"].reshape(P, DNH, NS, P).transpose(2, 1, 0, 3)[None],
        o["hgrn_s"].transpose(2, 1, 0, 3)[None],
    )
```

```python
from contextlib import ExitStack

import numpy as np

import concourse.bass as bass
from concourse import mybir

F32 = mybir.dt.float32
F32R = mybir.dt.float32r
I32 = mybir.dt.int32
ALU = mybir.AluOpType
ACT = mybir.ActivationFunctionType
AX = mybir.AxisListType

P = 128
D = 1024
KT = D // P
NS, QS = 8, 8
SAMP = NS * QS
META = 16
HEAD = SAMP + META
SEQ = 512
T = HEAD + SEQ
HALF = T // 2
NT = 1 + SEQ // P
PAST, PAGE = 256, 128
NPG = PAST // PAGE
NPOOL = 20
GROUP = 8
SLOTS = 4
A_HEADS, KVH, HD = 8, 2, 64
IDX_HEADS = 4
DNH = 4
HGH = 8
CONV_W = 4
NSEG = NS + 1
EPS = 1e-6
NEG = -3.0e38
K_PROMPT = SEQ // 4 - META
K_SAMPLE = (PAST + QS) // 4 - META

U_EVEN, U_OUT_E, U_FFN, U_ODD, U_OUT_O = 24, 8, 64, 32, 8
VUNITS = 8
UNITS = U_EVEN + U_OUT_E + U_FFN + U_ODD + U_OUT_O + U_FFN
Q0, K0, V0, Z0, IK0, AK0, IQ0, AQ0 = 0, 4, 8, 12, 16, 17, 18, 20
EVEN_TILES = list(range(IK0, 24)) + list(range(Q0, Z0)) + list(range(Z0, IK0))
CONV_AT = 8

SMALL = P + IDX_HEADS + 2 * DNH
O_IW, O_DB, O_DA = P, P + 4, P + 8

ROWS = [HEAD] + [P] * (NT - 1)
COL0 = [0] + [HEAD + P * i for i in range(NT - 1)]
LEVELS = 7
HLEVELS = 6
HC = 64


def constant_table():
    parts = {}
    i = np.arange(P)
    parts["ident"] = np.eye(P)
    parts["ones"] = np.ones((P, P))
    half = HD // 4 // 2
    rot = np.zeros((P, P))
    for b in (0, HD):
        for d in range(half):
            rot[b + d, b + half + d] = -1.0
            rot[b + half + d, b + d] = 1.0
    parts["rotT"] = rot.T
    pos = np.concatenate([PAST + np.tile(np.arange(QS), NS), np.arange(META + SEQ)]).astype(np.float32)
    inv = (np.float32(500000.0) ** (-np.arange(half, dtype=np.float32) / np.float32(half))).astype(np.float32)
    ang = (pos[None, :] * inv[:, None]).astype(np.float32).astype(np.float64)
    cos, sin = np.ones((P, T)), np.zeros((P, T))
    for b in (0, HD):
        for r in (0, half):
            cos[b + r:b + r + half] = np.cos(ang)
            sin[b + r:b + r + half] = np.sin(ang)
    parts["cos"], parts["sin"] = cos, sin
    seg = np.full(P, -1)
    seg[:SAMP] = np.arange(SAMP) // QS
    seg[SAMP:HEAD] = NS
    same = (seg[:, None] == seg[None, :]) & (seg[:, None] >= 0)
    upper = i[:, None] <= i[None, :]
    for n, blk in (("0", same), ("1", np.ones((P, P), bool))):
        parts["cum" + n] = blk & upper
        parts["rest" + n] = blk & ~upper
        parts["decm" + n] = np.where(blk & upper, 0.0, NEG)
    sm = np.zeros((P, NSEG))
    sm[np.arange(HEAD), seg[:HEAD]] = 1
    parts["seg"] = sm
    for l in range(LEVELS):
        b = 1 << l
        parts[f"lev{l}"] = ((i[:, None] // (2 * b) == i[None, :] // (2 * b))
                            & (i[:, None] % (2 * b) < b) & (i[None, :] % (2 * b) >= b))
    parts["causal"] = np.where(i[None, :] <= i[:, None], 0.0, NEG)
    nb = np.full((P, SAMP), NEG)
    s = np.arange(SAMP)
    nb[:SAMP] = np.where((s[:, None] // QS == s[None, :] // QS) & (s[None, :] <= s[:, None]), 0.0, NEG)
    parts["newb"] = nb
    mb = np.full((P, HEAD), NEG)
    mb[:, SAMP:] = np.where(np.arange(META)[None, :] <= (i % META)[:, None], 0.0, NEG)
    parts["metab"] = mb
    ex = np.zeros((P, 2, P))
    for a in range(2):
        for c in range(P):
            ex[(4 * a + c // 32) * QS + c % QS, a, c] = 1
    parts["expand"] = ex.reshape(P, 2 * P)
    keep = np.ones((P, T))
    keep[:, 0:SAMP:QS] = 0
    keep[:, SAMP] = 0
    keep[:, HEAD::HC] = 0
    parts["eps"] = np.full((P, 1), EPS)
    parts["eps128"] = np.full((P, 1), EPS * P)
    parts["one"] = np.ones((P, 1))
    at, cols = {}, 0
    for n, v in parts.items():
        at[n] = (cols, v.shape[1])
        cols += v.shape[1]
    return np.concatenate([v.astype(np.float32) for v in parts.values()], axis=1), at, keep.astype(np.float32)


def hybrid_step(nc, x, consts, keep, at, w, wsmall, vecs, stconv, sdelta, shgrn, kvpages, ptab,
                y, krows, vrows, ikrows, convo_p, convo_s, delta_p, delta_s, hgrn_p, hgrn_s):
    ctx = ExitStack()
    with ctx:
        def sb(name, shape, dt=F32):
            return ctx.enter_context(nc.sbuf_tensor(name, shape, dt))

        def sem(name):
            return ctx.enter_context(nc.semaphore(name))

        ps = ctx.enter_context(nc.psum_tensor("ps", [P, 8, 512], F32))
        def overlay(*parts):
            with ExitStack() as inner:
                return [inner.enter_context(nc.sbuf_tensor(*a)) for a in parts]

        NARENA = 31040
        NSPLIT, NX = 2 * 2 * KT * P, KT * T
        x_lo, hid, _, wsp, x_hi = overlay(("x_lo", [P, KT, T], F32R), ("hid", [P, 2, GROUP, T], F32R),
                                          ("gap", [P, NARENA - NX - NSPLIT - 2 * GROUP * T], F32),
                                          ("wsp", [P, 2, 2, KT * P], F32R), ("x_hi", [P, KT, T], F32R))
        xn = sb("xn", [P, KT, T])
        arena = sb("arena", [P, NARENA])
        h = sb("h", [P, KT, T])
        ring = sb("ring", [P, SLOTS, KT * P])
        cst = sb("cst", [P, consts.shape[1]])
        vec = sb("vec", [P, vecs.shape[1]])
        sq = sb("sq", [P, 2, T])
        rn = sb("rn", [P, T])
        NARENA = 31040
        tokm = sb("tokm", [P, NT, SMALL])
        gates = sb("gates", [P, 8, NT * 4])
        pt_sb = sb("pt_sb", [1, NS * NPG], I32)

        def C(name):
            a, n = at[name]
            return cst[:, a:a + n]

        def region(a, *dims):
            n = int(np.prod(dims))
            assert a + n <= NARENA, (a, dims)
            v = arena[:, a:a + n]
            if len(dims) == 1:
                return v
            if len(dims) == 2:
                return v.rearrange("p (a b) -> p a b", a=dims[0])
            return v.rearrange("p (a b c) -> p a b c", a=dims[0], b=dims[1])

        V_LN = 0
        V_CONV = 40
        V_DN, V_HGN = 88, 89
        V_DTB, V_ALOG = 90, 94
        V_LB0, V_LB1 = 98, 106
        negA = sb("negA", [P, 4])
        lbv = sb("lbv", [P, 2, 8])

        proj = region(0, 24, T)
        M = 24 * T
        NSCR = 6816
        ct2 = region(M + NSCR, 2, T)
        B = NARENA - NSPLIT - NX
        pages = region(B, NS * NPG, 3 * P).rearrange("p (s g) (a c) -> p s g a c", s=NS, a=3)

        S = {}

        def sg(name):
            if name not in S:
                S[name] = sem(name)
            return S[name]

        const_in, small_in = sg("const_in"), sg("small_in")
        w_in = [sg(f"w_in{s}") for s in range(SLOTS)]
        w_hi, w_lo, w_used = sg("w_hi"), sg("w_lo"), sg("w_used")
        bank_free = sg("bank_free")
        dve_chain, act_chain, pool_chain = sg("dve_chain"), sg("act_chain"), sg("pool_chain")
        counts = {}

        def linker(eng, chain):
            def link(ins, name=None):
                s_ = sg(name) if name else chain
                counts[s_.name] = counts.get(s_.name, 0) + 1
                ins.then_inc(s_, 1)
                eng.wait_ge(s_, counts[s_.name])
            return link

        dlink = linker(nc.vector, dve_chain)
        alink = linker(nc.scalar, act_chain)
        plink = linker(nc.gpsimd, pool_chain)

        def pairs(v):
            return v.rearrange("p (n c) -> p n c", n=2)

        def heads(v, n=4):
            return v.rearrange("p (h c) -> p h c", h=n)

        class Units:
            even = 0
            out_e = U_EVEN
            ffn0 = out_e + U_OUT_E
            odd = ffn0 + U_FFN
            values = odd + 24
            out_o = values + VUNITS
            ffn1 = out_o + U_OUT_O

        M_OUT_O = Units.out_o - VUNITS

        XIN = 4

        def act_square(n, k):
            if n == 0:
                nc.scalar.wait_ge(sg(f"x_in{k * XIN // KT}"), 16)
            else:
                m0 = (Units.out_e, Units.odd - 8, M_OUT_O, UNITS - VUNITS - 8)[n - 1]
                nc.scalar.wait_ge(bank_free, m0 + k + 3)
            if n in (2, 4) and k == 0:
                nc.scalar.wait_ge(sg("hid_split"), 4 * GROUP * n // 2)
            if k >= 2:
                nc.scalar.wait_ge(sg("norm_add"), (KT - 2) * n + max(1, k - 2))
            nc.scalar.activation(sq[:, k % 2, :], h[:, k, :], ACT.Square).then_inc(sg("norm_sq"), 1)

        def add_squares(eng, n):
            for k in range(1, KT - 1):
                c = (KT - 2) * n + k
                eng.wait_ge(sg("norm_sq"), KT * n + k + 1)
                if k == 1:
                    if n:
                        eng.wait_ge(sg("x_f"), KT * n)
                    eng.tensor_tensor(rn[:, :], sq[:, 0, :], sq[:, 1, :], ALU.add).then_inc(sg("norm_add"), 1)
                else:
                    eng.wait_ge(sg("norm_add"), c - 1)
                    eng.tensor_tensor(rn[:, :], rn[:, :], sq[:, k % 2, :], ALU.add).then_inc(sg("norm_add"), 1)

        def act_norm(n):
            nc.scalar.wait_ge(sg("norm_mm"), n + 1)
            act_root(rn[:, :], ps[:, 6:8, 0:HALF], 1.0 / D, C("eps"), "norm_ln", "norm_rt")
            if n < 4:
                for k in range(KT):
                    act_x_hi(xn if n else xn0, k, "x_f", KT * n + k + 1)

        def act_root(dst, sums, scale, bias, logs, roots):
            nc.scalar.activation(pairs(dst), sums, ACT.Ln, scale=scale, bias=bias).then_inc(sg(logs), 1)
            counts[logs] = counts.get(logs, 0) + 1
            nc.scalar.wait_ge(sg(logs), counts[logs])
            nc.scalar.activation(dst, dst, ACT.Exp, scale=-0.5).then_inc(sg(roots), 1)

        def pe_norm(n):
            nc.tensor.wait_ge(sg("norm_add"), (KT - 2) * (n + 1))
            if n:
                nc.tensor.wait_ge(sg("norm_ln"), n)
            for last, v in enumerate((rn[:, :], sq[:, 1, :])):
                if last:
                    nc.tensor.wait_ge(sg("norm_sq"), KT * (n + 1))
                for e in range(2):
                    mm = nc.tensor.matmul(ps[:, 6 + e, 0:HALF], C("ones"), v[:, e * HALF:(e + 1) * HALF],
                                          start=(not last), stop=bool(last))
            mm.then_inc(sg("norm_mm"), 1)

        def dve_norm(n, dst):
            nc.vector.wait_ge(sg("norm_rt"), n + 1)
            for k in range(KT + 1):
                if k < KT:
                    ins = nc.vector.scalar_tensor_tensor(out=dst[:, k, :], in0=h[:, k, :],
                                                         scalar=vec[:, V_LN + 8 * n + k:V_LN + 8 * n + k + 1],
                                                         in1=rn[:, :], op0=ALU.mult, op1=ALU.mult)
                    ins.then_inc(sg("x_f"), 1)
                if k and n < 4:
                    dve_x_lo(dst, k - 1)

        def act_x_hi(src, k, ready, n):
            nc.scalar.wait_ge(sg(ready), n)
            nc.scalar.activation(x_hi[:, k, :], src[:, k, :], ACT.Copy).then_inc(sg("x_hi"), 1)

        split_count = [0]

        def dve_x_lo(src, k):
            split_count[0] += 1
            nc.vector.wait_ge(sg("x_hi"), split_count[0])
            nc.vector.tensor_tensor(x_lo[:, k, :], src[:, k, :], x_hi[:, k, :].bitcast(F32), ALU.subtract)\
                .then_inc(sg("x_split"), 1)

        def loaded(base, per, i, j):
            return 16 * (base // SLOTS + per // SLOTS * i + j // SLOTS + 1)

        def act_w_hi(base, per, i, j):
            nc.scalar.wait_ge(w_in[j % SLOTS], loaded(base, per, i, j))
            if not (base == 0 and j < 2 and isinstance(i, int) and i == 0):
                nc.scalar.wait_ge(w_used, base + per * i + j - 1)
            nc.scalar.activation(wsp[:, j % 2, 0, :], ring[:, j % SLOTS, :], ACT.Copy).then_inc(w_hi, 1)

        def dve_w_lo(base, per, i, j):
            nc.vector.wait_ge(w_hi, base + per * i + j + 1)
            nc.vector.tensor_tensor(wsp[:, j % 2, 1, :], ring[:, j % SLOTS, :], wsp[:, j % 2, 0, :].bitcast(F32),
                                    ALU.subtract).then_inc(w_lo, 1)

        def pe_unit(base, per, i, j, x, first=None):
            nc.tensor.wait_ge(w_lo, base + per * i + j + 1)
            m0 = base if base < Units.out_o else base - VUNITS
            nc.tensor.wait_ge(bank_free, m0 + 1 + per * i + j)
            wh, wl = wsp[:, j % 2, 0, :], wsp[:, j % 2, 1, :]
            for k in range(KT):
                if first:
                    first(k)
                for a, b in ((wh, x[0]), (wh, x[1]), (wl, x[0])):
                    for e in range(2):
                        mm = nc.tensor.matmul(ps[:, 2 * (j % 2) + e, 0:HALF], a[:, k * P:(k + 1) * P],
                                              b[:, k, e * HALF:(e + 1) * HALF],
                                              start=(k == 0 and a is wh and b is x[0]),
                                              stop=(k == KT - 1 and a is wl))
            mm.then_inc(w_used, 1)

        X_SPLIT = (x_hi, x_lo)
        HID = (hid[:, 0], hid[:, 1])

        def x_tiles(n):
            return lambda k: nc.tensor.wait_ge(sg("x_split"), KT * n + k + 1)

        def pe_dense(groups, u0, n):
            with nc.tensor.Fori(0, groups) as i:
                for j in range(GROUP):
                    pe_unit(u0, GROUP, i, j, X_SPLIT, x_tiles(n) if j == 0 else None)

        def act_evacuate(base, i, j, dst, func):
            nc.scalar.wait_ge(w_used, base + GROUP * i + j + 1)
            if not isinstance(i, int):
                nc.scalar.wait_ge(const_in, 32)
            nc.scalar.activation(pairs(dst), ps[:, 2 * (j % 2):2 * (j % 2) + 2, 0:HALF], func).then_inc(bank_free, 1)

        def act_dense(groups, u0, dst, func, more=True):
            def step(i, last):
                for j in range(GROUP):
                    if j < GROUP - 2 or not last:
                        act_w_hi(u0, GROUP, i, j + 2)
                    act_evacuate(u0, i, j, dst[:, GROUP * i + j, :], func)
            with nc.scalar.Fori(0, groups if more else groups - 1) as i:
                step(i, False)
            if not more:
                step(groups - 1, True)

        def dve_w_los(groups, u0, more=True):
            def step(i, last):
                for j in range(GROUP):
                    if j < GROUP - 2 or not last:
                        dve_w_lo(u0, GROUP, i, j + 2)
            with nc.vector.Fori(0, groups if more else groups - 1) as i:
                step(i, False)
            if not more:
                step(groups - 1, True)

        def act_out(u0, norm):
            for j in range(GROUP):
                act_w_hi(u0, GROUP, 0, j + 2)
                act_square(norm, j)

        def dve_residual(base, per, i, j, k):
            nc.vector.wait_ge(w_used, base + per * i + j + 1)
            nc.vector.tensor_tensor(pairs(h[:, k, :]), pairs(h[:, k, :]), ps[:, 2 * (j % 2):2 * (j % 2) + 2, 0:HALF],
                                    ALU.add).then_inc(bank_free, 1)

        def dve_out(u0):
            for j in range(GROUP):
                dve_residual(u0, GROUP, 0, j, j)
                dve_w_lo(u0, GROUP, 0, j + 2)

        STEP, STEPS = 2 * GROUP, U_FFN // (2 * GROUP)

        def pe_ffn(n, u0):
            with nc.tensor.Fori(0, STEPS) as i:
                for j in range(GROUP):
                    pe_unit(u0, STEP, i, j, X_SPLIT, x_tiles(3 * n + 2) if j == 0 else None)
                for j in range(GROUP, STEP):
                    pe_unit(u0, STEP, i, j, HID, (lambda k: nc.tensor.wait_ge(
                        sg("hid_split"), 4 * GROUP * n + GROUP * i + k + 1)) if j == GROUP else None)

        def ffn_steps(eng, step, more):
            with eng.Fori(0, STEPS if more else STEPS - 1) as i:
                step(i, False)
            if not more:
                step(STEPS - 1, True)

        def act_ffn(n, u0, more=True):
            def step(i, last, squares=False):
                for j in range(STEP):
                    if j < STEP - 2 or not last:
                        act_w_hi(u0, STEP, i, j + 2)
                    if j < GROUP:
                        nc.scalar.wait_ge(sg("hid_sq"), 4 * GROUP * n + GROUP * i + j + 1)
                        nc.scalar.activation(hid[:, 0, j, :], sq[:, j % 2, :], ACT.Copy).then_inc(sg("hid_hi"), 1)
                    if squares and j >= GROUP:
                        act_square(2 * n + 2, j - GROUP)
            with nc.scalar.Fori(0, STEPS - 1) as i:
                step(i, False)
            step(STEPS - 1, not more, squares=True)

        def dve_ffn(n, u0, more=True):
            def step(i, last):
                for j in range(STEP):
                    if j < GROUP:
                        nc.vector.wait_ge(w_used, u0 + STEP * i + j + 1)
                        pr = ps[:, 2 * (j % 2):2 * (j % 2) + 2, 0:HALF]
                        nc.vector.tensor_scalar(pairs(sq[:, j % 2, :]), pr, 0.0, None, ALU.max).then_inc(bank_free, 1)
                        nc.vector.wait_ge(bank_free, u0 - VUNITS * n + STEP * i + j + 3)
                        nc.vector.tensor_tensor(sq[:, j % 2, :], sq[:, j % 2, :], sq[:, j % 2, :], ALU.mult)\
                            .then_inc(sg("hid_sq"), 1)
                    else:
                        dve_residual(u0, STEP, i, j, j - GROUP)
                    if j < STEP - 2 or not last:
                        dve_w_lo(u0, STEP, i, j + 2)
                    if j < GROUP:
                        nc.vector.wait_ge(sg("hid_hi"), 4 * GROUP * n + GROUP * i + j + 1)
                        nc.vector.tensor_tensor(hid[:, 1, j, :], sq[:, j % 2, :], hid[:, 0, j, :].bitcast(F32),
                                                ALU.subtract).then_inc(sg("hid_split"), 1)
            ffn_steps(nc.vector, step, more)

        def pe_small():
            nc.tensor.wait_ge(small_in, 16)
            nc.tensor.wait_ge(sg("x_f"), KT)
            for t in range(NT):
                if t >= 2:
                    nc.tensor.wait_ge(sg("small_ev"), t - 1)
                for k in range(KT):
                    mm = nc.tensor.matmul(ps[0:ROWS[t], 4 + t % 2, 0:SMALL], xn0[:, k, COL0[t]:COL0[t] + ROWS[t]],
                                          wsm[:, k, :], start=(k == 0), stop=(k == KT - 1))
                mm.then_inc(sg("small_mm"), 1)

        xn0 = region(M, KT, T)
        wsm = region(M + KT * T, KT, SMALL)

        def G(n):
            return gates[:, n, :].rearrange("p (t h) -> p t h", t=NT)

        def bct(v):
            return v.rearrange("p (o h) -> p o h", o=1).to_broadcast([P, NT, 4])

        G_BETA, G_G, G_IW, G_A, G_B, G_C, G_ED = range(7)

        def dve_small(link):
            link(nc.vector.memset(tokm[:, 0, :], 0.0))
            for t in range(NT):
                nc.vector.wait_ge(sg("small_mm"), t + 1)
                link(nc.vector.tensor_copy(tokm[0:ROWS[t], t, :], ps[0:ROWS[t], 4 + t % 2, 0:SMALL]), "small_ev")
            link(nc.vector.tensor_tensor(G(G_A), tokm[:, :, O_DA:O_DA + 4], bct(vec[:, V_DTB:V_DTB + 4]), ALU.add))
            nc.vector.tensor_scalar(G(G_IW), tokm[:, :, O_IW:O_IW + 4], (IDX_HEADS * HD) ** -0.5, None, ALU.mult)
            link(nc.vector.tensor_scalar(G(G_C), G(G_A), 0.0, None, ALU.max), "gate_z")

        def dve_decay(link):
            nc.vector.wait_ge(sg("gate_act"), 5)
            link(nc.vector.tensor_tensor(G(G_C), G(G_C), G(G_B), ALU.add))
            link(nc.vector.scalar_tensor_tensor(out=G(G_G), in0=G(G_C), scalar=-1.0,
                                                in1=bct(negA[:, :]), op0=ALU.mult, op1=ALU.mult), "gate_g")

        def act_small():
            nc.scalar.wait_ge(sg("gate_z"), 1)
            nc.scalar.activation(negA[:, :], vec[:, V_ALOG:V_ALOG + 4], ACT.Exp).then_inc(sg("gate_act"), 1)
            nc.scalar.activation(G(G_BETA), tokm[:, :, O_DB:O_DB + 4], ACT.Sigmoid).then_inc(sg("gate_act"), 1)
            nc.scalar.activation(G(G_B), G(G_A), ACT.Abs).then_inc(sg("gate_act"), 1)
            nc.scalar.wait_ge(sg("gate_act"), 3)
            nc.scalar.activation(G(G_B), G(G_B), ACT.Exp, scale=-1.0).then_inc(sg("gate_act"), 1)
            nc.scalar.wait_ge(sg("gate_act"), 4)
            nc.scalar.activation(G(G_B), G(G_B), ACT.Ln, bias=C("one")).then_inc(sg("gate_act"), 1)

        ROPED = list(range(IK0, 24))

        def pe_rope(n):
            nc.tensor.wait_ge(bank_free, n + 3)
            if n:
                nc.tensor.wait_ge(sg("rope_s"), n)
            for e in range(2):
                mm = nc.tensor.matmul(ps[:, 4 + e, 0:HALF], C("rotT"), proj[:, ROPED[n], e * HALF:(e + 1) * HALF],
                                      start=True, stop=True)
            mm.then_inc(sg("rope_mm"), 1)

        def pool_rope():
            for n, m in enumerate(ROPED):
                nc.gpsimd.wait_ge(sg("rope_mm"), n + 1)
                nc.gpsimd.tensor_tensor(proj[:, m, :], proj[:, m, :], C("cos"), ALU.mult).then_inc(sg("rope_c"), 1)

        def dve_rope(n, link):
            m = ROPED[n]
            nc.vector.wait_ge(sg("rope_mm"), n + 1)
            link(nc.vector.tensor_tensor(pairs(sq[:, n % 2, :]), ps[:, 4:6, 0:HALF], pairs(C("sin")), ALU.mult),
                 "rope_s")
            nc.vector.wait_ge(sg("rope_c"), n + 1)
            nc.vector.tensor_tensor(proj[:, m, :], proj[:, m, :], sq[:, n % 2, :], ALU.add).then_inc(sg("roped"), 1)

        spb = sb("spb", [P, 12 * NS * (CONV_W - 1 + QS)])
        hist = spb.rearrange("p (m s q) -> p m s q", m=12, s=NS)
        ctail = sb("ctail", [P, 12, CONV_W - 1])

        def tap(m, j):
            return vec[:, V_CONV + 4 * m + j:V_CONV + 4 * m + j + 1]

        def pool_conv():
            nc.gpsimd.wait_ge(sg("hist_in"), 16)
            link = plink
            tmp = region(M + 6512, NS, QS)
            for m in range(12):
                nc.gpsimd.wait_ge(bank_free, CONV_AT + m + 3)
                if m >= 2:
                    nc.gpsimd.wait_ge(sg("silu"), m - 1)
                link(nc.gpsimd.tensor_copy(hist[:, m, :, 3:11],
                                           proj[:, m, 0:SAMP].rearrange("p (s q) -> p s q", s=NS)))
                c4 = ct2[:, m % 2, 0:SAMP].rearrange("p (s q) -> p s q", s=NS)
                for j in range(CONV_W):
                    link(nc.gpsimd.tensor_scalar(tmp if j else c4, hist[:, m, :, j:j + QS], tap(m, j), None, ALU.mult))
                    if j:
                        link(nc.gpsimd.tensor_tensor(c4, c4, tmp, ALU.add), "conv_s" if j == CONV_W - 1 else None)

        def act_tap(m):
            nc.scalar.wait_ge(bank_free, CONV_AT + m + 3)
            nc.scalar.activation(ct2[:, m % 2, SAMP:T], proj[:, m, SAMP:T], ACT.Copy, scale=tap(m, 3))\
                .then_inc(sg("conv_t"), 1)

        def dve_conv(m, link):
            nc.vector.wait_ge(sg("conv_t"), m + 1)
            for j in (2, 1, 0):
                d = 3 - j
                link(nc.vector.scalar_tensor_tensor(out=ct2[:, m % 2, SAMP + d:T], in0=proj[:, m, SAMP:T - d],
                                                    scalar=tap(m, j), in1=ct2[:, m % 2, SAMP + d:T],
                                                    op0=ALU.mult, op1=ALU.add))
            link(nc.vector.tensor_copy(ctail[:, m, :], proj[:, m, T - 3:T]), "conv_p")

        def act_silu(m):
            nc.scalar.wait_ge(sg("conv_p"), m + 1)
            nc.scalar.wait_ge(sg("conv_s"), m + 1)
            nc.scalar.activation(proj[:, m, :], ct2[:, m % 2, :], ACT.Silu).then_inc(sg("silu"), 1)

        l2r = [rn[:, :], ct2[:, 0, :]]

        def act_l2_squares(pair):
            if pair == 0:
                nc.scalar.wait_ge(sg("silu"), 12)
                nc.scalar.wait_ge(sg("roped"), len(ROPED))
            for n in (2 * pair, 2 * pair + 1):
                if n >= 2:
                    nc.scalar.wait_ge(sg("l2_mm"), n - 1)
                nc.scalar.activation(sq[:, n % 2, :], proj[:, n, :], ACT.Square).then_inc(sg("l2_sq"), 1)

        def act_l2_roots(pair):
            for n in (2 * pair, 2 * pair + 1):
                nc.scalar.wait_ge(sg("l2_mm"), n + 1)
                if n >= 2:
                    nc.scalar.wait_ge(sg("l2_done"), n - 1)
                sc_, b = (float(P), C("eps128")) if n < 4 else (1.0, C("eps"))
                act_root(l2r[n % 2], ps[:, 4 + 2 * (n % 2):6 + 2 * (n % 2), 0:HALF], sc_, b, "l2_ln", "l2_rt")

        def pe_l2(pair):
            if pair == 0:
                nc.tensor.wait_ge(sg("idx_rel"), IDX_HEADS * (NT - 1))
            for n in (2 * pair, 2 * pair + 1):
                nc.tensor.wait_ge(sg("l2_sq"), n + 1)
                if n >= 2:
                    nc.tensor.wait_ge(sg("l2_ln"), n - 1)
                for e in range(2):
                    mm = nc.tensor.matmul(ps[:, 4 + 2 * (n % 2) + e, 0:HALF], C("ones"),
                                          sq[:, n % 2, e * HALF:(e + 1) * HALF], start=True, stop=True)
                mm.then_inc(sg("l2_mm"), 1)

        def dve_l2(n):
            nc.vector.wait_ge(sg("l2_rt"), n + 1)
            nc.vector.tensor_tensor(proj[:, n, :], proj[:, n, :], l2r[n % 2], ALU.mult).then_inc(sg("l2_done"), 1)

        GD = B
        xflat = xn.rearrange("p k t -> p (k t)")

        def in_xn(a):
            return xflat[:, a:a + 512].rearrange("p (h c) -> p h c", h=4)

        Tt = [region(GD + 512 * t, 4, P) for t in range(NT)]
        kd = [region(GD + 2560 + 512 * t, 4, P) for t in range(NT)]
        at_s = [region(GD + 5120, 4, P)] + [in_xn(4 * T + 512 * e) for e in range(4)]
        st = region(16 * T, 4, NS * P)
        X = [region(M + 512 * t, 4, P) for t in range(NT)]
        Ti = [region(M + 2560 + 512 * t, 4, P) for t in range(NT)]
        dec = [region(M + 5120 + 512 * e, 4, P) for e in range(2)]
        XL = [region(M + 6144, 4, P), rn[:, 0:512].rearrange("p (h c) -> p h c", h=4)]
        P1 = [sq[:, e, 0:512].rearrange("p (h c) -> p h c", h=4) for e in range(2)]
        ebc = sq[:, 1, 0:512].rearrange("p (h c) -> p h c", h=4)
        gcol = sb("gcol", [P, NT, 8])
        egl = sb("egl", [P, NT, 4, NSEG])

        def kT(hd, t):
            return proj[:, 4 + hd, COL0[t]:COL0[t] + ROWS[t]]

        def qT(hd, t):
            return proj[:, hd, COL0[t]:COL0[t] + ROWS[t]]

        def bank(b, R=P, C_=P):
            return ps[0:R, b, :].rearrange("p (h c) -> p h c", h=4)[:, :, 0:C_]

        def nseg(t):
            return NSEG if t == 0 else 1

        def pe_gdn_prep():
            nc.tensor.wait_ge(sg("gate_g"), 1)
            nc.tensor.wait_ge(sg("l2_done"), 8)
            nc.tensor.wait_ge(sg("mix_a"), len(DONE))
            for t in range(NT):
                R, v = ROWS[t], "0" if t == 0 else "1"
                g = G(G_G)[0:R, t, :]
                if t:
                    nc.tensor.wait_ge(sg("gd_col"), t)
                    nc.tensor.wait_ge(sg("gd_egl"), t)
                nc.tensor.matmul(ps[0:R, 4, 0:4], C("cum" + v)[0:R, 0:R], g, start=True, stop=True)
                nc.tensor.matmul(ps[0:R, 4, 4:8], C("rest" + v)[0:R, 0:R], g, start=True, stop=True)
                ends = C("seg")[0:R, :] if t == 0 else C("one")[0:R, :]
                for hd in range(DNH):
                    mm = nc.tensor.matmul(ps[:, 4, 16 + NSEG * hd:16 + NSEG * hd + nseg(t)],
                                          g[:, hd:hd + 1].to_broadcast([R, P]), ends, start=True, stop=True)
                mm.then_inc(sg("gd_a"), 1)
                if t:
                    nc.tensor.wait_ge(sg("gd_dec"), t)
                    nc.tensor.wait_ge(sg("gd_ebc"), t)
                for hd in range(DNH):
                    mm = nc.tensor.matmul(bank(5, P, R)[:, hd], g[:, hd:hd + 1].to_broadcast([R, P]),
                                          C("cum" + v)[0:R, 0:R], start=True, stop=True)
                mm.then_inc(sg("gd_b"), 1)
                if t:
                    nc.tensor.wait_ge(sg("gd_attn"), t)
                    nc.tensor.wait_ge(sg("gd_x"), t)
                    nc.tensor.wait_ge(sg("gd_kd"), t)
                for hd in range(DNH):
                    nc.tensor.matmul(bank(6, R, R)[:, hd], kT(hd, t), qT(hd, t), start=True, stop=True)
                    nc.tensor.matmul(bank(7, R, R)[:, hd], kT(hd, t), kT(hd, t), start=True, stop=True)
                    mm = nc.tensor.transpose(bank(0, R)[:, hd], kT(hd, t), C("ident"))
                mm.then_inc(sg("gd_c"), 1)

        def dve_gdn_prep(link):
            nc.vector.wait_ge(sg("conv_out"), 32)
            for t in range(NT):
                R, v, e = ROWS[t], "0" if t == 0 else "1", t % 2
                nc.vector.wait_ge(sg("gd_a"), t + 1)
                link(nc.vector.tensor_copy(gcol[0:R, t, :], ps[0:R, 4, 0:8]), "gd_col")
                nc.vector.wait_ge(sg("gd_b"), t + 1)
                for hd in range(DNH):
                    ins = nc.vector.scalar_tensor_tensor(out=dec[e][0:R, hd, 0:R], in0=bank(5, R, R)[:, hd],
                                                         scalar=gcol[0:R, t, hd:hd + 1],
                                                         in1=C("decm" + v)[0:R, 0:R], op0=ALU.subtract, op1=ALU.add)
                link(ins, "gd_dec")
                nc.vector.wait_ge(sg("gd_c"), t + 1)
                nc.vector.wait_ge(sg("gd_ex"), t + 1)
                link(nc.vector.tensor_tensor(at_s[t][0:R, :, 0:R], bank(6, R, R), dec[e][0:R, :, 0:R], ALU.mult),
                     "gd_attn")
                for hd in range(DNH):
                    ins = nc.vector.scalar_tensor_tensor(out=X[t][0:R, hd, 0:R], in0=bank(7, R, R)[:, hd],
                                                         scalar=G(G_BETA)[0:R, t, hd:hd + 1],
                                                         in1=dec[e][0:R, hd, 0:R], op0=ALU.mult, op1=ALU.mult)
                link(ins, "gd_x")
                nc.vector.wait_ge(sg("gd_ebc"), t + 1)
                q_, k_ = proj[:, 0:4, COL0[t]:COL0[t] + R], proj[:, 4:8, COL0[t]:COL0[t] + R]
                nc.vector.tensor_tensor(q_, q_, ebc[:, :, 0:R], ALU.mult)
                link(nc.vector.scalar_tensor_tensor(out=k_, in0=k_, scalar=-1.0, in1=ebc[:, :, 0:R],
                                                    op0=ALU.mult, op1=ALU.mult), "gd_qk")

        def act_gdn_prep():
            for t in range(NT):
                R, e = ROWS[t], t % 2
                nc.scalar.wait_ge(sg("gd_col"), t + 1)
                alink(nc.scalar.activation(G(G_ED)[0:R, t, :], gcol[0:R, t, 4:8], ACT.Exp))
                nc.scalar.activation(egl[:, t, :, 0:nseg(t)],
                                     ps[:, 4, 16:16 + 4 * NSEG].rearrange("p (h s) -> p h s", h=4)[:, :, 0:nseg(t)],
                                     ACT.Exp).then_inc(sg("gd_egl"), 1)
                nc.scalar.wait_ge(sg("gd_dec"), t + 1)
                nc.scalar.activation(dec[e][0:R, :, 0:R], dec[e][0:R, :, 0:R], ACT.Exp).then_inc(sg("gd_ex"), 1)
                if t:
                    nc.scalar.wait_ge(sg("gd_qk"), t)
                nc.scalar.activation(ebc[:, :, 0:R], bank(5, P, R), ACT.Exp).then_inc(sg("gd_ebc"), 1)
                nc.scalar.wait_ge(sg("gd_c"), t + 1)
                for hd in range(DNH):
                    ins = nc.scalar.activation(kd[t][0:R, hd, :], bank(0, R)[:, hd], ACT.Copy,
                                               scale=G(G_ED)[0:R, t, hd:hd + 1])
                ins.then_inc(sg("gd_kd"), 1)

        INV = [(l, t) for l in range(LEVELS) for t in range(NT) if t or l < 4]
        LAST = {t: (3 if t == 0 else LEVELS - 1) for t in range(NT)}

        def pool_inv():
            for n, (l, t) in enumerate(INV):
                R = ROWS[t]
                if l == 0:
                    nc.gpsimd.wait_ge(sg("gd_x"), t + 1)
                if n >= 2 and INV[n - 2][0] == 0:
                    nc.gpsimd.wait_ge(sg("inv_used"), n - 1)
                elif n >= 2:
                    nc.gpsimd.wait_ge(sg("inv_1"), n - 1 - NT)
                m = C(f"lev{l}")[0:R, 0:R].rearrange("p (o c) -> p o c", o=1).to_broadcast([R, 4, R])
                nc.gpsimd.tensor_tensor(XL[n % 2][0:R, :, 0:R], X[t][0:R, :, 0:R], m, ALU.mult)\
                    .then_inc(sg("inv_xl"), 1)

        def pe_inv():
            nc.tensor.wait_ge(sg("l2_rt"), 8)
            nc.tensor.wait_ge(sg("gd_kd"), NT)
            for n in range(len(INV) + 1):
                if n < len(INV):
                    l, t = INV[n]
                    R = ROWS[t]
                    nc.tensor.wait_ge(sg("inv_xl"), n + 1)
                    if l:
                        nc.tensor.wait_ge(sg("inv_used"), INV.index((l - 1, t)) + 1)
                        if n >= 2 + NT:
                            nc.tensor.wait_ge(sg("inv_p1"), n - 1 - NT)
                        for hd in range(DNH):
                            mm = nc.tensor.matmul(bank(n % 2, R, R)[:, hd], XL[n % 2][0:R, hd, 0:R],
                                                  Ti[t][0:R, hd, 0:R], start=True, stop=True)
                        mm.then_inc(sg("inv_1"), 1)
                    else:
                        if n >= 2:
                            nc.tensor.wait_ge(sg("inv_used"), n - 1)
                        for hd in range(DNH):
                            mm = nc.tensor.transpose(bank(2 + 2 * (n % 2), R, R)[:, hd], XL[n % 2][0:R, hd, 0:R],
                                                     C("ident")[0:R, 0:R])
                        mm.then_inc(sg("inv_2"), 1)
                m = n - 1
                if m < NT:
                    continue
                l, t = INV[m]
                R = ROWS[t]
                nc.tensor.wait_ge(sg("inv_p1"), m + 1 - NT)
                nc.tensor.wait_ge(sg("inv_used"), m - 1)
                for hd in range(DNH):
                    if l < LAST[t]:
                        nc.tensor.matmul(bank(2 + 2 * (m % 2), R, R)[:, hd], Tt[t][0:R, hd, 0:R],
                                         P1[m % 2][0:R, hd, 0:R], start=True, stop=True)
                    mm = nc.tensor.matmul(bank(3 + 2 * (m % 2), R, R)[:, hd], P1[m % 2][0:R, hd, 0:R],
                                          Tt[t][0:R, hd, 0:R], start=True, stop=True)
                mm.then_inc(sg("inv_2"), 1)

        def act_inv():
            nc.scalar.wait_ge(sg("gd_qk"), NT)
            for n, (l, t) in enumerate(INV):
                R = ROWS[t]
                if l:
                    nc.scalar.wait_ge(sg("inv_1"), n + 1 - NT)
                    if n >= 2 + NT:
                        nc.scalar.wait_ge(sg("inv_2"), n - 1)
                    nc.scalar.activation(P1[n % 2][0:R, :, 0:R], bank(n % 2, R, R), ACT.Copy)\
                        .then_inc(sg("inv_p1"), 1)

        def dve_inv(link):
            for n, (l, t) in enumerate(INV):
                R = ROWS[t]
                nc.vector.wait_ge(sg("inv_2"), n + 1)
                if l == 0:
                    i4 = C("ident")[0:R, 0:R].rearrange("p (o c) -> p o c", o=1).to_broadcast([R, 4, R])
                    nc.vector.wait_ge(sg("inv_xl"), n + 1)
                    nc.vector.tensor_tensor(Ti[t][0:R, :, 0:R], i4, bank(2 + 2 * (n % 2), R, R), ALU.subtract)
                    link(nc.vector.tensor_tensor(Tt[t][0:R, :, 0:R], i4, XL[n % 2][0:R, :, 0:R], ALU.subtract),
                         "inv_used")
                    continue
                if l < LAST[t]:
                    nc.vector.tensor_tensor(Ti[t][0:R, :, 0:R], Ti[t][0:R, :, 0:R], bank(2 + 2 * (n % 2), R, R),
                                            ALU.subtract)
                link(nc.vector.tensor_tensor(Tt[t][0:R, :, 0:R], Tt[t][0:R, :, 0:R],
                                             bank(3 + 2 * (n % 2), R, R), ALU.subtract),
                     "inv_used")

        RB = M + 512 * 10
        rbuf = region(RB, 4, P)
        vnew = region(RB + 512, 4, P)
        rT = region(RB + 1024, 4, P)
        qS = region(M + NSCR, DNH, SAMP)
        sp_st = spb[:, 0:2 * DNH * P].rearrange("p (a h c) -> p a h c", a=2, h=DNH)
        vmask = region(M, NSEG, P)
        oT = region(M + 2560, 4, T)

        def pe_gdn_scan():
            nc.tensor.wait_ge(sg("inv_used"), len(INV))
            nc.tensor.wait_ge(sg("gd_qk"), NT)
            nc.tensor.wait_ge(sg("st_in"), 16)
            for hd in range(DNH):
                both = ps[:, 0, P * hd:P * (hd + 1)].rearrange("p (a c) -> p a c", a=2)
                for s in range(NS):
                    c = slice(QS * s, QS * (s + 1))
                    mm = nc.tensor.matmul(both[:, :, c], st[:, hd, P * s:P * (s + 1)], proj[:, hd:hd + 5:4, c],
                                          start=True, stop=True)
            mm.then_inc(sg("sc_ks"), 1)
            nc.tensor.wait_ge(sg("sc_rt"), 1)
            for hd in range(DNH):
                mm = nc.tensor.transpose(bank(1, HEAD)[:, hd], rT[:, hd, 0:HEAD], C("ident"))
            mm.then_inc(sg("sc_r"), 1)
            for t in range(NT):
                R = ROWS[t]
                if t:
                    for hd in range(DNH):
                        nc.tensor.matmul(bank(1, R)[:, hd], proj[:, 8 + hd, COL0[t]:COL0[t] + R], C("ident"),
                                         start=(hd == 0), stop=False, skip_group_check=True)
                    nc.tensor.wait_ge(sg("sc_s"), t)
                    for hd in range(DNH):
                        mm = nc.tensor.matmul(bank(1, R)[:, hd], kT(hd, t), sp_st[:, t % 2, hd, :],
                                              start=False, stop=True, skip_group_check=True)
                    mm.then_inc(sg("sc_r"), 1)
                nc.tensor.wait_ge(sg("sc_rb"), t + 1)
                for hd in range(DNH):
                    mm = nc.tensor.matmul(bank(2, R)[:, hd], Tt[t][0:R, hd, 0:R], rbuf[0:R, hd, :],
                                          start=True, stop=True)
                mm.then_inc(sg("sc_v"), 1)
                nc.tensor.wait_ge(sg("sc_vn"), t + 1)
                if t:
                    for hd in range(DNH):
                        mm = nc.tensor.matmul(bank(4)[:, hd], kd[t][0:R, hd, :], vnew[0:R, hd, :],
                                              start=True, stop=True)
                    mm.then_inc(sg("sc_kv"), 1)
                    nc.tensor.wait_ge(sg("sc_ob"), t)
                for hd in range(DNH):
                    o = bank(3, P, R)[:, hd]
                    if t:
                        nc.tensor.matmul(o, sp_st[:, t % 2, hd, :], qT(hd, t), start=True, stop=False)
                    mm = nc.tensor.matmul(o, vnew[0:R, hd, :], at_s[t][0:R, hd, 0:R], start=(t == 0), stop=True)
                mm.then_inc(sg("sc_o"), 1)
                if t == 0:
                    for hd in range(DNH):
                        nc.tensor.wait_ge(sg("sc_vm"), hd + 1)
                        if hd:
                            nc.tensor.wait_ge(sg("sc_kv0"), hd)
                        for b, (a, n) in enumerate(((0, 4), (4, 4), (8, 1))):
                            mm = nc.tensor.matmul(ps[:, 4 + b, 0:n * P], kd[0][0:R, hd, :],
                                                  vmask[0:R, a:a + n, :].rearrange("p s c -> p (s c)"),
                                                  start=True, stop=True)
                        mm.then_inc(sg("sc_kvm"), 1)

        def pool_gdn_scan():
            nc.gpsimd.wait_ge(sg("sc_vn"), 1)
            for hd in range(DNH):
                if hd:
                    nc.gpsimd.wait_ge(sg("sc_kvm"), hd)
                nc.gpsimd.tensor_tensor(vmask[0:HEAD], vnew[0:HEAD, hd:hd + 1, :].to_broadcast([HEAD, NSEG, P]),
                                        C("seg")[0:HEAD, :].rearrange("p (s o) -> p s o", o=1)
                                        .to_broadcast([HEAD, NSEG, P]), ALU.mult).then_inc(sg("sc_vm"), 1)

        def act_gdn_scan():
            for t in range(NT):
                R = ROWS[t]
                nc.scalar.wait_ge(sg("sc_r"), t + 1)
                nc.scalar.activation(rbuf[0:R], bank(1, R), ACT.Copy).then_inc(sg("sc_rb"), 1)
                nc.scalar.wait_ge(sg("sc_v"), t + 1)
                if t == 1:
                    nc.scalar.wait_ge(sg("sc_vm"), DNH)
                if t:
                    nc.scalar.wait_ge(sg("sc_o"), t)
                for hd in range(DNH):
                    ins = nc.scalar.activation(vnew[0:R, hd, :], bank(2, R)[:, hd], ACT.Copy,
                                               scale=G(G_BETA)[0:R, t, hd:hd + 1])
                ins.then_inc(sg("sc_vn"), 1)

        def dve_gdn_scan(link):
            nc.vector.wait_ge(sg("sc_ks"), 1)
            nc.vector.tensor_copy(rT[:, :, SAMP:HEAD], proj[:, 8:12, SAMP:HEAD])
            nc.vector.tensor_copy(qS, bank(0, P, SAMP))
            link(nc.vector.tensor_tensor(rT[:, :, 0:SAMP], proj[:, 8:12, 0:SAMP], bank(0)[:, :, SAMP:2 * SAMP],
                                         ALU.add), "sc_rt")
            for t in range(NT):
                R = ROWS[t]
                if t == 0:
                    nc.vector.wait_ge(sg("sc_o"), 1)
                    nc.vector.tensor_copy(oT[:, :, SAMP:HEAD], bank(3)[:, :, SAMP:HEAD])
                    nc.vector.tensor_tensor(oT[:, :, 0:SAMP], qS, bank(3, P, SAMP), ALU.add).then_inc(sg("sc_ob"), 1)
                    for hd in range(DNH):
                        nc.vector.wait_ge(sg("sc_kvm"), hd + 1)
                        for s in range(NS):
                            nc.vector.scalar_tensor_tensor(out=st[:, hd, P * s:P * (s + 1)],
                                                           in0=st[:, hd, P * s:P * (s + 1)],
                                                           scalar=egl[:, 0, hd, s:s + 1],
                                                           in1=ps[:, 4 + s // 4, P * (s % 4):P * (s % 4 + 1)],
                                                           op0=ALU.mult, op1=ALU.add)
                        link(nc.vector.tensor_copy(sp_st[:, 1, hd, :], ps[:, 6, 0:P]), "sc_kv0")
                    nc.vector.sem_inc(sg("sc_s"), 1)
                    continue
                nc.vector.wait_ge(sg("sc_kv"), t)
                for hd in range(DNH):
                    ins = nc.vector.scalar_tensor_tensor(out=sp_st[:, (t + 1) % 2, hd, :], in0=sp_st[:, t % 2, hd, :],
                                                         scalar=egl[:, t, hd, 0:1], in1=bank(4)[:, hd],
                                                         op0=ALU.mult, op1=ALU.add)
                link(ins, "sc_s")
                nc.vector.wait_ge(sg("sc_o"), t + 1)
                nc.vector.tensor_copy(oT[:, :, COL0[t]:COL0[t] + R], bank(3, P, R)).then_inc(sg("sc_ob"), 1)

        def gate_norm(eng, nh, o, z, nv, tag, base_bank):
            if eng == "act":
                for n in range(nh):
                    b = base_bank - 2 * (n % 2)
                    if n == 0:
                        nc.scalar.wait_ge(*o["ready"])
                        nc.scalar.activation(sq[:, 0, :], o["v"](0), ACT.Square).then_inc(sg(tag + "_sq"), 1)
                        nc.scalar.activation(sq[:, 1, :], o["v"](1), ACT.Square).then_inc(sg(tag + "_sq"), 1)
                    nc.scalar.wait_ge(sg(tag + "_mm"), n + 1)
                    if n:
                        nc.scalar.wait_ge(sg(tag + "_x"), n)
                    act_root(rn[:, :], ps[:, b:b + 2, 0:HALF], 1.0 / P, C("eps"), tag + "_ln", tag + "_rt")
                    if n + 2 < nh:
                        nc.scalar.activation(sq[:, n % 2, :], o["v"](n + 2), ACT.Square).then_inc(sg(tag + "_sq"), 1)
                    if n:
                        act_x_hi(xn, KT - nh + n - 1, tag + "_out", n)
                act_x_hi(xn, KT - 1, tag + "_out", nh)
                return
            if eng == "pe":
                for n in range(nh):
                    nc.tensor.wait_ge(sg(tag + "_sq"), n + 1)
                    if n >= 2:
                        nc.tensor.wait_ge(sg(tag + "_ln"), n - 1)
                    for e in range(2):
                        mm = nc.tensor.matmul(ps[:, base_bank - 2 * (n % 2) + e, 0:HALF], C("ones"),
                                              sq[:, n % 2, e * HALF:(e + 1) * HALF], start=True, stop=True)
                    mm.then_inc(sg(tag + "_mm"), 1)
                return
            for n in range(nh):
                nc.vector.wait_ge(sg(tag + "_rt"), n + 1)
                dlink(nc.vector.scalar_tensor_tensor(out=o["v"](n), in0=o["v"](n), scalar=vec[:, nv:nv + 1],
                                                     in1=rn[:, :], op0=ALU.mult, op1=ALU.mult), tag + "_x")
                nc.vector.tensor_tensor(xn[:, KT - nh + n, :], o["v"](n), z(n), ALU.mult).then_inc(sg(tag + "_out"), 1)
                if n:
                    dve_x_lo(xn, KT - nh + n - 1)
            dve_x_lo(xn, KT - 1)

        O_E = {"ready": (sg("sc_ob"), NT), "v": lambda n: oT[:, n, :]}

        def z_e(n):
            return proj[:, Z0 + n, :]

        bias = [None] + [region(M + o, HEAD + P * i) for i, o in ((1, 0), (2, 208), (3, 544), (4, 1008))]
        sbias = region(M + 1600, PAST + HEAD)
        ebias = region(M + 1936, 2, PAST + HEAD)
        sc, wk, gt, eq, cum = [region(M + 2608 + 512 * n, 512) for n in range(5)]
        rel = [region(M + 2608 + 2560 + 512 * n, 512) for n in range(2)]
        qs = region(M + 6192, NS, 4, QS)
        qm = region(M + 6448, 4, META)
        iqpad = region(B + 3 * NS * PAST, 2, NS, SAMP)
        scs = region(B + 3 * NS * PAST + 2 * NS * SAMP, 512)
        best = sb("best", [P, 8])
        cnt = sb("cnt", [P, 2])
        SEL = [(t, ROWS[t], P * t) for t in range(1, NT)] + [(0, SAMP, PAST + SAMP)]

        def pool_sample_queries():
            nc.gpsimd.wait_ge(sg("roped"), len(ROPED))
            nc.gpsimd.wait_ge(w_used, U_EVEN)
            plink(nc.gpsimd.memset(iqpad, 0.0))
            for s in range(NS):
                c = slice(QS * s, QS * (s + 1))
                ins = nc.gpsimd.tensor_copy(iqpad[:, :, s, c], proj[:, IQ0:IQ0 + 2, c])
            ins.then_inc(sg("sq_ready"), 1)
            nc.gpsimd.tensor_copy(qs.rearrange("p s h q -> p h s q"),
                                  proj[:, AQ0:AQ0 + 4, 0:SAMP].rearrange("p h (s q) -> p h s q", s=NS))\
                .then_inc(sg("sq_ready"), 1)
            nc.gpsimd.tensor_copy(qm, proj[:, AQ0:AQ0 + 4, SAMP:HEAD]).then_inc(sg("sq_ready"), 1)

        SCORE_AT = {5: 0, 8: 1, 13: 2, 20: 3}

        def idx_bank(n):
            if n >= IDX_HEADS * (NT - 1):
                return 7
            return 6 + n % 2 if n < IDX_HEADS else 4 + n % 4

        def pe_scores(i):
            t, R, W = SEL[i]
            nc.tensor.wait_ge(sg("roped"), len(ROPED) if i else ROPED.index(IQ0 + 1) + 1)
            for hd in range(IDX_HEADS):
                n = IDX_HEADS * i + hd
                b = HD * (hd % 2)
                if i:
                    nc.tensor.wait_ge(sg("idx_rel"), n - 3)
                elif n >= 2:
                    nc.tensor.wait_ge(sg("idx_rel"), n - 1)
                nc.tensor.matmul(ps[:, idx_bank(n), 0:W], proj[b:b + HD, IQ0 + hd // 2, COL0[t]:COL0[t] + R],
                                 proj[b:b + HD, IK0, HEAD:HEAD + W], start=True, stop=True).then_inc(sg("idx_mm"), 1)

        def pe_sample_scores(hd):
            b = HD * (hd % 2)
            if hd == 0:
                nc.tensor.wait_ge(sg("pages_in"), 16 * NS * NPG)
                nc.tensor.wait_ge(sg("sq_ready"), 3)
                nc.tensor.wait_ge(sg("mix_a"), 1)
            else:
                nc.tensor.wait_ge(sg("idx_rel"), IDX_HEADS * (NT - 1) + hd)
            for s in range(NS):
                nc.tensor.matmul(ps[0:SAMP, 7, 0:PAST], iqpad[b:b + HD, hd // 2, s, :], pages[b:b + HD, s, :, 1, :],
                                 start=(s == 0), stop=(s == NS - 1))
            nc.tensor.matmul(ps[0:SAMP, 7, PAST:PAST + SAMP], proj[b:b + HD, IQ0 + hd // 2, 0:SAMP],
                             proj[b:b + HD, IK0, 0:SAMP], start=True, stop=True).then_inc(sg("idx_mm"), 1)

        def act_scores(i, heads_=range(IDX_HEADS)):
            t, R, W = SEL[i]
            for hd in heads_:
                n = IDX_HEADS * i + hd
                nc.scalar.wait_ge(sg("idx_mm"), n + 1)
                if n >= 2:
                    nc.scalar.wait_ge(sg("idx_acc"), n - 1)
                nc.scalar.activation(rel[n % 2][0:R, 0:W], ps[0:R, idx_bank(n), 0:W], ACT.Relu)\
                    .then_inc(sg("idx_rel"), 1)

        def dve_scores(i, link, heads_=range(IDX_HEADS)):
            t, R, W = SEL[i]
            v = slice(0, R)
            sc_ = (sc if t else scs)[v, 0:W]
            for hd in heads_:
                n = IDX_HEADS * i + hd
                nc.vector.wait_ge(sg("idx_rel"), n + 1)
                wv = G(G_IW)[v, t, hd:hd + 1]
                if hd == 0:
                    link(nc.vector.tensor_scalar(sc_, rel[n % 2][v, 0:W], wv, None, ALU.mult), "idx_acc")
                else:
                    link(nc.vector.scalar_tensor_tensor(out=sc_, in0=rel[n % 2][v, 0:W], scalar=wv, in1=sc_,
                                                        op0=ALU.mult, op1=ALU.add), "idx_acc")

        def dve_choose(i, link):
            t, R, W = SEL[i]
            v = slice(0, R)
            last = slice(W - P, W) if t else slice(PAST, PAST + SAMP)
            hide = C("causal") if t else C("newb")[v]
            src = sc if t else scs
            link(nc.vector.tensor_tensor(src[v, last], src[v, last], hide, ALU.add))
            a, K = (0, K_PROMPT) if t else (META, K_SAMPLE)
            s_, k_, g_, e_, c_ = (u[v, a:W] for u in (src, wk, gt, eq, cum))
            link(nc.vector.max(best[v, :], s_))
            yield
            for r in range(1, -(-K // 8)):
                link(nc.vector.match_replace(out=k_, in_to_replace=best[v, :], in_values=s_ if r == 1 else k_,
                                             imm_value=NEG))
                link(nc.vector.max(best[v, :], k_))
                yield
            thr = best[v, (K - 1) % 8:(K - 1) % 8 + 1]
            link(nc.vector.tensor_scalar(g_, s_, thr, 0.0, ALU.is_gt, ALU.add, accum_out=cnt[v, 0:1]))
            link(nc.vector.tensor_scalar(e_, s_, thr, None, ALU.is_equal))
            yield
            link(nc.vector.tensor_scalar(cnt[v, 1:2], cnt[v, 0:1], -1.0, float(K), ALU.mult, ALU.add))
            link(nc.vector.tensor_tensor_scan(c_, C("one")[v].to_broadcast([R, W - a]), e_, 0.0,
                                              ALU.mult, ALU.add))
            yield
            link(nc.vector.scalar_tensor_tensor(out=c_, in0=c_, scalar=cnt[v, 1:2], in1=e_,
                                                op0=ALU.is_le, op1=ALU.mult))
            link(nc.vector.tensor_tensor(g_, g_, c_, ALU.add))
            yield
            if t:
                out_ = bias[t]
                nc.vector.memset(out_[:, 0:SAMP], NEG)
                nc.vector.memset(out_[:, SAMP:HEAD], 0.0)
                link(nc.vector.tensor_scalar(out_[:, HEAD:HEAD + W], g_, -1.0, -NEG, ALU.add, ALU.mult))
                d = out_[:, HEAD + W - P:HEAD + W]
                link(nc.vector.tensor_tensor(d, d, C("causal"), ALU.min), "chosen")
            else:
                nc.vector.memset(sbias[v, 0:META], 0.0)
                nc.vector.memset(sbias[v, PAST + SAMP:PAST + HEAD], NEG)
                link(nc.vector.tensor_scalar(sbias[v, META:W], g_, -1.0, -NEG, ALU.add, ALU.mult))
                d = sbias[v, PAST:PAST + SAMP]
                link(nc.vector.tensor_tensor(d, d, C("newb")[v], ALU.min), "chosen")

        def pe_expand(a):
            nc.tensor.wait_ge(sg("chosen"), NT)
            nc.tensor.wait_ge(sg("mix_a"), NT - 2)
            if a:
                nc.tensor.wait_ge(sg("expanded"), 1)
            nc.tensor.matmul(ps[:, 7, 0:PAST + HEAD], C("expand")[0:SAMP, P * a:P * (a + 1)], sbias[0:SAMP, :],
                             start=True, stop=True).then_inc(sg("ex_mm"), 1)

        def dve_expand(a, link):
            nc.vector.wait_ge(sg("ex_mm"), a + 1)
            link(nc.vector.tensor_copy(ebias[:, a, :], ps[:, 7, 0:PAST + HEAD]), "expanded")

        ITEMS = [("p", t, hd) for t in range(1, NT) for hd in range(A_HEADS)]
        ITEMS += [("s", g, a) for g in range(KVH) for a in range(2)] + [("m", 0, 0)]
        lm = [ct2[:, e, :] for e in range(2)]
        pT = [xflat[:, 4 * T + 640 * e:4 * T + 640 * (e + 1)].rearrange("p (u c) -> p u c", u=5) for e in range(2)]
        on = xflat[:, 4 * T + 1280:4 * T + 1792]
        mx = sb("mx", [P, 2])
        rsum = sb("rsum", [P, 3, 8])

        def width(it):
            return {"p": HEAD + P * it[1], "s": PAST + HEAD, "m": HEAD}[it[0]]

        def logits(n):
            W, pr = width(ITEMS[n]), 2 * (n % 2)
            return ps[:, pr, 0:W] if W <= 512 else ps[:, pr:pr + 2, 0:W // 2]

        def as_logits(v):
            return v if v.shape[1] <= 512 else pairs(v)

        def key_tiles(it):
            if it[0] == "p":
                return [(ROWS[u], COL0[u]) for u in range(it[1] + 1)]
            if it[0] == "s":
                return [(P, 0), (P, P), (HEAD, PAST)]
            return [(HEAD, 0)]

        def pe_logits(n):
            it = ITEMS[n]
            W = width(it)
            if n >= 2:
                nc.tensor.wait_ge(sg("lg_max"), n - 1)
            if it[0] == "p":
                g, j = it[2] // 4, it[2] % 4
                q = proj[HD * g:HD * (g + 1), AQ0 + j, COL0[it[1]]:COL0[it[1]] + P]
                k = proj[HD * g:HD * (g + 1), AK0, :]
                if W <= 512:
                    mm = nc.tensor.matmul(ps[:, 2 * (n % 2), 0:W], q, k[:, 0:W], start=True, stop=True)
                else:
                    for e in range(2):
                        mm = nc.tensor.matmul(ps[:, 2 * (n % 2) + e, 0:W // 2], q, k[:, e * W // 2:(e + 1) * W // 2],
                                              start=True, stop=True)
            elif it[0] == "s":
                g, a = it[1:]
                b = slice(HD * g, HD * (g + 1))
                qa = qs[b, 4 * a:4 * a + 4].rearrange("p s h q -> p (s h q)")
                for s in range(4):
                    nc.tensor.matmul(ps[32 * s:32 * (s + 1), 2 * (n % 2), 0:PAST], qa[:, 32 * s:32 * (s + 1)],
                                     pages[b, 4 * a + s, :, 0, :], start=True, stop=True)
                mm = nc.tensor.matmul(ps[:, 2 * (n % 2), PAST:PAST + HEAD], qa, proj[b, AK0, 0:HEAD],
                                      start=True, stop=True)
            else:
                for g in range(KVH):
                    b = slice(HD * g, HD * (g + 1))
                    mm = nc.tensor.matmul(ps[b, 2 * (n % 2), 0:HEAD], qm[b].rearrange("p h q -> p (h q)"),
                                          proj[b, AK0, 0:HEAD], start=True, stop=True)
            mm.then_inc(sg("lg_mm"), 1)

        def turned(it, u):
            if it[0] == "p":
                return (5, P * (u // 4)) if u % 4 == 0 else (4, P * (u - 1))
            return (5, 0) if it[0] == "m" or u == 2 else (4, P * u)

        def pe_turn(n):
            it = ITEMS[n]
            nc.tensor.wait_ge(sg("pr_exp"), n + 1)
            if n:
                nc.tensor.wait_ge(sg("pr_ev_a"), n)
                nc.tensor.wait_ge(sg("pr_ev_d"), n)
            for u, (K, c) in enumerate(key_tiles(it)):
                tb, tc = turned(it, u)
                mm = nc.tensor.transpose(ps[0:K, tb, tc:tc + P], lm[n % 2][:, c:c + K], C("ident"))
            mm.then_inc(sg("pr_tr"), 1)

        def pe_values(n):
            it = ITEMS[n]
            tiles = key_tiles(it)
            nc.tensor.wait_ge(sg("pr_ev_a"), n + 1)
            nc.tensor.wait_ge(sg("pr_ev_d"), n + 1)
            if it[0] == "p":
                hd = it[2]
                if hd == 0 and it[1] > 1:
                    nc.tensor.wait_ge(sg("o_ev"), it[1] - 1)
                for u, (K, c) in enumerate(tiles):
                    mm = nc.tensor.matmul(ps[:, 6, HD * hd:HD * (hd + 1)], pT[n % 2][0:K, u, :],
                                          tokm[0:K, u, HD * (hd // 4):HD * (hd // 4 + 1)],
                                          start=(u == 0), stop=(u == len(tiles) - 1))
            else:
                nc.tensor.wait_ge(sg("o_ev"), NT - 1 + ITEMS_S.index(n))
                if it[0] == "s":
                    g, a = it[1:]
                    for s in range(4):
                        for u, (K, c) in enumerate(tiles):
                            vv = pages[:, 4 * a + s, u, 2, HD * g:HD * (g + 1)] if u < NPG else \
                                tokm[0:K, 0, HD * g:HD * (g + 1)]
                            mm = nc.tensor.matmul(ps[32 * s:32 * (s + 1), 6, 0:HD],
                                                  pT[n % 2][0:K, u, 32 * s:32 * (s + 1)], vv,
                                                  start=(u == 0), stop=(u == len(tiles) - 1))
                else:
                    for g in range(KVH):
                        mm = nc.tensor.matmul(ps[HD * g:HD * (g + 1), 6, 0:HD],
                                              pT[n % 2][0:HEAD, 0, HD * g:HD * (g + 1)],
                                              tokm[0:HEAD, 0, HD * g:HD * (g + 1)], start=True, stop=True)
            mm.then_inc(sg("o_mm"), 1)

        ITEMS_S = [n for n, it in enumerate(ITEMS) if it[0] != "p"]
        DONE = [n for n, it in enumerate(ITEMS) if it[0] != "p" or it[2] == A_HEADS - 1]

        def pe_o_turn(n):
            d = DONE.index(n)
            nc.tensor.wait_ge(sg("o_ev"), d + 1)
            if d == 1:
                nc.tensor.wait_ge(sg("idx_rel"), IDX_HEADS * NT)
            if d == NT - 2:
                nc.tensor.wait_ge(sg("expanded"), 2)
            if d:
                nc.tensor.wait_ge(sg("mix_a"), d)
            if ITEMS[n][0] == "p":
                for u in range(4):
                    mm = nc.tensor.transpose(ps[:, 7, P * u:P * (u + 1)], on[:, P * u:P * (u + 1)], C("ident"))
            else:
                mm = nc.tensor.transpose(ps[0:HD, 7, 0:P], on[:, 0:HD], C("ident"))
            mm.then_inc(sg("o_tr"), 1)

        SAMPLE_AT = [10, 11, 12, 13]
        EXPAND_AT = [28, 30]

        def pe_attention():
            nc.tensor.wait_ge(bank_free, U_EVEN + 2)
            nc.tensor.wait_ge(sg("l2_ln"), 8)
            pe_logits(0)
            for n in range(len(ITEMS) + 2):
                if n + 1 < len(ITEMS):
                    pe_logits(n + 1)
                if n < len(ITEMS):
                    pe_turn(n)
                if 1 <= n <= len(ITEMS):
                    pe_values(n - 1)
                if n - 2 in DONE:
                    pe_o_turn(n - 2)
                if n in SAMPLE_AT:
                    pe_sample_scores(SAMPLE_AT.index(n))
                if n in EXPAND_AT:
                    pe_expand(EXPAND_AT.index(n))

        def dve_attention(link, choice):
            for n in range(len(ITEMS) + 2):
                if n == SAMPLE_AT[-1] + 2:
                    for _ in choice:
                        pass
                    choice = dve_choose(NT - 1, link)
                if n == 0:
                    nc.vector.wait_ge(sg("l2_done"), 8)
                if n == EXPAND_AT[0]:
                    for _ in choice:
                        pass
                if n < len(ITEMS):
                    it = ITEMS[n]
                    W = width(it)
                    b = bias[it[1]] if it[0] == "p" else ebias[:, it[2], :] if it[0] == "s" else C("metab")
                    nc.vector.wait_ge(sg("lg_mm"), n + 1)
                    if n >= 2:
                        nc.vector.wait_ge(sg("pr_tr"), n - 1)
                    link(nc.vector.tensor_tensor_reduce(
                        out=as_logits(lm[n % 2][:, 0:W]), in0=logits(n), in1=as_logits(b[:, 0:W]), scale=1.0,
                        scalar=NEG, op0=ALU.add, op1=ALU.max, accum_out=mx[:, n % 2:n % 2 + 1]))
                    link(nc.vector.tensor_scalar(mx[:, n % 2:n % 2 + 1], mx[:, n % 2:n % 2 + 1], -HD ** -0.5, None,
                                                 ALU.mult), "lg_max")
                if 1 <= n <= len(ITEMS):
                    m = n - 1
                    it = ITEMS[m]
                    nc.vector.wait_ge(sg("pr_tr"), m + 1)
                    if m >= 2:
                        nc.vector.wait_ge(sg("o_mm"), m - 1)
                    u = 2 if it[0] == "s" else 0
                    ins = nc.vector.tensor_copy(pT[m % 2][0:HEAD, u, :], ps[0:HEAD, 5, 0:P])
                    if it[0] == "p" and it[1] == 4:
                        ins = nc.vector.tensor_copy(pT[m % 2][:, 4, :], ps[:, 5, P:2 * P])
                    ins.then_inc(sg("pr_ev_d"), 1)
                if n - 1 in SAMPLE_AT:
                    dve_scores(NT - 1, link, [SAMPLE_AT.index(n - 1)])
                if n - 1 in EXPAND_AT:
                    dve_expand(EXPAND_AT.index(n - 1), link)
                if n < EXPAND_AT[0]:
                    next(choice, None)
                if n - 2 in DONE:
                    m = n - 2
                    it, d = ITEMS[m], DONE.index(m)
                    nc.vector.wait_ge(sg("o_mm"), m + 1)
                    if d:
                        nc.vector.wait_ge(sg("o_tr"), d)
                    if it[0] == "p":
                        rs = rsum[:, it[1] % 2, :]
                        link(nc.vector.reciprocal(rs, rs))
                        link(nc.vector.tensor_tensor(on.rearrange("p (h c) -> p h c", h=8),
                                                     ps[:, 6, :].rearrange("p (h c) -> p h c", h=8),
                                                     rs.rearrange("p (h o) -> p h o", o=1)
                                                     .to_broadcast([P, 8, HD]), ALU.mult), "o_ev")
                    else:
                        rs = rsum[:, 2, m - len(ITEMS) + 5:m - len(ITEMS) + 6]
                        link(nc.vector.reciprocal(rs, rs))
                        link(nc.vector.tensor_scalar(on[:, 0:HD], ps[:, 6, 0:HD], rs, None, ALU.mult), "o_ev")

        def act_attention():
            for n in range(len(ITEMS) + 2):
                if n < len(ITEMS):
                    it = ITEMS[n]
                    nc.scalar.wait_ge(sg("lg_max"), n + 1)
                    if it[0] == "p":
                        rs = rsum[:, it[1] % 2, it[2]:it[2] + 1]
                        if it[2] == 0 and it[1] >= 3:
                            nc.scalar.wait_ge(sg("o_ev"), it[1] - 2)
                    else:
                        rs = rsum[:, 2, n - len(ITEMS) + 5:n - len(ITEMS) + 6]
                    p = lm[n % 2][:, 0:width(it)]
                    nc.scalar.activation(p, p, ACT.Exp, scale=HD ** -0.5, bias=mx[:, n % 2:n % 2 + 1], accum_out=rs)\
                        .then_inc(sg("pr_exp"), 1)
                if 1 <= n <= len(ITEMS):
                    m = n - 1
                    it = ITEMS[m]
                    nc.scalar.wait_ge(sg("pr_tr"), m + 1)
                    if m >= 2:
                        nc.scalar.wait_ge(sg("o_mm"), m - 1)
                    if it[0] == "m":
                        nc.scalar.sem_inc(sg("pr_ev_a"), 1)
                    else:
                        u, N = (1, min(it[1], 3)) if it[0] == "p" else (0, 2)
                        nc.scalar.activation(pT[m % 2][:, u:u + N, :].rearrange("p u c -> p (u c)"),
                                             ps[:, 4, 0:P * N], ACT.Copy).then_inc(sg("pr_ev_a"), 1)
                if n - 1 in SAMPLE_AT:
                    act_scores(NT - 1, [SAMPLE_AT.index(n - 1)])
                if n - 2 in DONE:
                    it, d = ITEMS[n - 2], DONE.index(n - 2)
                    nc.scalar.wait_ge(sg("o_tr"), d + 1)
                    if it[0] == "p":
                        nc.scalar.activation(xn[:, 0:4, COL0[it[1]]:COL0[it[1]] + P],
                                             ps[:, 7, :].rearrange("p (u c) -> p u c", u=4), ACT.Copy)\
                            .then_inc(sg("mix_a"), 1)
                        continue
                    for e in range(2):
                        if it[0] == "s":
                            g, a = it[1:]
                            src = ps[0:HD, 7, 0:P].rearrange("p (s h q) -> p h s q", s=4, h=4)[:, e::2]
                            dst = xn[HD * e:HD * (e + 1), 2 * g:2 * g + 2, 32 * a:32 * (a + 1)]\
                                .rearrange("p h (s q) -> p h s q", s=4)
                        else:
                            src = ps[0:HD, 7, 0:P].rearrange("p (h q) -> p h q", h=8)[:, e::2]
                            dst = xn[HD * e:HD * (e + 1), 0:4, SAMP:HEAD]
                        ins = nc.scalar.activation(dst, src, ACT.Copy)
                    ins.then_inc(sg("mix_a"), 1)

        def pe_even():
            for u in range(U_EVEN):
                pe_unit(Units.even, U_EVEN, 0, u, X_SPLIT, x_tiles(0) if u == 0 else None)
                if u == 1:
                    pe_small()
                    nc.tensor.wait_ge(sg("small_ev"), NT)
                if 1 <= u <= len(ROPED):
                    pe_rope(u - 1)
                if u in SCORE_AT:
                    pe_scores(SCORE_AT[u])
                if u >= L2_AT:
                    pe_l2(u - L2_AT)
            for pair in (2, 3):
                pe_l2(pair)

        def act_even():
            for u in range(U_EVEN):
                if u + 2 < U_EVEN:
                    act_w_hi(Units.even, U_EVEN, 0, u + 2)
                m = EVEN_TILES[u]
                act_evacuate(Units.even, 0, u, proj[:, m, :], ACT.Copy)
                if u == 2:
                    act_small()
                if 0 <= u - CONV_AT < 12:
                    act_tap(u - CONV_AT)
                if 0 <= u - CONV_AT - 1 < 12:
                    act_silu(u - CONV_AT - 1)
                if u == CONV_AT + 12:
                    nc.scalar.preload_act_table_set("natural_log_exp_and_others")
                if u in SCORE_AT:
                    act_scores(SCORE_AT[u])
                if u >= L2_AT:
                    act_l2_roots(u - L2_AT)
                if u >= L2_AT - 1:
                    act_l2_squares(u - L2_AT + 1)
            act_l2_roots(2)
            act_l2_squares(3)
            act_l2_roots(3)

        L2_AT = 22
        ROUNDS = [0, 0, 0, 0, 0, 4, 7, 7, 2, 4, 4, 4, 4, 1, 3, 3, 3, 3, 3, 3, 2, 4, 4, 4]

        def dve_even(link):
            choice = iter(())
            for u in range(U_EVEN):
                if u + 2 < U_EVEN:
                    dve_w_lo(Units.even, U_EVEN, 0, u + 2)
                if u == 1:
                    dve_small(link)
                if u == 2:
                    dve_decay(link)
                if 1 <= u <= len(ROPED):
                    dve_rope(u - 1, link)
                if 0 <= u - CONV_AT < 12:
                    dve_conv(u - CONV_AT, link)
                if u in SCORE_AT:
                    for _ in choice:
                        pass
                    dve_scores(SCORE_AT[u], link)
                    choice = dve_choose(SCORE_AT[u], link)
                for _ in range(ROUNDS[u]):
                    next(choice, None)
                if u >= L2_AT:
                    for n in (2 * (u - L2_AT), 2 * (u - L2_AT) + 1):
                        dve_l2(n)
            for n in range(4, 8):
                next(choice, None)
                dve_l2(n)
            return choice

        v5 = region(M, NT, HGH * P)
        kkall = region(M + NT * HGH * P, HGH, T)
        EARLY = (B - M - NT * HGH * P) // T
        HB = M + NT * HGH * P + HGH * T
        at5 = [region(HB + NT * P * e, NT, P) for e in range(2)]
        kd5 = region(HB + 2 * NT * P, NT, P)
        hsp = region(HB + 3 * NT * P, SEQ // HC, P)
        HC0 = HB + 3 * NT * P + SEQ // HC * P
        hmask = region(HC0, NSEG, P)
        hst = [region(HC0 + NSEG * P + NS * P * e, NS, P) for e in range(2)]
        qe = region(HC0 + NSEG * P + 2 * NS * P, T)
        xt = [xn[:, k, :] for k in range(KT)]
        cb, dd, ee, kdT = (xt[0], xt[1]), (xt[2], xt[3]), (xt[4], xt[5]), (xt[6], xt[7])
        xe = [sq[:, 0, :], sq[:, 1, :]]
        hp_fin = spb[:, 0:HGH * P].rearrange("p (h c) -> p h c", h=HGH)
        oT5 = region(0, HGH, T)
        ecl = sb("ecl", [P, 2, NSEG + SEQ // HC])
        FROM = [0, 0, 0, SAMP, HEAD, HEAD]

        def v_bank(a, t):
            return (NT * a + t) % 8

        def pe_values5():
            for j in range(VUNITS):
                a, q = j // 4, j % 4
                nc.tensor.wait_ge(w_lo, Units.values + j + 1)
                nc.tensor.wait_ge(bank_free, Units.values + 2)
                wh, wl = wsp[:, j % 2, 0, :], wsp[:, j % 2, 1, :]
                for t in range(NT):
                    if a and q == 0 and v_bank(a, t) < NT:
                        nc.tensor.wait_ge(sg("v_out"), v_bank(a, t) + 1)
                    c = slice(COL0[t], COL0[t] + ROWS[t])
                    for k in range(2):
                        for x, w_ in ((x_hi, wh), (x_hi, wl), (x_lo, wh)):
                            mm = nc.tensor.matmul(ps[0:ROWS[t], v_bank(a, t), :], x[:, 2 * q + k, c],
                                                  w_[:, 512 * k:512 * (k + 1)],
                                                  start=(q == 0 and k == 0 and x is x_hi and w_ is wh),
                                                  stop=(q == 3 and k == 1 and x is x_lo))
                mm.then_inc(w_used, 1)

        def act_values5():
            for j in range(VUNITS):
                if j < VUNITS - 2:
                    act_w_hi(Units.values, VUNITS, 0, j + 2)
                if j == 0:
                    nc.scalar.wait_ge(bank_free, Units.values + 2)
                    nc.scalar.wait_ge(sg("lb_diff"), 1)
                    nc.scalar.activation(lbv[:, :, :], lbv[:, :, :], ACT.Sigmoid).then_inc(sg("lb"), 1)
                if j < EARLY:
                    act_sigmoids(j)
                if j == 4:
                    nc.scalar.preload_act_table_set("natural_log_exp_and_others")
                    act_front_ln(0)
                if j == VUNITS - 1:
                    nc.scalar.wait_ge(w_used, Units.values + 7)
                    act_decay(dec_no(0, -1), 0)
                    act_decay(dec_no(0, 0), 0)
                a, q = j // 4, j % 4
                if q == 3:
                    nc.scalar.wait_ge(w_used, Units.values + j + 1)
                    for t in range(NT):
                        nc.scalar.activation(v5[0:ROWS[t], t, 512 * a:512 * (a + 1)], ps[0:ROWS[t], v_bank(a, t), :],
                                             ACT.Copy).then_inc(sg("v_out"), 1)

        def lower_bounds():
            dlink(nc.vector.tensor_tensor(lbv[:, 0, :], vec[:, V_LB1:V_LB1 + 8], vec[:, V_LB0:V_LB0 + 8],
                                          ALU.subtract))
            dlink(nc.vector.tensor_scalar(lbv[:, 1, :], lbv[:, 0, :], -1.0, None, ALU.mult), "lb_diff")

        def blocks(v, l):
            b = 1 << l
            return v[:, FROM[l]:T].rearrange("p (n o b) -> p n o b", o=2, b=b)

        NL = HLEVELS + 1

        def ends(v):
            out = []
            for a, n, c in ((0, NS, QS), (SAMP, 1, META), (HEAD, SEQ // HC, HC)):
                w_ = v[:, a:a + n * c].rearrange("p (n c) -> p n c", c=c)
                out.append((w_, w_[:, :, c - 1:c]))
            return out

        PERIODS = range(HGH + 2)

        def dec_no(hd, l):
            return NL * hd + 1 + l

        def act_hgrn():
            nc.scalar.wait_ge(sg("v_out"), 2 * NT)
            for hd in PERIODS:
                for l in range(NL):
                    if hd == 0 and l == HLEVELS - 1:
                        for late in range(EARLY, HGH):
                            act_sigmoids(late)
                        nc.scalar.preload_act_table_set("natural_log_exp_and_others")
                    if hd < HGH and l < HLEVELS - 1:
                        act_decay(dec_no(hd, l + 1), FROM[l + 1])
                    if hd + 1 < HGH and l >= HLEVELS - 1:
                        act_decay(dec_no(hd + 1, l - HLEVELS), 0)
                    if l == 0 and 0 <= hd - 2:
                        act_hgrn_out(hd - 2)
                    if 0 <= hd - 1 < HGH:
                        act_hgrn_post(hd - 1, l)
                    if l == 1 and 0 <= hd - 2:
                        nc.scalar.wait_ge(sg("go_mm"), hd - 1)
                        act_root(rn[:, :], ps[:, 6:8, 0:HALF], 1.0 / P, C("eps"), "go_ln", "go_rt")
                    if l == 2 and hd + 1 < HGH:
                        act_front_ln(hd + 1)
                    if l == 5 and hd < HGH:
                        if hd:
                            nc.scalar.wait_ge(sg("hg_done"), hd)
                        nc.scalar.activation(qe, cb[hd % 2], ACT.Exp).then_inc(sg("hg_qe"), 1)

        def act_sigmoids(hd):
            nc.scalar.activation(kkall[:, hd], proj[:, hd, :], ACT.Sigmoid, scale=-1.0).then_inc(sg("hg_sig"), 1)
            nc.scalar.activation(proj[:, hd, :], proj[:, hd, :], ACT.Sigmoid).then_inc(sg("hg_sig"), 1)

        def act_front_ln(hd):
            nc.scalar.wait_ge(sg("hg_f"), hd + 1)
            nc.scalar.activation(proj[:, hd, :], proj[:, hd, :], ACT.Ln).then_inc(sg("hg_ln"), 1)

        def act_decay(i, a):
            nc.scalar.wait_ge(sg("hg_dif"), i + 1)
            if i >= 2:
                nc.scalar.wait_ge(sg("hg_mul"), i - 1)
            nc.scalar.activation(ee[i % 2][:, a:T], dd[i % 2][:, a:T], ACT.Exp).then_inc(sg("hg_exp"), 1)

        def act_hgrn_post(hd, l):
            if l == 0:
                nc.scalar.wait_ge(sg("hg_kt"), hd + 1)
                if hd:
                    nc.scalar.wait_ge(sg("hp_kv"), hd)
                nc.scalar.activation(kd5[:, 1:NT, :], ps[:, 4, :].rearrange("p (t c) -> p t c", t=4), ACT.Copy)
                nc.scalar.activation(kd5[0:HEAD, 0, :], ps[0:HEAD, 5, 0:P], ACT.Copy).then_inc(sg("hg_kdt"), 1)
            if l == 2:
                nc.scalar.wait_ge(sg("hs_o"), hd + 1)
                nc.scalar.activation(oT5[:, hd, 0:HEAD], ps[:, 5, 0:HEAD], ACT.Copy).then_inc(sg("hs_ob"), 1)

        def act_hgrn_out(hd):
            nc.scalar.wait_ge(sg("hp_o"), hd + 1)
            nc.scalar.activation(oT5[:, hd, HEAD:T].rearrange("p (n o c) -> p o n c", o=2, c=HC),
                                 ps[:, 4:6, 0:SEQ // 2].rearrange("p o (n c) -> p o n c", c=HC), ACT.Copy)\
                .then_inc(sg("hp_ob"), 1)
            nc.scalar.wait_ge(sg("hp_ob"), hd + 1)
            if hd:
                nc.scalar.wait_ge(sg("go_x"), hd)
            nc.scalar.activation(rn[:, :], oT5[:, hd, :], ACT.Square).then_inc(sg("go_sq"), 1)

        def pool_hgrn():
            nc.gpsimd.wait_ge(w_used, Units.values + 6)
            pool_dif_end(0)
            for hd in range(HGH):
                for l in range(HLEVELS):
                    if hd == 0 and l == 1:
                        nc.gpsimd.wait_ge(sg("v_out"), 2 * NT)
                        for e in range(2):
                            nc.gpsimd.memset(at5[e], 0.0).then_inc(sg("hg_zero"), 1)
                    i = dec_no(hd, l)
                    nc.gpsimd.wait_ge(sg("hg_exp"), i - 1)
                    b = 1 << l
                    c_, d_ = blocks(cb[hd % 2], l), blocks(dd[i % 2], l)
                    mid = c_[:, :, 0, b - 1:b].to_broadcast([P, c_.shape[1], b])
                    nc.gpsimd.tensor_tensor(d_[:, :, 0, :], mid, c_[:, :, 0, :], ALU.subtract)
                    nc.gpsimd.tensor_tensor(d_[:, :, 1, :], c_[:, :, 1, :], mid, ALU.subtract)\
                        .then_inc(sg("hg_dif"), 1)
                if hd + 1 < HGH:
                    pool_dif_end(hd + 1)
                if hd:
                    nc.gpsimd.wait_ge(sg("hs_kv"), hd)
                nc.gpsimd.tensor_tensor(hmask[0:HEAD], v5[0:HEAD, 0:1, P * hd:P * (hd + 1)]
                                        .to_broadcast([HEAD, NSEG, P]),
                                        C("seg")[0:HEAD, :].rearrange("p (s o) -> p s o", o=1)
                                        .to_broadcast([HEAD, NSEG, P]), ALU.mult).then_inc(sg("hs_vm"), 1)

        def pool_dif_end(hd):
            i = dec_no(hd, -1)
            nc.gpsimd.wait_ge(sg("hg_cb"), hd + 1)
            if i >= 2:
                nc.gpsimd.wait_ge(sg("hg_exp"), i - 1)
            for (w_, l_), (o_, _) in zip(ends(cb[hd % 2]), ends(dd[i % 2])):
                ins = nc.gpsimd.tensor_tensor(o_, l_.to_broadcast(list(w_.shape)), w_, ALU.subtract)
            ins.then_inc(sg("hg_dif"), 1)

        def dve_front_f(hd):
            nc.vector.wait_ge(sg("hg_sig"), 2 * hd + 2)
            nc.vector.tensor_scalar(kkall[:, hd], kkall[:, hd], lbv[:, 1, hd:hd + 1], None, ALU.mult)
            nc.vector.tensor_scalar(proj[:, hd, :], proj[:, hd, :], lbv[:, 1, hd:hd + 1], lbv[:, 0, hd:hd + 1],
                                    ALU.mult, ALU.add).then_inc(sg("hg_f"), 1)

        def dve_front_scan(hd):
            nc.vector.wait_ge(sg("hg_ln"), hd + 1)
            if hd >= 2:
                nc.vector.wait_ge(sg("hg_qe"), hd - 1)
                nc.vector.wait_ge(sg("hg_dif"), NL * (hd - 1))
            nc.vector.tensor_tensor_scan(cb[hd % 2], C("sin"), proj[:, hd, :], 0.0, ALU.mult, ALU.add)\
                .then_inc(sg("hg_cb"), 1)

        def dve_front_kd(hd):
            i = dec_no(hd, -1)
            nc.vector.wait_ge(sg("hg_exp"), i + 1)
            nc.vector.wait_ge(sg("hg_f"), hd + 1)
            if hd >= 2:
                nc.vector.wait_ge(sg("hg_kt"), hd - 1)
            nc.vector.tensor_tensor(kdT[hd % 2], kkall[:, hd], ee[i % 2], ALU.mult).then_inc(sg("hg_mul"), 1)

        def dve_level(hd, l):
            n, i = NL * hd + l, dec_no(hd, l)
            nc.vector.wait_ge(sg("hg_exp"), i + 1)
            if n >= 2:
                nc.vector.wait_ge(sg("hg_g"), xe_reader(hd, l))
            e_, x_ = blocks(ee[i % 2], l), blocks(xe[l % 2], l)
            nc.vector.tensor_tensor(x_[:, :, 0, :], blocks(kkall[:, hd], l)[:, :, 0, :], e_[:, :, 0, :], ALU.mult)
            nc.vector.tensor_tensor(x_[:, :, 1, :], blocks(proj[:, 8 + hd, :], l)[:, :, 1, :], e_[:, :, 1, :],
                                    ALU.mult).then_inc(sg("hg_mul"), 1)

        def dve_hgrn(link):
            nc.vector.wait_ge(sg("state_out"), 32)
            nc.vector.wait_ge(w_used, Units.values + VUNITS)
            dve_front_kd(0)
            dve_level(0, 0)
            nc.vector.wait_ge(sg("v_out"), 2 * NT)
            nc.vector.wait_ge(sg("hg_zero"), 2)
            for hd in PERIODS:
                for l in range(NL):
                    if hd < HGH and l < HLEVELS - 1:
                        dve_level(hd, l + 1)
                    if hd + 1 < HGH and l == HLEVELS - 1:
                        dve_front_kd(hd + 1)
                    if hd + 1 < HGH and l == HLEVELS:
                        dve_level(hd + 1, 0)
                    p_, g_ = hd - 1, hd - 2
                    post = 0 <= p_ < HGH
                    if l == 3 and post:
                        nc.vector.wait_ge(sg("hs_m"), p_ + 1)
                        if hd < HGH:
                            nc.vector.wait_ge(sg("hg_g"), NL * hd + 3)
                        link(nc.vector.tensor_copy(hsp[:, 0, :], ps[:, meta_bank(p_), P:2 * P]), "hs_m0")
                    if l == 0 and post:
                        take(p_, HLEVELS)
                        nc.vector.wait_ge(sg("hg_qe"), p_ + 1)
                        q = proj[:, 8 + p_, :]
                        nc.vector.tensor_tensor(q, q, qe, ALU.mult)
                        a = 0
                        for _, l_ in ends(qe):
                            n = l_.shape[1]
                            ins = nc.vector.tensor_copy(ecl[:, p_ % 2, a:a + n].rearrange("p (n o) -> p n o", o=1), l_)
                            a += n
                        link(ins, "hg_done")
                    if l and hd < HGH:
                        take(hd, l - 1)
                    if l == 1 and hd + 1 < HGH:
                        dve_front_f(hd + 1)
                    if l == 3 and hd + 1 < HGH:
                        dve_front_scan(hd + 1)
                    if l == 2 and 0 <= g_:
                        o = oT5[:, g_, :]
                        nc.vector.wait_ge(sg("go_rt"), g_ + 1)
                        link(nc.vector.scalar_tensor_tensor(out=o, in0=o, scalar=vec[:, V_HGN:V_HGN + 1],
                                                            in1=rn[:, :], op0=ALU.mult, op1=ALU.mult), "go_x")
                        nc.vector.tensor_tensor(o, o, proj[:, 16 + g_, :], ALU.mult).then_inc(sg("go_out"), 1)
                    if l == 3 and post:
                        nc.vector.wait_ge(sg("hs_kv"), p_ + 1)
                        for s in range(NS):
                            st_ = hst[p_ % 2][:, s, :]
                            ins = nc.vector.scalar_tensor_tensor(out=st_, in0=st_, scalar=ecl[:, p_ % 2, s:s + 1],
                                                                 in1=ps[:, 6 + s // 4, P * (s % 4):P * (s % 4 + 1)],
                                                                 op0=ALU.mult, op1=ALU.add)
                        ins.then_inc(sg("hs_s"), 1)
                    if l == 5 and post:
                        nc.vector.wait_ge(sg("hp_kv"), p_ + 1)
                        for c in range(SEQ // HC):
                            dst = hsp[:, c + 1, :] if c + 1 < SEQ // HC else hp_fin[:, p_, :]
                            link(nc.vector.scalar_tensor_tensor(
                                out=dst, in0=hsp[:, c, :], scalar=ecl[:, p_ % 2, NSEG + c:NSEG + c + 1],
                                in1=ps[:, 6 + c % 2, P * (c // 2):P * (c // 2 + 1)], op0=ALU.mult, op1=ALU.add), "hp_s")

        def xe_reader(hd, l):
            return NL * hd + l - 1 if l >= 2 else NL * (hd - 1) + HLEVELS - 1 + (l % 2)

        def take(hd, l):
            n = NL * hd + l
            m = C("ident" if l == HLEVELS else f"lev{l}").bitcast(I32)
            nc.vector.wait_ge(sg("hg_g"), n + 1)
            if hd >= 2 and l == 0:
                nc.vector.wait_ge(sg("hp_o"), hd - 1)
            b = 2 * (n % 2)
            a_ = at5[hd % 2]
            ins = nc.vector.copy_predicated(a_[:, 1:NT, :], m.rearrange("p (o c) -> p o c", o=1)
                                            .to_broadcast([P, 4, P]),
                                            ps[:, b, :].rearrange("p (t c) -> p t c", t=4))
            r = slice(0, HEAD) if l < 3 or l == HLEVELS else slice(SAMP, HEAD)
            if l <= 3 or l == HLEVELS:
                ins = nc.vector.copy_predicated(a_[r, 0, r], m[r, r], ps[r, b + 1, r])
            dlink(ins, "hg_take")

        def meta_bank(hd):
            return 2 * ((NL * (hd + 1) + 2) % 2) + 1

        def pe_level(hd, l):
            n = NL * hd + l
            if n >= 2:
                nc.tensor.wait_ge(sg("hg_take"), n - 1)
            if l == HLEVELS:
                nc.tensor.wait_ge(sg("hg_f"), hd + 1)
            else:
                nc.tensor.wait_ge(sg("hg_mul"), dec_no(hd, l) + 1)
            b = 2 * (n % 2)
            x_ = xe[l % 2]
            for t in range(NT):
                c = slice(COL0[t], COL0[t] + ROWS[t])
                o = ps[0:HEAD, b + 1, 0:HEAD] if t == 0 else ps[:, b, P * (t - 1):P * t]
                if l == HLEVELS:
                    mm = nc.tensor.matmul(o, kkall[:, hd, c], proj[:, 8 + hd, c], start=True, stop=True)
                elif t or l < 3:
                    mm = nc.tensor.matmul(o, x_[:, c], x_[:, c], start=True, stop=True)
                elif l == 3:
                    c = slice(SAMP, HEAD)
                    mm = nc.tensor.matmul(ps[c, b + 1, c], x_[:, c], x_[:, c], start=True, stop=True)
            mm.then_inc(sg("hg_g"), 1)

        def pe_hgrn():
            for hd in PERIODS:
                for l in range(NL):
                    p_ = hd - 1
                    post = 0 <= p_ < HGH
                    if l == 2 and post:
                        nc.tensor.wait_ge(sg("hg_kdt"), p_ + 1)
                        nc.tensor.wait_ge(sg("hs_vm"), p_ + 1)
                        nc.tensor.wait_ge(sg("hg_take"), min(NL * hd + 1, NL * HGH))
                        nc.tensor.matmul(ps[:, meta_bank(p_), P:2 * P], kd5[0:HEAD, 0, :], hmask[0:HEAD, NS, :],
                                         start=True, stop=True).then_inc(sg("hs_m"), 1)
                    if hd < HGH:
                        pe_level(hd, l)
                    if l == 0 and 0 <= hd - 2:
                        nc.tensor.wait_ge(sg("go_sq"), hd - 1)
                        nc.tensor.wait_ge(sg("hp_s"), SEQ // HC * (hd - 1))
                        for e in range(2):
                            mm = nc.tensor.matmul(ps[:, 6 + e, 0:HALF], C("ones"), rn[:, e * HALF:(e + 1) * HALF],
                                                  start=True, stop=True)
                        mm.then_inc(sg("go_mm"), 1)
                    if post:
                        pe_hgrn_post(p_, l)

        def pe_hgrn_post(hd, l):
            vh = slice(P * hd, P * (hd + 1))
            if l == 0:
                if hd:
                    nc.tensor.wait_ge(sg("hp_ob"), hd)
                    nc.tensor.wait_ge(sg("hs_ob"), hd)
                for t in range(NT):
                    c = slice(COL0[t], COL0[t] + ROWS[t])
                    o = ps[0:HEAD, 5, 0:P] if t == 0 else ps[:, 4, P * (t - 1):P * t]
                    mm = nc.tensor.transpose(o, kdT[hd % 2][:, c], C("ident"))
                mm.then_inc(sg("hg_kt"), 1)
            if l == 1:
                nc.tensor.wait_ge(sg("hg_kdt"), hd + 1)
                nc.tensor.wait_ge(sg("hg_done"), hd + 1)
                nc.tensor.wait_ge(sg("hs_in" + str(hd % 2)), 16 * (hd // 2 + 1))
                for s in range(NS):
                    c = slice(QS * s, QS * (s + 1))
                    nc.tensor.matmul(ps[:, 5, c], hst[hd % 2][:, s, :], proj[:, 8 + hd, c], start=(s == 0),
                                     stop=False, skip_group_check=True)
                nc.tensor.matmul(ps[:, 5, 0:HEAD], v5[0:HEAD, 0, vh], at5[hd % 2][0:HEAD, 0, 0:HEAD],
                                 start=False, stop=True, skip_group_check=True).then_inc(sg("hs_o"), 1)
            if l == 2:
                if hd:
                    nc.tensor.wait_ge(sg("go_ln"), hd)
                for b in range(2):
                    mm = nc.tensor.matmul(ps[:, 6 + b, :], kd5[0:HEAD, 0, :],
                                          hmask[0:HEAD, 4 * b:4 * b + 4, :].rearrange("p s c -> p (s c)"),
                                          start=True, stop=True)
                mm.then_inc(sg("hs_kv"), 1)
            if l == 4:
                nc.tensor.wait_ge(sg("hs_s"), hd + 1)
                for c in range(SEQ // HC):
                    t, r = 1 + c // 2, slice(HC * (c % 2), HC * (c % 2) + HC)
                    mm = nc.tensor.matmul(ps[:, 6 + c % 2, P * (c // 2):P * (c // 2 + 1)], kd5[r, t, :], v5[r, t, vh],
                                          start=True, stop=True)
                mm.then_inc(sg("hp_kv"), 1)
            if l == 6:
                nc.tensor.wait_ge(sg("hs_ob"), hd + 1)
                nc.tensor.wait_ge(sg("hp_s"), SEQ // HC * (hd + 1) - 1)
                for c in range(SEQ // HC):
                    t, r = 1 + c // 2, slice(HC * (c % 2), HC * (c % 2) + HC)
                    o = ps[:, 4 + c % 2, HC * (c // 2):HC * (c // 2 + 1)]
                    nc.tensor.matmul(o, v5[r, t, vh], at5[hd % 2][r, t, r], start=True, stop=False)
                    mm = nc.tensor.matmul(o, hsp[:, c, :], proj[:, 8 + hd, HEAD + HC * c:HEAD + HC * (c + 1)],
                                          start=False, stop=True)
                mm.then_inc(sg("hp_o"), 1)

        def sp_hgrn_states(sp):
            sp.wait_ge(sg("v_out"), 2 * NT)
            for hd in range(HGH + 2):
                if hd >= 2:
                    sp.wait_ge(sg("hs_s"), hd - 1)
                    sp.dma_start(hgrn_s[:, hd - 2], hst[hd % 2]).then_inc(sg("hs_out" + str(hd % 2)), 16)
                if hd < HGH:
                    if hd >= 2:
                        sp.wait_ge(sg("hs_out" + str(hd % 2)), 16 * (hd // 2))
                    sp.dma_start(hst[hd % 2], shgrn[:, hd]).then_inc(sg("hs_in" + str(hd % 2)), 16)
            sp.wait_ge(sg("hp_s"), SEQ // HC * HGH)
            sp.dma_start(hgrn_p, hp_fin).then_inc(sg("hp_out"), 16)

        def sp_weights(sp, a, b):
            with sp.Fori(0, b - a) as i:
                for s in range(SLOTS):
                    sp.wait_ge(w_lo, SLOTS * i + (SLOTS * a + s + 1))
                    sp.dma_start(ring[:, s, :], w[SLOTS * i + (SLOTS * (a + 1) + s)]).then_inc(w_in[s], 16)

        block = ctx.enter_context(nc.Block())

        @block.sync
        def _(sp):
            for i in range(XIN):
                c = slice(KT // XIN * i, KT // XIN * (i + 1))
                sp.dma_start(h[:, c, :], x[:, c, :]).then_inc(sg(f"x_in{i}"), 16)
            for s in range(SLOTS):
                sp.dma_start(ring[:, s, :], w[s]).then_inc(w_in[s], 16)
            sp_weights(sp, 0, U_EVEN // SLOTS)
            sp.wait_ge(sg("pt_in"), 16)
            sp.wait_ge(w_used, U_EVEN)
            for s in range(NS):
                for g in range(NPG):
                    pg = sp.value_load(pt_sb[0:1, NPG * s + g:NPG * s + g + 1], min_val=0, max_val=NPOOL - 1)
                    sp.dma_start(pages[:, s, g], kvpages[pg]).then_inc(sg("pages_in"), 16)
            sp_weights(sp, U_EVEN // SLOTS, Units.out_o // SLOTS)
            sp_hgrn_states(sp)
            sp_weights(sp, Units.out_o // SLOTS, UNITS // SLOTS - 1)
            sp.wait_ge(sg("x_f"), 5 * KT)
            sp.dma_start(y, xn[:, :, :]).then_inc(sg("y_out"), 16)
            sp.wait_ge(sg("y_out"), 16)
            sp.wait_ge(sg("hs_out0"), 16 * (HGH // 2))
            sp.wait_ge(sg("hs_out1"), 16 * (HGH // 2))
            sp.wait_ge(sg("hp_out"), 16)

        @block.gpsimd
        def _(pool):
            pool.dma_start(pt_sb[:, :], ptab).then_inc(sg("pt_in"), 16)
            pool.dma_start(hist[:, :, :, 0:CONV_W - 1], stconv).then_inc(sg("hist_in"), 16)
            pool_rope()
            pool_conv()
            pool.wait_ge(sg("roped"), len(ROPED))
            pool.dma_start(C("sin"), keep).then_inc(sg("keep_in"), 16)
            pool.dma_start(krows, proj[:, AK0, :]).then_inc(sg("rows_out"), 16)
            pool.dma_start(ikrows, proj[0:HD, IK0, :]).then_inc(sg("rows_out"), 16)
            pool.dma_start(vrows, tokm[:, :, 0:P]).then_inc(sg("rows_out"), 16)
            pool.wait_ge(sg("conv_p"), 12)
            pool.dma_start(convo_p, ctail[:, :, :]).then_inc(sg("conv_out"), 16)
            pool.dma_start(convo_s, hist).then_inc(sg("conv_out"), 16)
            pool_sample_queries()
            pool.wait_ge(sg("conv_out"), 32)
            pool.wait_ge(sg("l2_done"), 8)
            pool.wait_ge(sg("mix_a"), len(DONE))
            pool.wait_ge(sg("rows_out"), 48)
            pool.dma_start(st, sdelta).then_inc(sg("st_in"), 16)
            pool_inv()
            pool_gdn_scan()
            pool.wait_ge(sg("sc_kv0"), DNH)
            pool.wait_ge(sg("sc_s"), NT)
            pool.dma_start(delta_s, st).then_inc(sg("state_out"), 16)
            pool.dma_start(delta_p, sp_st[:, NT % 2]).then_inc(sg("state_out"), 16)
            add_squares(nc.gpsimd, 1)
            add_squares(nc.gpsimd, 2)
            pool_hgrn()
            add_squares(nc.gpsimd, 3)
            add_squares(nc.gpsimd, 4)

        @block.scalar
        def _(act):
            act.dma_start(cst[:, :], consts).then_inc(const_in, 16)
            act.dma_start(vec[:, :], vecs).then_inc(const_in, 16)
            act.dma_start(wsm, wsmall).then_inc(small_in, 16)
            act.wait_ge(const_in, 32)
            for k in range(KT):
                act_square(0, k)
            act_w_hi(0, GROUP, 0, 0)
            act_w_hi(0, GROUP, 0, 1)
            act_norm(0)
            act_even()
            act_attention()
            act_gdn_prep()
            act_inv()
            nc.scalar.activation(proj[:, Z0:Z0 + 4, :], proj[:, Z0:Z0 + 4, :], ACT.Silu).then_inc(sg("z_gate"), 1)
            nc.scalar.preload_act_table_set("natural_log_exp_and_others")
            act_gdn_scan()
            act.wait_ge(sg("sc_ob"), NT)
            act.wait_ge(sg("conv_out"), 32)
            act_w_hi(Units.out_e, GROUP, 0, 0)
            act_w_hi(Units.out_e, GROUP, 0, 1)
            for k in range(4):
                act_x_hi(xn, k, "mix_a", len(DONE))
            gate_norm("act", DNH, O_E, z_e, V_DN, "ge", 6)
            act_out(Units.out_e, 1)
            act_norm(1)
            act_ffn(0, Units.ffn0)
            act_norm(2)
            act.wait_ge(sg("state_out"), 32)
            act_dense(1, Units.odd, proj, ACT.Copy)
            act_dense(2, Units.odd + 8, region(8 * T, 16, T), ACT.Silu)
            act_values5()
            act_hgrn()
            act.wait_ge(sg("go_mm"), HGH)
            act_w_hi(Units.out_o, GROUP, 0, 0)
            act_w_hi(Units.out_o, GROUP, 0, 1)
            act.wait_ge(sg("hs_out0"), 16 * (HGH // 2))
            act.wait_ge(sg("hs_out1"), 16 * (HGH // 2))
            for k in range(KT):
                act_x_hi(oT5, k, "go_out", k + 1)
            act_out(Units.out_o, 3)
            act_norm(3)
            act_ffn(1, Units.ffn1, more=False)
            act_norm(4)

        @block.vector
        def _(dve):
            dve.wait_ge(const_in, 32)
            dlink(nc.vector.memset(mx[:, :], 0.0), "bank_free")
            dlink(nc.vector.memset(mx[:, :], 0.0), "bank_free")
            add_squares(nc.vector, 0)
            dve_w_lo(0, GROUP, 0, 0)
            dve_w_lo(0, GROUP, 0, 1)
            dve_norm(0, xn0)
            choice = dve_even(dlink)
            dve_attention(dlink, choice)
            dve_gdn_prep(dlink)
            dve_inv(dlink)
            dve_gdn_scan(dlink)
            dve_w_lo(Units.out_e, GROUP, 0, 0)
            dve_w_lo(Units.out_e, GROUP, 0, 1)
            for k in range(4):
                dve_x_lo(xn, k)
            gate_norm("dve", DNH, O_E, z_e, V_DN, "ge", 6)
            dve_out(Units.out_e)
            dve_norm(1, xn)
            dve_ffn(0, Units.ffn0)
            dve_norm(2, xn)
            lower_bounds()
            dve_w_los(3, Units.odd)
            for j in range(VUNITS - 2):
                dve_w_lo(Units.values, VUNITS, 0, j + 2)
                if j == 4:
                    dve.wait_ge(sg("lb"), 1)
                    dve_front_f(0)
                if j == 5:
                    dve.wait_ge(sg("keep_in"), 16)
                    dve.wait_ge(w_used, Units.values + 5)
                    dve_front_scan(0)
            dve_hgrn(dlink)
            dve_w_lo(Units.out_o, GROUP, 0, 0)
            dve_w_lo(Units.out_o, GROUP, 0, 1)
            for k in range(KT):
                dve_x_lo(oT5, k)
            dve_out(Units.out_o)
            dve_norm(3, xn)
            dve_ffn(1, Units.ffn1, more=False)
            dve_norm(4, xn)

        @block.tensor
        def _(pe):
            pe.wait_ge(const_in, 32)
            pe_norm(0)
            pe_even()
            pe_attention()
            pe_gdn_prep()
            pe_inv()
            pe_gdn_scan()
            gate_norm("pe", DNH, O_E, z_e, V_DN, "ge", 6)
            pe_dense(1, Units.out_e, 1)
            pe_norm(1)
            pe_ffn(0, Units.ffn0)
            pe_norm(2)
            pe_dense(3, Units.odd, 3)
            pe_values5()
            pe.wait_ge(sg("v_out"), 2 * NT)
            pe_hgrn()
            pe_dense(1, Units.out_o, 4)
            pe_norm(3)
            pe_ffn(1, Units.ffn1)
            pe_norm(4)


def unit_columns():
    dq = 1092
    cols = [np.arange(dq + P * m, dq + P * (m + 1)) for m in range(12)]
    cols += [np.arange(2636 + P * m, 2636 + P * (m + 1)) for m in range(4)]
    ik = np.arange(1024, 1088)
    cols += [np.concatenate([ik, ik]), np.arange(512, 640)]
    cols += [np.arange(768 + P * m, 768 + P * (m + 1)) for m in range(2)]
    cols += [np.concatenate([np.arange(HD * j, HD * j + HD), np.arange(HD * (j + 4), HD * (j + 5))]) for j in range(4)]
    return np.concatenate([cols[m] for m in EVEN_TILES])


def units_up(w):
    n = w.shape[1] // P
    return w.reshape(KT, P, n, P).transpose(2, 1, 0, 3).reshape(n, P, KT * P)


def units_ffn(up, down):
    down = down.reshape(4, KT, P, KT, P).transpose(0, 3, 2, 1, 4).reshape(4, GROUP, P, KT * P)
    return np.concatenate([units_up(up).reshape(4, GROUP, P, KT * P), down], axis=1).reshape(U_FFN, P, KT * P)


def units_values(w):
    return w.reshape(4, 2, P, 2, 512).transpose(3, 0, 2, 1, 4).reshape(VUNITS, P, KT * P)


def kernel(x_prompt, x_sample, cache_k, cache_v, cache_ik, state_conv, state_delta, state_hgrn, page_table,
           meta, ln_mix, ln_ffn, ln_final, w_in_e, w_out_e, dn_conv, dn_a_log, dn_dt_bias, dn_norm,
           w_in_o, w_out_o, hg_lb, hg_norm, w_up, w_down):
    import concourse.bacc as _bacc
    from concourse.bass_utils import run_bass_kernel_spmd as _run

    A = np.asarray

    def fm(v):
        return A(v).reshape(-1, KT, P).transpose(2, 1, 0)

    def cols(v):
        return A(v).reshape(-1, P).T

    table, at, keep = constant_table()
    wi = A(w_in_e)[0]
    wo = A(w_in_o)[0]
    fqz = np.concatenate([wo[:, D:2 * D], wo[:, 0:D], wo[:, 3 * D:4 * D]], axis=1)
    units = np.concatenate([
        units_up(wi[:, unit_columns()]), units_up(A(w_out_e)[0]), units_ffn(A(w_up)[0], A(w_down)[0]),
        units_up(fqz), units_values(wo[:, 2 * D:3 * D]), units_up(A(w_out_o)[0]),
        units_ffn(A(w_up)[1], A(w_down)[1])])
    small = wi[:, np.concatenate([np.arange(640, 768), np.arange(1088, 1092), np.arange(2628, 2636)])]
    lb = A(hg_lb)
    ik = A(cache_ik)[0].transpose(0, 2, 1)
    vecs = np.concatenate([
        cols(A(ln_mix)[0]), cols(A(ln_ffn)[0]), cols(A(ln_mix)[1]), cols(A(ln_ffn)[1]), cols(ln_final),
        A(dn_conv)[0].reshape(CONV_W, 12, P).transpose(2, 1, 0).reshape(P, 48),
        cols(A(dn_norm)[0]), cols(A(hg_norm)[0]),
        np.broadcast_to(A(dn_dt_bias)[0], (P, 4)), np.broadcast_to(A(dn_a_log)[0], (P, 4)),
        cols(lb[0]), cols(lb[1])], axis=1)
    ins = {
        "x": np.concatenate([fm(A(x_sample).reshape(SAMP, D)), fm(meta), fm(A(x_prompt)[0])], axis=2),
        "consts": table, "keep": keep, "w": units,
        "wsmall": small.reshape(KT, P, SMALL).transpose(1, 0, 2),
        "vecs": vecs,
        "stconv": A(state_conv)[0].reshape(NS, 3, 12, P).transpose(3, 2, 0, 1),
        "sdelta": A(state_delta)[0].transpose(2, 1, 0, 3).reshape(P, DNH, NS * P),
        "shgrn": A(state_hgrn)[0].transpose(2, 1, 0, 3),
        "kvpages": np.stack([A(cache_k)[0].reshape(NPOOL, PAGE, P).transpose(0, 2, 1),
                             np.concatenate([ik, ik], axis=1), A(cache_v)[0].reshape(NPOOL, PAGE, P)], axis=2),
        "ptab": A(page_table).reshape(1, NS * NPG),
    }
    outs = {
        "y": (P, KT, T), "krows": (P, T), "vrows": (P, NT, P), "ikrows": (HD, T), "convo_p": (P, 12, 3),
        "convo_s": (P, 12, NS, 11), "delta_p": (P, DNH, P), "delta_s": (P, DNH, NS * P),
        "hgrn_p": (P, HGH, P), "hgrn_s": (P, HGH, NS, P),
    }
    nc = _bacc.Bacc("TRN2", target_bir_lowering=False, num_devices=1)
    arrays, args = {}, {}
    for name, a in ins.items():
        a = np.ascontiguousarray(a)
        arrays["in_" + name] = a
        args[name] = nc.dram_tensor("in_" + name, a.shape, mybir.dt.from_np(a.dtype), kind="ExternalInput").ap()
    for name, shape in outs.items():
        args[name] = nc.dram_tensor("out_" + name, shape, F32, kind="ExternalOutput").ap()
    hybrid_step(nc, at=at, **args)
    r = _run(nc, [arrays], core_ids=[0]).results[0]
    o = {name: A(r["out_" + name]).reshape(shape) for name, shape in outs.items()}

    y = o["y"].transpose(2, 1, 0).reshape(T, D)
    kr, ikr = o["krows"].T, o["ikrows"].T
    vr = np.concatenate([o["vrows"][0:HEAD, 0]] + [o["vrows"][:, t] for t in range(1, NT)])
    cs = o["convo_s"][:, :, :, 8:11].transpose(2, 3, 1, 0).reshape(1, NS, 3, 12 * P)
    return (
        y[None, HEAD:], y[:SAMP].reshape(NS, QS, D),
        kr[SAMP:].reshape(1, 1, META + SEQ, KVH, HD), vr[SAMP:].reshape(1, 1, META + SEQ, KVH, HD),
        ikr[SAMP:].reshape(1, 1, META + SEQ, HD),
        o["convo_p"].transpose(2, 1, 0).reshape(1, 1, 3, 12 * P),
        o["delta_p"].transpose(1, 0, 2)[None, None],
        o["hgrn_p"].transpose(1, 0, 2)[None, None],
        kr[:SAMP].reshape(1, NS, QS, KVH, HD), vr[:SAMP].reshape(1, NS, QS, KVH, HD),
        ikr[:SAMP].reshape(1, NS, QS, HD), cs,
        o["delta_s"].reshape(P, DNH, NS, P).transpose(2, 1, 0, 3)[None],
        o["hgrn_s"].transpose(2, 1, 0, 3)[None],
    )
```
